# Optimizing a Trainium2 kernel written in Bass

```python
import jax, jax.numpy as jnp
from jax import lax
import numpy as np

D_MODEL = 1024
BATCH = 1
SEQ = 256
DEPTH = 2

CHUNK = 64
N_HEADS = 16
N_KV_HEADS = 4
HEAD_DIM = 64
WINDOW = 128
WINDOW_CHUNKS = WINDOW // CHUNK
BAND = WINDOW_CHUNKS * CHUNK
CONV_DIM = 512
CONV_WIDTH = 31
D_FF = 2816
N_EXPERTS = 8
TOP_K = 2
D_FF_EXPERT = 3584
ALPHA = (2.0 * DEPTH) ** 0.25
BETA = (8.0 * DEPTH) ** -0.25
LN_EPS = 1e-5
Q_DIM = N_HEADS * HEAD_DIM
KV_DIM = N_KV_HEADS * HEAD_DIM
IN_DIM = Q_DIM + 2 * KV_DIM + 2 * CONV_DIM + 2 * D_MODEL
N_DENSE = (DEPTH + 1) // 2
N_MOE = DEPTH // 2
MASK_VALUE = -1e30

kernel_name = "hybrid_conformer_swa_sink_moe_trunk"

def layer_norm(x, g, b):
    xf = x.astype(jnp.float32)
    mu = jnp.mean(xf, axis=-1, keepdims=True)
    var = jnp.mean(jnp.square(xf - mu), axis=-1, keepdims=True)
    y = (xf - mu) * lax.rsqrt(var + LN_EPS)
    return (y * g.astype(jnp.float32) + b.astype(jnp.float32)).astype(x.dtype)

def conformer_conv(u, dw_w, dw_b, ln_g, ln_b, w_out):
    a, g = jnp.split(u, 2, axis=-1)
    z = a * jax.nn.sigmoid(g)
    z = lax.conv_general_dilated(
        z, dw_w[:, None, :].astype(z.dtype), window_strides=(1,),
        padding=[(CONV_WIDTH - 1, 0)],
        dimension_numbers=('NWC', 'WIO', 'NWC'),
        feature_group_count=CONV_DIM) + dw_b
    z = jax.nn.silu(layer_norm(z, ln_g, ln_b))
    return z @ w_out

def band_chunks(t, nc):
    b = t.shape[0]
    tc = t.reshape(b, nc, CHUNK, N_KV_HEADS, HEAD_DIM)
    parts = [jnp.pad(tc, ((0, 0), (w, 0), (0, 0), (0, 0), (0, 0)))[:, :nc]
             for w in range(WINDOW_CHUNKS - 1, 0, -1)] + [tc]
    return jnp.concatenate(parts, axis=2)

def window_sink_attention(q, k, v, sinks):
    b, s, _ = q.shape
    nc = s // CHUNK
    grp = N_HEADS // N_KV_HEADS
    qc = q.reshape(b, nc, CHUNK, N_KV_HEADS, grp, HEAD_DIM)
    kb = band_chunks(k.reshape(b, s, N_KV_HEADS, HEAD_DIM), nc)
    vb = band_chunks(v.reshape(b, s, N_KV_HEADS, HEAD_DIM), nc)
    scores = jnp.einsum('bnqhgd,bnkhd->bnhgqk', qc, kb).astype(jnp.float32) * (HEAD_DIM ** -0.5)
    chunk_idx = jnp.arange(nc, dtype=jnp.int32)[:, None]
    q_pos = chunk_idx * CHUNK + jnp.arange(CHUNK, dtype=jnp.int32)[None, :]
    k_pos = chunk_idx * CHUNK + jnp.arange(BAND, dtype=jnp.int32)[None, :] - (WINDOW_CHUNKS - 1) * CHUNK
    dist = jnp.abs(q_pos[:, :, None] - k_pos[:, None, :]).astype(jnp.float32)
    slopes = 2.0 ** (-8.0 * jnp.arange(1, N_HEADS + 1, dtype=jnp.float32) / N_HEADS)
    slopes = slopes.reshape(N_KV_HEADS, grp)
    scores = scores - slopes[None, None, :, :, None, None] * dist[None, :, None, None, :, :]
    valid = (k_pos >= 0)[None, :, None, None, None, :]
    scores = jnp.where(valid, scores, MASK_VALUE)
    sink = sinks.astype(jnp.float32).reshape(N_KV_HEADS, grp)[None, None, :, :, None]
    m = jnp.maximum(jnp.max(scores, axis=-1), sink)
    p = jnp.exp(scores - m[..., None])
    denom = jnp.sum(p, axis=-1) + jnp.exp(sink - m)
    probs = (p / denom[..., None]).astype(vb.dtype)
    out = jnp.einsum('bnhgqk,bnkhd->bnqhgd', probs, vb)
    return out.reshape(b, s, Q_DIM)

def swiglu(h, w1, w3, w2):
    return (jax.nn.silu(h @ w1) * (h @ w3)) @ w2

def moe_swiglu(h, w_router, w1, w3, w2):
    b, s, d = h.shape
    t = h.reshape(b * s, d)
    logits = (t @ w_router).astype(jnp.float32)
    top_v, top_i = lax.top_k(logits, TOP_K)
    top_w = jax.nn.softmax(top_v, axis=-1)
    gates = jnp.sum(jax.nn.one_hot(top_i, N_EXPERTS, dtype=jnp.float32) * top_w[..., None], axis=1)
    out = jnp.zeros_like(t)
    for e in range(N_EXPERTS):
        out = out + gates[:, e:e + 1].astype(t.dtype) * swiglu(t, w1[e], w3[e], w2[e])
    return out.reshape(b, s, d)

def setup_inputs(seed: int = 0) -> dict:
    key = jax.random.key(seed)
    ks = jax.random.split(key, 24)
    f32 = jnp.float32
    D = D_MODEL

    def nrm(k, shape, std):
        return jax.random.normal(k, shape, f32) * std

    x = nrm(ks[0], (BATCH, SEQ, D), 1.0)
    c = nrm(ks[1], (BATCH, D), 1.0)
    w_ada = nrm(ks[2], (DEPTH, D, 6 * D), 0.5 * D ** -0.5)
    gate_offset = jnp.tile(jnp.concatenate([jnp.zeros((2 * D,), f32), jnp.ones((D,), f32)]), 2)
    b_ada = nrm(ks[3], (DEPTH, 6 * D), 0.02) + gate_offset
    col_scale = jnp.concatenate([jnp.ones((Q_DIM + KV_DIM,), f32), jnp.full((KV_DIM,), BETA, f32),
                                 jnp.ones((2 * CONV_DIM + 2 * D,), f32)])
    w_in = nrm(ks[4], (DEPTH, D, IN_DIM), D ** -0.5) * col_scale
    conv_dw_w = nrm(ks[5], (DEPTH, CONV_WIDTH, CONV_DIM), CONV_WIDTH ** -0.5)
    conv_dw_b = nrm(ks[6], (DEPTH, CONV_DIM), 0.02)
    conv_ln_g = 1.0 + nrm(ks[7], (DEPTH, CONV_DIM), 0.02)
    conv_ln_b = nrm(ks[8], (DEPTH, CONV_DIM), 0.02)
    w_conv_out = nrm(ks[9], (DEPTH, CONV_DIM, D), CONV_DIM ** -0.5)
    w_attn_out = nrm(ks[10], (DEPTH, Q_DIM, D), Q_DIM ** -0.5)
    attn_sinks = nrm(ks[11], (DEPTH, N_HEADS), 0.5)
    w_o = nrm(ks[12], (DEPTH, D, D), BETA * D ** -0.5)
    post_ln_g = 1.0 + nrm(ks[13], (DEPTH, 2, D), 0.02)
    post_ln_b = nrm(ks[14], (DEPTH, 2, D), 0.02)
    ffn_w1 = nrm(ks[15], (N_DENSE, D, D_FF), D ** -0.5)
    ffn_w3 = nrm(ks[16], (N_DENSE, D, D_FF), D ** -0.5)
    ffn_w2 = nrm(ks[17], (N_DENSE, D_FF, D), BETA * D_FF ** -0.5)
    moe_router = nrm(ks[18], (N_MOE, D, N_EXPERTS), D ** -0.5)
    moe_w1 = nrm(ks[19], (N_MOE, N_EXPERTS, D, D_FF_EXPERT), D ** -0.5)
    moe_w3 = nrm(ks[20], (N_MOE, N_EXPERTS, D, D_FF_EXPERT), D ** -0.5)
    moe_w2 = nrm(ks[21], (N_MOE, N_EXPERTS, D_FF_EXPERT, D), BETA * D_FF_EXPERT ** -0.5)
    return {"x": x, "c": c, "w_ada": w_ada, "b_ada": b_ada, "w_in": w_in,
            "conv_dw_w": conv_dw_w, "conv_dw_b": conv_dw_b, "conv_ln_g": conv_ln_g, "conv_ln_b": conv_ln_b,
            "w_conv_out": w_conv_out, "w_attn_out": w_attn_out, "attn_sinks": attn_sinks, "w_o": w_o,
            "post_ln_g": post_ln_g, "post_ln_b": post_ln_b,
            "ffn_w1": ffn_w1, "ffn_w3": ffn_w3, "ffn_w2": ffn_w2,
            "moe_router": moe_router, "moe_w1": moe_w1, "moe_w3": moe_w3, "moe_w2": moe_w2}

def reference(x, c, w_ada, b_ada, w_in, conv_dw_w, conv_dw_b, conv_ln_g, conv_ln_b,
              w_conv_out, w_attn_out, attn_sinks, w_o, post_ln_g, post_ln_b,
              ffn_w1, ffn_w3, ffn_w2, moe_router, moe_w1, moe_w3, moe_w2):
    splits = [Q_DIM, Q_DIM + KV_DIM, Q_DIM + 2 * KV_DIM, Q_DIM + 2 * KV_DIM + 2 * CONV_DIM,
              Q_DIM + 2 * KV_DIM + 2 * CONV_DIM + D_MODEL]
    c_act = jax.nn.silu(c)
    for l in range(DEPTH):
        mod = (c_act @ w_ada[l] + b_ada[l])[:, None, :]
        sh1, sc1, g1, sh2, sc2, g2 = jnp.split(mod, 6, axis=-1)

        h = x * (1.0 + sc1) + sh1
        proj = h @ w_in[l]
        q, k, v, u, gate_a, gate_b = jnp.split(proj, splits, axis=-1)
        y_conv = conformer_conv(u, conv_dw_w[l], conv_dw_b[l], conv_ln_g[l], conv_ln_b[l], w_conv_out[l])
        y_attn = window_sink_attention(q, k, v, attn_sinks[l]) @ w_attn_out[l]
        merged = jax.nn.sigmoid(gate_a) * y_conv + jax.nn.sigmoid(gate_b) * y_attn
        y = merged @ w_o[l]
        x = layer_norm(ALPHA * x + g1 * y, post_ln_g[l, 0], post_ln_b[l, 0])

        h = x * (1.0 + sc2) + sh2
        if l % 2 == 0:
            i = l // 2
            y = swiglu(h, ffn_w1[i], ffn_w3[i], ffn_w2[i])
        else:
            i = l // 2
            y = moe_swiglu(h, moe_router[i], moe_w1[i], moe_w3[i], moe_w2[i])
        x = layer_norm(ALPHA * x + g2 * y, post_ln_g[l, 1], post_ln_b[l, 1])
    return x


_drawn_inputs = setup_inputs


def setup_inputs(seed=0):
    import zlib

    import numpy as np

    out = dict(_drawn_inputs(seed))
    spreads = {}
    factors = {'conv_dw_b': 4.455, 'conv_ln_g': 8.0, 'conv_ln_b': 5.363, 'attn_sinks': 8.0}
    for name, (base, spread) in spreads.items():
        noise = np.random.default_rng([zlib.crc32(name.encode()), seed]).standard_normal(out[name].shape)
        drawn = base * np.exp(spread * noise) if base else spread * noise
        out[name] = __import__('jax').numpy.asarray(drawn.astype(out[name].dtype))
    for name, factor in factors.items():
        out[name] = (out[name] * factor).astype(out[name].dtype)
    return out
```

```python
from contextlib import ExitStack

import concourse.bass as bass
from concourse import mybir

F32 = mybir.dt.float32
I32 = mybir.dt.int32
ALU = mybir.AluOpType
ACT = mybir.ActivationFunctionType
AX = mybir.AxisListType

P = 128
D = 1024
KB = D // P
S = 256
TB = S // P
DEPTH = 2
HEADS, KV_HEADS, HD = 16, 4, 64
GRP = HEADS // KV_HEADS
CHUNK = 64
CONV = 512
CB = CONV // P
TAPS = 31
PAD = TAPS - 1
DFF = 2816
FT = 256
NFT = DFF // FT
E = 8
DFFE = 3584
ET = 512
NET = DFFE // ET
ALPHA = (2.0 * DEPTH) ** 0.25
EPS = 1e-5
FAR = -1e38
SLOTS = 7
SLOT = 4096
ITEM_BLOCKS = 3 * NET
MAX_ITEMS = E + 3

C_BADA, C_LNG, C_LNB, C_C, C_CG, C_CB, C_DWB, C_DW = 0, 96, 128, 160, 168, 176, 184, 256


def mixing_steps(l):
    ada = {0: [(0, 4), (0, 5), (0, 6), (0, 7), (0, 8), (0, 9), (0, 10), (0, 11), (1, 0), (1, 1), (1, 2), (1, 3)],
           1: []}[l]
    main = [("u", l, 0), ("u", l, 1), ("q", l, 0), ("q", l, 1), ("kv", l, 0), ("scores", l, 0),
            ("gate", l, 0), ("probsT", l, 0), ("pv", l, 0), ("scores", l, 1),
            ("gate", l, 1), ("probsT", l, 1), ("pv", l, 1), ("scores", l, 2),
            ("gate", l, 2), ("probsT", l, 2), ("pv", l, 2), ("scores", l, 3),
            ("gate", l, 3), ("probsT", l, 3), ("pv", l, 3), ("convT", l, 0), ("attn_out", l, 0),
            ("normT", l, 0), ("attn_out", l, 1), ("gains", 2 * l, 0), ("conv_out", l, 0),
            ("w_o", l, 0), ("w_o", l, 1)]
    out = []
    for n, step in enumerate(main):
        fill = n >= 1 and step[0] in ("u", "q", "kv", "gate", "scores") and ada
        if fill:
            al, ai = ada.pop(0)
            out += [("ada", al, ai), step, ("ada_cols", al, ai)]
        else:
            out.append(step)
    assert not ada
    return out


def all_steps():
    steps = []
    for i in range(4):
        steps += [("ada", 0, i), ("ada_cols", 0, i)]
    steps += [("turn", 0, 0)] + mixing_steps(0)
    steps += [("turn", 1, 0), ("ffn_up", 0, 0), ("ffn_up", 0, 1), ("ffn_down", 0, 0)]
    rest = [(1, i) for i in range(4, 12)]
    for f in range(2, NFT):
        if rest:
            steps += [("ada", *rest[0]), ("ffn_up", 0, f), ("ada_cols", *rest.pop(0)), ("ffn_down", 0, f - 1)]
        else:
            steps += [("ffn_up", 0, f), ("ffn_down", 0, f - 1)]
    steps += [("gains", 1, 0), ("ffn_down", 0, NFT - 1)]
    steps += [("turn", 2, 0)] + mixing_steps(1)
    steps += [("turn", 3, 0), ("router", 1, 0), ("ranks", 1, 0), ("gains", 3, 0)]
    return steps


def weight_blocks(steps):
    load, done = [], []
    for kind, l, i in steps:
        if kind in ("ada", "u", "q", "kv", "gate", "conv_out", "attn_out", "w_o", "ffn_up"):
            load.append((kind, l, i))
            done.append((kind, l, i))
        if kind == "ffn_down":
            if i % 2 == 0:
                load.append(("ffn_down", l, i // 2))
            if i % 2 == 1 or i == NFT - 1:
                done.append(("ffn_down", l, i // 2))
    return load, {b: n for n, b in enumerate(done)}


def w1_place(f):
    return 0 if f == 0 else 3 * f - 1


def w3_place(f):
    return 1 if f == 0 else 3 * f


def w2_place(f):
    return 3 * f + 4 if f < NET - 1 else ITEM_BLOCKS - 1


def trunk(nc, x, c, w_ada, b_ada, w_in, conv_dw_w, conv_dw_b, conv_ln_g, conv_ln_b, w_conv_out,
          w_attn_out, attn_sinks, w_o, post_ln_g, post_ln_b, ffn_w1, ffn_w3, ffn_w2, moe_router,
          moe_w1, moe_w3, moe_w2, out):
    steps = all_steps()
    load, used_place = weight_blocks(steps)
    slot_of = {b: n % SLOTS for n, b in enumerate(load)}
    parts = {b: 2 if b[0] == "ffn_up" else 1 for b in load}
    landed, per_slot = {}, [0] * SLOTS
    for b in load:
        per_slot[slot_of[b]] += 16 * parts[b]
        landed[b] = per_slot[slot_of[b]]
    N0 = len(load)

    with ExitStack() as ctx:
        def sb(name, shape, dt=F32):
            return ctx.enter_context(nc.sbuf_tensor(name, shape, dt))

        def sem(name):
            return ctx.enter_context(nc.semaphore(name))

        ring = sb("ring", [P, SLOTS, SLOT])
        x_tok = sb("x_tok", [P, TB, D])
        xn = sb("xn", [P, TB, D])
        hT = sb("hT", [P, KB, S])
        arena = sb("arena", [P, 13432])
        cols = sb("cols", [P, 512])
        mod_raw = sb("mod_raw", [P, DEPTH, 48])
        scale_c = sb("scale_c", [P, 4, KB])
        shift_c = sb("shift_c", [P, 4, KB])
        tiny = sb("tiny", [P, 4, KB])
        mod_part = sb("mod_part", [P, 512])
        lnbuf = sb("lnbuf", [P, D])
        gains = sb("gains", [P, D])
        neg_dist = sb("neg_dist", [P, TB, S])
        ident = sb("ident", [P, P])
        ones = sb("ones", [P, P])
        before = sb("before", [P, P])
        pick4 = sb("pick4", [P, 1])
        c_wide = sb("c_wide", [P, KB, 32])
        c_act = sb("c_act", [P, KB])
        sinks = sb("sinks", [P, DEPTH * HEADS])
        w_router = sb("w_router", [P, KB, E])
        epsc = sb("epsc", [P, 1])
        st_max = sb("st_max", [P, 8])
        st_neg = sb("st_neg", [P, 8])
        st_dsink = sb("st_dsink", [P, 8])
        st_den = sb("st_den", [P, 8])
        st_esink = sb("st_esink", [P, 8])
        st_rden = sb("st_rden", [P, 8])
        bn = sb("bn", [P, 2, 2, 6])
        mv = sb("mv", [P, 2, 2])
        sd = sb("sd", [P, 2])
        rs = sb("rs", [P, 2])
        route = sb("route", [P, 16, 16])
        item_pos = sb("item_pos", [P, TB, MAX_ITEMS + 1])
        item_gate = sb("item_gate", [P, TB, MAX_ITEMS + 1])
        items_f = sb("items_f", [P, 4])
        items_i = sb("items_i", [P, 4], I32)
        ps = ctx.enter_context(nc.psum_tensor("ps", [P, 8, 512], F32))

        at = [0]

        def part(*shape):
            n = 1
            for k in shape:
                n *= k
            v = arena[:, at[0]:at[0] + n]
            at[0] += n
            if len(shape) == 2:
                v = v.rearrange("p (a b) -> p a b", a=shape[0])
            if len(shape) == 3:
                v = v.rearrange("p (a b c) -> p a b c", a=shape[0], b=shape[1])
            return v

        qT = part(KB, S)
        kT = part(KV_HEADS, S)
        v_tok = part(TB, KV_HEADS * HD)
        zp = part(CB, S + PAD)
        conv = part(CB, S)
        gT = part(2 * KB, S)
        probs = part(8, S)
        pT = part(GRP, 3 * P)
        zn = conv.rearrange("p a b -> p (a b)").rearrange("p (a b) -> p a b", a=TB)
        zT = zp[:, :, 0:S]
        assert at[0] == 13432
        at[0] = 0
        hid = part(2, ET)
        gated = part(2, ET)
        hTi = part(KB, P)
        y_item = part(D)
        y_sum = part(TB, D)
        put = part(TB, P)
        put_g = part(TB, P)
        put_gT = part(S)
        fin_g = part(D)
        fin_b = part(D)
        slot_no = part(P)
        e_rev = part(TB, E)
        e_idx = part(E)
        at[0] = 0
        rows = part(4, P)
        at[0] = 12000
        iota_i = arena[:, 12000:12000 + 512].bitcast(I32)

        slot_in = [sem(f"slot_in{i}") for i in range(SLOTS)]
        rows_in = sem("rows_in")
        x_in = sem("x_in")
        sinks_in = sem("sinks_in")
        router_in = sem("router_in")
        consts = sem("consts")
        rows_zero = sem("rows_zero")
        cols_t = sem("cols_t")
        cols_ready = sem("cols_ready")
        c_ready = sem("c_ready")
        cw_ready = sem("cw_ready")
        dist_ready = sem("dist_ready")
        wts_used = sem("wts_used")
        ada_cols_done = sem("ada_cols_done")
        mod_part_ready = sem("mod_part_ready")
        mod_raw_ready = sem("mod_raw_ready")
        scales_ready = sem("scales_ready")
        turn_done = sem("turn_done")
        hT_ready = sem("hT_ready")
        sg_ready = sem("sg_ready")
        z_ready = sem("z_ready")
        pad_ready = sem("pad_ready")
        conv_step = sem("conv_step")
        q_ready = sem("q_ready")
        kv_ready = sem("kv_ready")
        gate_ready = sem("gate_ready")
        scores_done = sem("scores_done")
        biased = sem("biased")
        max_ready = sem("max_ready")
        exp_ready = sem("exp_ready")
        probs_ready = sem("probs_ready")
        probsT_done = sem("probsT_done")
        pT_ready = sem("pT_ready")
        pv_done = sem("pv_done")
        oT_ready = sem("oT_ready")
        convT_done = sem("convT_done")
        cvar_ready = sem("cvar_ready")
        csd_ready = sem("csd_ready")
        zn_ready = sem("zn_ready")
        normT_done = sem("normT_done")
        zT_ready = sem("zT_ready")
        gated_conv = sem("gated_conv")
        gated_attn = sem("gated_attn")
        merged = sem("merged")
        diag_ready = sem("diag_ready")
        gains_done = sem("gains_done")
        gains_ready = sem("gains_ready")
        y_gained = sem("y_gained")
        var_ready = sem("var_ready")
        sd_ready = sem("sd_ready")
        xn_ready = sem("xn_ready")
        ln_in = sem("ln_in")
        x_ready = sem("x_ready")
        silu_ready = sem("silu_ready")
        hid_ready = sem("hid_ready")
        ffn_half = sem("ffn_half")
        gap_ready = sem("gap_ready")
        gap_exp = sem("gap_exp")
        router_done = sem("router_done")
        mask_ready = sem("mask_ready")
        ranks_done = sem("ranks_done")
        items_ready = sem("items_ready")
        put_ready = sem("put_ready")
        put_g_ready = sem("put_g_ready")
        gather_done = sem("gather_done")
        hTi_ready = sem("hTi_ready")
        putT_done = sem("putT_done")
        putT_ready = sem("putT_ready")
        y_item_ready = sem("y_item_ready")
        scatter_done = sem("scatter_done")
        y_added = sem("y_added")
        fin_in = sem("fin_in")
        out_ready = sem("out_ready")
        out_done = sem("out_done")
        dve_chain = sem("dve_chain")
        pool_chain = sem("pool_chain")

        def sources(b):
            kind, l, i = b
            if kind == "ada":
                return [w_ada[l].rearrange("(kb p) n -> p kb n", p=P)[:, :, 512 * i:512 * i + 512]]
            first = {"q": 0, "kv": 2, "u": 3, "gate": 5}
            if kind in first:
                j = first[kind] + i
                return [w_in[l].rearrange("(kb p) n -> p kb n", p=P)[:, :, 512 * j:512 * j + 512]]
            if kind == "conv_out":
                return [w_conv_out[l].rearrange("(kb p) n -> p kb n", p=P)]
            if kind in ("attn_out", "w_o"):
                w = w_attn_out if kind == "attn_out" else w_o
                return [w[l].rearrange("(kb p) n -> p kb n", p=P)[:, :, 512 * i:512 * i + 512]]
            if kind == "ffn_up":
                return [w[0].rearrange("(kb p) n -> p kb n", p=P)[:, :, FT * i:FT * i + FT]
                        for w in (ffn_w1, ffn_w3)]
            return [ffn_w2[0, 512 * i:min(512 * i + 512, DFF)].rearrange("(kb p) n -> p kb n", p=P)]

        moe1 = moe_w1.rearrange("a e (kb p) n -> (a e) p kb n", p=P)
        moe3 = moe_w3.rearrange("a e (kb p) n -> (a e) p kb n", p=P)
        moe2 = moe_w2.rearrange("a e (kb p) n -> (a e) p kb n", p=P)

        def ring_slot(b):
            s = ring[:, slot_of[b], :]
            if b[0] == "conv_out":
                return s.rearrange("p (k n) -> p k n", k=CB)
            if b[0] == "ffn_down":
                return s.rearrange("p (k n) -> p k n", k=4)
            if b[0] == "ffn_up":
                return s.rearrange("p (w k n) -> p w k n", w=2, k=KB)
            return s.rearrange("p (k n) -> p k n", k=KB)

        bank_of = {}
        block = ctx.enter_context(nc.Block())

        @block.tensor
        def _(pe):
            holder = [None] * 8
            turn, size = [0], [8]

            def take(key, freed_by, banks=None):
                if banks is None:
                    b = turn[0] % size[0]
                    turn[0] += 1
                else:
                    b = banks
                if holder[b] is not None:
                    pe.wait_ge(*holder[b])
                holder[b] = freed_by
                bank_of[key] = b
                return b

            def weights(b):
                pe.wait_ge(slot_in[slot_of[b]], landed[b])
                return ring_slot(b)

            pe.wait_ge(rows_in, 16 * 11)
            pe.wait_ge(consts, 1)
            b = take(("cols", 0), (cols_ready, 4))
            for j, r in enumerate((128, 64, 124, 124)):
                mm = nc.tensor.transpose(ps[:, b, 128 * j:128 * j + r], rows[0:r, j, :], ident[0:r, 0:r])
            mm.then_inc(cols_t, 1)
            pe.wait_ge(cw_ready, 1)
            pe.wait_ge(consts, 4)

            def ada(l, i):
                w = weights(("ada", l, i))
                b = take(("ada", l, i), (mod_part_ready, 12 * l + i + 1))
                for r in range(2):
                    for j in range(4):
                        kb = 2 * j + r
                        mm = nc.tensor.matmul(ps[32 * j:32 * j + 32, b, :], c_wide[:, kb, :], w[:, kb, :],
                                              start=(r == 0), stop=(r == 1), tile_position=(0, 32 * j))
                mm.then_inc(wts_used, 1)

            def ada_cols(l, i):
                n = 12 * l + i
                b = take(("ada_cols", l, i), (mod_raw_ready, n + 1))
                pe.wait_ge(mod_part_ready, n + 1)
                for j in range(4):
                    mm = nc.tensor.matmul(ps[:, b, j:j + 1], mod_part[:, P * j:P * j + P], pick4[:, :],
                                          start=True, stop=True)
                mm.then_inc(ada_cols_done, 1)

            def turn_stream(s, _):
                src = x_tok if s == 0 else xn
                if s == 0:
                    pe.wait_ge(x_in, 16)
                else:
                    pe.wait_ge(xn_ready, 2 * s)
                for j in range(4):
                    b = take(("turn", s, j), (hT_ready, 8 * (s + 1)))
                    for kb in (2 * j, 2 * j + 1):
                        for t in range(TB):
                            mm = nc.tensor.transpose(
                                ps[:, b, S * (kb % 2) + P * t:S * (kb % 2) + P * t + P],
                                src[:, t, P * kb:P * kb + P], ident[:, :])
                    mm.then_inc(turn_done, 1)
                pe.wait_ge(hT_ready, 8 * (s + 1))

            def columns(b, w, c0, act, nk, start=0):
                for j in range(2):
                    for kb in range(nk):
                        mm = nc.tensor.matmul(ps[:, b, S * j:S * j + S],
                                              w[:, kb, c0 + P * j:c0 + P * j + P], act[:, kb, :],
                                              start=(kb == 0), stop=(kb == nk - 1))
                return mm

            def project(kind, freed_by, act=hT):
                def run(l, i):
                    w = weights((kind, l, i))
                    for h in range(2):
                        b = take((kind, l, i, h), freed_by(l, i, h))
                        mm = columns(b, w, 256 * h, act, KB)
                    mm.then_inc(wts_used, 1)
                return run

            def kv(l, _):
                w = weights(("kv", l, 0))
                b = take(("kv", l, 0), (kv_ready, 5 * l + 4))
                columns(b, w, 0, hT, KB)
                b = take(("kv", l, 1), (kv_ready, 5 * l + 5))
                for t in range(TB):
                    for kb in range(KB):
                        mm = nc.tensor.matmul(ps[:, b, S * t:S * t + S], hT[:, kb, P * t:P * t + P],
                                              w[:, kb, 256:512], start=(kb == 0), stop=(kb == KB - 1))
                mm.then_inc(wts_used, 1)

            def scores(l, g):
                if g == 0:
                    pe.wait_ge(q_ready, 4 * (l + 1))
                    pe.wait_ge(kv_ready, 5 * (l + 1))
                for i in range(GRP):
                    h = GRP * g + i
                    half = HD * (h % 2)
                    b = take(("scores", l, g, i), (biased, 16 * l + h + 1))
                    for t in range(TB):
                        mm = nc.tensor.matmul(ps[:, b, S * t:S * t + S],
                                              qT[half:half + HD, h // 2, P * t:P * t + P],
                                              kT[half:half + HD, g, :], start=True, stop=True)
                    mm.then_inc(scores_done, 1)

            def probs_turn(l, g):
                pe.wait_ge(probs_ready, 8 * (4 * l + g + 1))
                for i in range(GRP):
                    b = take(("probsT", l, g, i), (pT_ready, 16 * l + GRP * g + i + 1))
                    for n, (t, kb) in enumerate(((0, 0), (1, 0), (1, 1))):
                        mm = nc.tensor.transpose(ps[:, b, P * n:P * n + P],
                                                 probs[:, 2 * i + t, P * kb:P * kb + P], ident[:, :])
                    mm.then_inc(probsT_done, 1)

            def pv(l, g):
                pe.wait_ge(pT_ready, 16 * l + GRP * (g + 1))
                b = take(("pv", l, g), (oT_ready, 4 * l + g + 1))
                for i in range(GRP):
                    half, c0 = HD * (i % 2), S * (i // 2)
                    for n, (t, kb) in enumerate(((0, 0), (1, 0), (1, 1))):
                        mm = nc.tensor.matmul(ps[half:half + HD, b, c0 + P * t:c0 + P * t + P],
                                              v_tok[:, kb, HD * g:HD * g + HD], pT[:, i, P * n:P * n + P],
                                              start=(n != 2), stop=(n != 1), tile_position=(0, half))
                mm.then_inc(pv_done, 1)

            def conv_turn(l, _):
                pe.wait_ge(conv_step, CB * TAPS * (l + 1))
                for t in range(TB):
                    b = take(("convT", l, t), (zn_ready, 2 * l + t + 1))
                    for cb in range(CB):
                        mm = nc.tensor.transpose(ps[:, b, P * cb:P * cb + P],
                                                 conv[:, cb, P * t:P * t + P], ident[:, :])
                    mm.then_inc(convT_done, 1)

            def norm_turn(l, _):
                pe.wait_ge(zn_ready, 2 * (l + 1))
                for j in range(2):
                    b = take(("normT", l, j), (zT_ready, 4 * l + 2 * j + 2))
                    for cb in (2 * j, 2 * j + 1):
                        for t in range(TB):
                            mm = nc.tensor.transpose(
                                ps[:, b, S * (cb % 2) + P * t:S * (cb % 2) + P * t + P],
                                zn[:, t, P * cb:P * cb + P], ident[:, :])
                    mm.then_inc(normT_done, 1)

            def conv_out(l, _):
                w = weights(("conv_out", l, 0))
                pe.wait_ge(zT_ready, 4 * (l + 1))
                for j in range(4):
                    b = take(("conv_out", l, j), (gated_conv, 4 * l + j + 1))
                    mm = columns(b, w, 256 * j, zT, CB)
                mm.then_inc(wts_used, 1)

            def attn_out(l, i):
                if i == 0:
                    pe.wait_ge(oT_ready, 4 * (l + 1))
                project("attn_out", lambda l, i, h: (gated_attn, 4 * l + 2 * i + h + 1), qT)(l, i)

            def out_proj(l, i):
                w = weights(("w_o", l, i))
                if i == 0:
                    pe.wait_ge(merged, 4 * (l + 1))
                for t in range(TB):
                    b = take(("y", 2 * l, t, i), (y_gained, 8 * l + 2 * t + i + 1))
                    for kb in range(KB):
                        mm = nc.tensor.matmul(ps[:, b, :], gT[:, kb, P * t:P * t + P], w[:, kb, :],
                                              start=(kb == 0), stop=(kb == KB - 1))
                mm.then_inc(wts_used, 1)

            def spread_gains(s, _):
                pe.wait_ge(diag_ready, s + 1)
                for h in range(2):
                    b = take(("gains", s, h), (gains_ready, 2 * s + h + 1))
                    mm = nc.tensor.matmul(ps[:, b, :], ones[:, :], lnbuf[:, 512 * h:512 * h + 512],
                                          start=True, stop=True)
                mm.then_inc(gains_done, 1)

            def ffn_up(l, f):
                w = weights(("ffn_up", 0, f))
                for h in range(2):
                    b = take(("ffn_up", f, h), (hid_ready, f + 1))
                    for j in range(2):
                        for kb in range(KB):
                            mm = nc.tensor.matmul(ps[:, b, S * j:S * j + S],
                                                  w[:, h, kb, P * j:P * j + P], hT[:, kb, :],
                                                  start=(kb == 0), stop=(kb == KB - 1))
                mm.then_inc(wts_used, 1)

            def ffn_down(l, f):
                blk = ("ffn_down", 0, f // 2)
                w = weights(blk)
                if f == 0:
                    for t in range(TB):
                        for h in range(2):
                            take(("y", 1, t, h), (y_gained, 4 + 2 * t + h + 1), 4 + 2 * t + h)
                pe.wait_ge(hid_ready, f + 1)
                for j in range(2):
                    for t in range(TB):
                        for h in range(2):
                            mm = nc.tensor.matmul(ps[:, 4 + 2 * t + h, :],
                                                  hid[:, f % 2, S * j + P * t:S * j + P * t + P],
                                                  w[:, 2 * (f % 2) + j, 512 * h:512 * h + 512],
                                                  start=(f == 0 and j == 0), stop=(f == NFT - 1 and j == 1),
                                                  skip_group_check=True)
                if f % 2 == 1 or f == NFT - 1:
                    mm.then_inc(wts_used, 1)
                else:
                    mm.then_inc(ffn_half, 1)

            def router(l, _):
                pe.wait_ge(router_in, 16)
                b = take(("router", 0), (mask_ready, 1))
                for t in range(TB):
                    for kb in range(KB):
                        mm = nc.tensor.matmul(ps[:, b, E * t:E * t + E], hT[:, kb, P * t:P * t + P],
                                              w_router[:, kb, :], start=(kb == 0), stop=(kb == KB - 1))
                mm.then_inc(router_done, 1)

            def ranks(l, _):
                pe.wait_ge(mask_ready, 1)
                b = take(("ranks", 0), (items_ready, 1))
                m0, m1 = route[:, 0, 0:E], route[:, 0, E:2 * E]
                nc.tensor.matmul(ps[:, b, 0:E], before[:, :], m0, start=True, stop=True)
                nc.tensor.matmul(ps[:, b, E:2 * E], ones[:, :], m0, start=True, stop=False)
                nc.tensor.matmul(ps[:, b, E:2 * E], before[:, :], m1, start=False, stop=True)
                nc.tensor.matmul(ps[:, b, 2 * E:3 * E], ones[:, :], m0, start=True, stop=False)
                nc.tensor.matmul(ps[:, b, 2 * E:3 * E], ones[:, :], m1, start=False, stop=True)\
                    .then_inc(ranks_done, 1)

            do = {"ada": ada, "ada_cols": ada_cols, "turn": turn_stream,
                  "u": project("u", lambda l, i, h: (z_ready, 2 * l + h + 1)),
                  "q": project("q", lambda l, i, h: (q_ready, 4 * l + 2 * i + h + 1)),
                  "gate": project("gate", lambda l, i, h: (gate_ready, 8 * l + 2 * i + h + 1)),
                  "kv": kv, "scores": scores, "probsT": probs_turn, "pv": pv, "convT": conv_turn,
                  "normT": norm_turn, "conv_out": conv_out, "attn_out": attn_out, "w_o": out_proj,
                  "gains": spread_gains, "ffn_up": ffn_up, "ffn_down": ffn_down, "router": router,
                  "ranks": ranks}
            for kind, l, i in steps:
                if kind == "ffn_up" and i == 0:
                    turn[0], size[0] = 0, 4
                if kind == "turn":
                    turn[0], size[0] = 0, 8
                do[kind](l, i)

            for b in range(8):
                if holder[b] is not None:
                    pe.wait_ge(*holder[b])

            def gather(n):
                pe.wait_ge(put_ready, 2 * n)
                for h in range(2):
                    for j in range(4):
                        kb = 4 * h + j
                        for t in range(TB):
                            mm = nc.tensor.matmul(ps[:, 6 + h, P * j:P * j + P], xn[:, t, P * kb:P * kb + P],
                                                  put[:, t, :], start=(t == 0), stop=(t == TB - 1))
                mm.then_inc(gather_done, 1)

            pe.sem_inc(putT_done, 1)
            pe.sem_inc(scatter_done, 1)

            def expert_block(it, place):
                n = N0 + place
                s = n % SLOTS
                k = place // SLOTS
                pe.wait_ge(slot_in[s], it * 48 + (per_slot[s] + 16 * (k + 1)))
                return ring[:, s, :]

            gather(1)
            n_items = pe.value_load(items_i[0:1, 0:1], min_val=E, max_val=MAX_ITEMS)
            with pe.Fori(0, n_items) as it:
                def down(f):
                    w = expert_block(it, w2_place(f)).rearrange("p (k n) -> p k n", k=4)
                    pe.wait_ge(hid_ready, it * NET + (NFT + f + 1))
                    if f == 0:
                        pe.wait_ge(y_item_ready, it * 2 + 1)
                    for j in range(4):
                        for h in range(2):
                            mm = nc.tensor.matmul(ps[:, 4 + h, :], hid[:, f % 2, P * j:P * j + P],
                                                  w[:, j, 512 * h:512 * h + 512],
                                                  start=(f == 0 and j == 0), stop=(f == NET - 1 and j == 3),
                                                  skip_group_check=True)
                    mm.then_inc(wts_used, 1)

                pe.wait_ge(hTi_ready, it * 8 + 8)
                for f in range(NET):
                    for h, place in ((0, w1_place(f)), (1, w3_place(f))):
                        w = expert_block(it, place).rearrange("p (k n) -> p k n", k=KB)
                        if h == 0:
                            pe.wait_ge(hid_ready, it * NET + (NFT + max(f - 1, 0)))
                        for j in range(4):
                            for kb in range(KB):
                                mm = nc.tensor.matmul(ps[:, 2 * (f % 2) + h, P * j:P * j + P],
                                                      w[:, kb, P * j:P * j + P], hTi[:, kb, :],
                                                      start=(kb == 0), stop=(kb == KB - 1))
                        mm.then_inc(wts_used, 1)
                    if f == NET - 1:
                        pe.wait_ge(y_added, it * 4 + 1)
                        gather(it + 2)
                    if f >= 1:
                        down(f - 1)
                pe.wait_ge(hTi_ready, it * 8 + 16)
                pe.wait_ge(put_g_ready, it * 2 + 2)
                for t in range(TB):
                    mm = nc.tensor.transpose(ps[:, 6, P * t:P * t + P], put_g[:, t, :], ident[:, :])
                mm.then_inc(putT_done, 1)
                down(NET - 1)
                pe.wait_ge(putT_ready, it + 1)
                for t in range(TB):
                    for h in range(2):
                        if t == 0:
                            pe.wait_ge(y_item_ready, it * 2 + (h + 2))
                        if t == 1:
                            pe.wait_ge(y_added, it * 4 + (h + 2))
                        nc.tensor.matmul(ps[:, 6 + h, :], put_gT[:, P * t:P * t + P],
                                         y_item[:, 512 * h:512 * h + 512], start=True, stop=True)\
                            .then_inc(scatter_done, 1)

        @block.scalar
        def _(act):
            act.wait_ge(rows_zero, 1)
            bada_r = b_ada.rearrange("l (r p) -> (l r) p", p=P)
            act.dma_start(rows[0:96, 0, :], bada_r).then_inc(rows_in, 16)
            act.dma_start(rows[96:128, 0, :], post_ln_g.rearrange("l s (r p) -> (l s r) p", p=P)).then_inc(rows_in, 16)
            act.dma_start(rows[0:32, 1, :], post_ln_b.rearrange("l s (r p) -> (l s r) p", p=P)).then_inc(rows_in, 16)
            act.dma_start(rows[32:40, 1, :], c.rearrange("a (r p) -> (a r) p", p=P)).then_inc(rows_in, 16)
            act.dma_start(rows[40:48, 1, :], conv_ln_g.rearrange("l (r p) -> (l r) p", p=P)).then_inc(rows_in, 16)
            act.dma_start(rows[48:56, 1, :], conv_ln_b.rearrange("l (r p) -> (l r) p", p=P)).then_inc(rows_in, 16)
            act.dma_start(rows[56:64, 1, :], conv_dw_b.rearrange("l (r p) -> (l r) p", p=P)).then_inc(rows_in, 16)
            for l in range(DEPTH):
                for h in range(2):
                    r = conv_dw_w[l].rearrange("j (r p) -> (j r) p", p=P)[62 * h:62 * h + 62, :]
                    act.dma_start(rows[62 * h:62 * h + 62, 2 + l, :], r).then_inc(rows_in, 16)
            act.dma_start(x_tok[:, :, :], x[0].rearrange("(t p) d -> p t d", p=P)).then_inc(x_in, 16)
            act.dma_start(sinks[:, :], attn_sinks.rearrange("l h -> (l h)").partition_broadcast(P)).then_inc(sinks_in, 16)
            act.dma_start(w_router[:, :, :], moe_router[0].rearrange("(kb p) e -> p kb e", p=P)).then_inc(router_in, 16)

            act.wait_ge(cols_t, 1)
            act.wait_ge(consts, 4)
            b = bank_of[("cols", 0)]
            for j, r in enumerate((128, 64, 124, 124)):
                nc.scalar.copy(cols[:, P * j:P * j + r], ps[:, b, P * j:P * j + r]).then_inc(cols_ready, 1)
            act.wait_ge(cols_ready, 4)
            nc.scalar.activation(c_act[:, :], cols[:, C_C:C_C + KB], ACT.Silu).then_inc(c_ready, 1)

            def weights_done(b):
                act.wait_ge(wts_used, used_place[b] + 1)

            def ada(l, i):
                n = 12 * l + i
                weights_done(("ada", l, i))
                if n:
                    act.wait_ge(ada_cols_done, n)
                nc.scalar.copy(mod_part[:, :], ps[:, bank_of[("ada", l, i)], :]).then_inc(mod_part_ready, 1)

            def ada_cols(l, i):
                act.wait_ge(ada_cols_done, 12 * l + i + 1)
                nc.scalar.copy(mod_raw[:, l, 4 * i:4 * i + 4], ps[:, bank_of[("ada_cols", l, i)], 0:4])\
                    .then_inc(mod_raw_ready, 1)

            def turn_stream(s, _):
                act.wait_ge(scales_ready, s + 1)
                if s:
                    act.wait_ge(wts_used, used_place[{1: ("gate", 0, 3), 2: ("ffn_up", 0, NFT - 1),
                                                      3: ("gate", 1, 3)}[s]] + 1)
                for j in range(2):
                    act.wait_ge(turn_done, 4 * s + j + 1)
                    for kb in (2 * j, 2 * j + 1):
                        nc.scalar.activation(hT[:, kb, :], ps[:, bank_of[("turn", s, j)], S * (kb % 2):S * (kb % 2) + S],
                                             ACT.Identity, bias=shift_c[:, s, kb:kb + 1],
                                             scale=scale_c[:, s, kb:kb + 1]).then_inc(hT_ready, 1)

            def u(l, i):
                if i == 1:
                    weights_done(("u", l, 1))
                    for h in range(2):
                        nc.scalar.activation(conv[:, 2 * h:2 * h + 2, :].rearrange("p a b -> p (a b)"),
                                             ps[:, bank_of[("u", l, 1, h)], :], ACT.Sigmoid).then_inc(sg_ready, 1)

            def q(l, i):
                weights_done(("q", l, i))
                for h in range(2):
                    kb = 4 * i + 2 * h
                    nc.scalar.mul(qT[:, kb:kb + 2, :].rearrange("p a b -> p (a b)"),
                                  ps[:, bank_of[("q", l, i, h)], :], HD ** -0.5).then_inc(q_ready, 1)

            def kv(l, _):
                weights_done(("kv", l, 0))
                src = ps[:, bank_of[("kv", l, 0)], :].rearrange("p (a b) -> p a b", a=2)
                for half in range(2):
                    for to in range(2):
                        nc.scalar.copy(kT[HD * to:HD * to + HD, half::2, :],
                                       src[HD * half:HD * half + HD, :, :]).then_inc(kv_ready, 1)
                nc.scalar.copy(v_tok.rearrange("p a b -> p (a b)"), ps[:, bank_of[("kv", l, 1)], :])\
                    .then_inc(kv_ready, 1)

            def gate(l, i):
                weights_done(("gate", l, i))
                for h in range(2):
                    kb = 4 * i + 2 * h
                    nc.scalar.activation(gT[:, kb:kb + 2, :].rearrange("p a b -> p (a b)"),
                                         ps[:, bank_of[("gate", l, i, h)], :], ACT.Sigmoid).then_inc(gate_ready, 1)

            def scores(l, g):
                n = 4 * l + g
                act.wait_ge(max_ready, n + 1)
                nc.scalar.activation(st_esink[:, :], st_dsink[:, :], ACT.Exp).then_inc(exp_ready, 1)
                for j in range(8):
                    nc.scalar.activation(probs[:, j, :], probs[:, j, :], ACT.Exp, bias=st_neg[:, j:j + 1],
                                         accum_out=st_den[:, j:j + 1]).then_inc(exp_ready, 1)

            def probs_turn(l, g):
                for i in range(GRP):
                    act.wait_ge(probsT_done, 16 * l + GRP * g + i + 1)
                    if i == 0 and 4 * l + g:
                        act.wait_ge(pv_done, 4 * l + g)
                    nc.scalar.copy(pT[:, i, :], ps[:, bank_of[("probsT", l, g, i)], 0:3 * P]).then_inc(pT_ready, 1)

            def pv(l, g):
                act.wait_ge(pv_done, 4 * l + g + 1)
                nc.scalar.copy(qT[:, 2 * g:2 * g + 2, :].rearrange("p a b -> p (a b)"),
                               ps[:, bank_of[("pv", l, g)], :]).then_inc(oT_ready, 1)

            def conv_turn(l, _):
                for t in range(TB):
                    act.wait_ge(cvar_ready, 2 * l + t + 1)
                    nc.scalar.activation(sd[:, t:t + 1], mv[:, t, 1:2], ACT.Sqrt, bias=epsc[:, 0:1]).then_inc(csd_ready, 1)

            def norm_turn(l, _):
                for j in range(2):
                    act.wait_ge(normT_done, 2 * l + j + 1)
                    for cb in (2 * j, 2 * j + 1):
                        nc.scalar.activation(zT[:, cb, :], ps[:, bank_of[("normT", l, j)], S * (cb % 2):S * (cb % 2) + S],
                                             ACT.Silu, bias=cols[:, C_CB + CB * l + cb:C_CB + CB * l + cb + 1],
                                             scale=cols[:, C_CG + CB * l + cb:C_CG + CB * l + cb + 1]).then_inc(zT_ready, 1)

            def spread_gains(s, _):
                act.wait_ge(gains_done, s + 1)
                if s:
                    act.wait_ge(y_gained, 4 * s)
                for h in range(2):
                    nc.scalar.copy(gains[:, 512 * h:512 * h + 512], ps[:, bank_of[("gains", s, h)], :])\
                        .then_inc(gains_ready, 1)

            def residual(s):
                for t in range(TB):
                    act.wait_ge(var_ready, 2 * s + t + 1)
                    nc.scalar.activation(sd[:, t:t + 1], mv[:, t, 1:2], ACT.Sqrt, bias=epsc[:, 0:1]).then_inc(sd_ready, 1)

            def out_proj(l, i):
                if i == 1:
                    residual(2 * l)

            def ffn_up(l, f):
                weights_done(("ffn_up", 0, f))
                if f >= 2:
                    act.wait_ge(hid_ready, f - 1)
                nc.scalar.activation(gated[:, f % 2, :], ps[:, bank_of[("ffn_up", f, 0)], :], ACT.Silu)\
                    .then_inc(silu_ready, 1)

            def ffn_down(l, f):
                if f == NFT - 1:
                    residual(1)

            def router(l, _):
                act.wait_ge(gap_ready, 1)
                nc.scalar.activation(route[:, 11, 0:2], route[:, 9, 0:2], ACT.Exp).then_inc(gap_exp, 1)

            do = {"ada": ada, "ada_cols": ada_cols, "turn": turn_stream, "u": u, "q": q, "kv": kv,
                  "gate": gate, "scores": scores, "probsT": probs_turn, "pv": pv, "convT": conv_turn,
                  "normT": norm_turn, "gains": spread_gains, "w_o": out_proj, "ffn_up": ffn_up,
                  "ffn_down": ffn_down, "router": router}
            for kind, l, i in steps:
                if kind in do:
                    do[kind](l, i)

            def gathered():
                for j in range(4):
                    nc.scalar.activation(hTi[:, j, :], ps[:, 6, P * j:P * j + P], ACT.Identity,
                                         bias=shift_c[:, 3, j:j + 1], scale=scale_c[:, 3, j:j + 1]).then_inc(hTi_ready, 1)

            act.sem_inc(y_item_ready, 1)
            act.wait_ge(gather_done, 1)
            gathered()
            n_items = act.value_load(items_i[0:1, 0:1], min_val=E, max_val=MAX_ITEMS)
            with act.Fori(0, n_items) as it:
                for f in range(NET):
                    act.wait_ge(wts_used, it * ITEM_BLOCKS + (N0 + w1_place(f) + 1))
                    act.wait_ge(hid_ready, it * NET + (NFT + max(f - 1, 0)))
                    nc.scalar.activation(gated[:, f % 2, :], ps[:, 2 * (f % 2), :], ACT.Silu).then_inc(silu_ready, 1)
                act.wait_ge(gather_done, it + 2)
                gathered()
                act.wait_ge(putT_done, it + 2)
                act.wait_ge(scatter_done, it * 4 + 1)
                nc.scalar.copy(put_gT[:, :], ps[:, 6, 0:S]).then_inc(putT_ready, 1)
                act.wait_ge(wts_used, it * ITEM_BLOCKS + (N0 + ITEM_BLOCKS))
                for h in range(2):
                    nc.scalar.copy(y_item[:, 512 * h:512 * h + 512], ps[:, 4 + h, :]).then_inc(y_item_ready, 1)
            residual(3)

        @block.vector
        def _(dve):
            count = [0]

            def link(ins):
                count[0] += 1
                ins.then_inc(dve_chain, 1)
                dve.wait_ge(dve_chain, count[0])

            dve.wait_ge(c_ready, 1)
            dve.wait_ge(consts, 3)
            for kb in range(KB):
                ins = nc.vector.tensor_scalar(c_wide[:, kb, :], ones[:, 0:32], c_act[:, kb:kb + 1], None, ALU.mult)
            ins.then_inc(cw_ready, 1)
            nd = neg_dist[:, :, :].rearrange("p a b -> p (a b)")
            link(nc.vector.tensor_copy(nd, iota_i))
            link(nc.vector.scalar_tensor_tensor(out=nd, in0=nd, scalar=-1.0, in1=nd, op0=ALU.mult, op1=ALU.min))
            for p0, t, a, z in ((0, 0, CHUNK, S), (CHUNK, 0, 2 * CHUNK, S), (0, 1, 0, CHUNK),
                                (0, 1, 3 * CHUNK, S), (CHUNK, 1, 0, 2 * CHUNK)):
                link(nc.vector.memset(neg_dist[p0:p0 + CHUNK, t, a:z], FAR))

            def weights_done(b):
                dve.wait_ge(wts_used, used_place[b] + 1)

            def turn_stream(s, _):
                dve.wait_ge(scales_ready, s + 1)
                if s:
                    dve.wait_ge(wts_used, used_place[{1: ("gate", 0, 3), 2: ("ffn_up", 0, NFT - 1),
                                                      3: ("gate", 1, 3)}[s]] + 1)
                for j in range(2, 4):
                    dve.wait_ge(turn_done, 4 * s + j + 1)
                    for kb in (2 * j, 2 * j + 1):
                        nc.vector.tensor_scalar(hT[:, kb, :], ps[:, bank_of[("turn", s, j)], S * (kb % 2):S * (kb % 2) + S],
                                                scale_c[:, s, kb:kb + 1], shift_c[:, s, kb:kb + 1],
                                                ALU.mult, ALU.add).then_inc(hT_ready, 1)

            def u(l, i):
                if i == 0:
                    if l:
                        weights_done(("ffn_down", 0, (NFT - 1) // 2))
                    link(nc.vector.memset(zp[:, :, 0:PAD], 0.0))
                    return
                for h in range(2):
                    dve.wait_ge(sg_ready, 2 * l + h + 1)
                    nc.vector.tensor_tensor(zp[:, 2 * h:2 * h + 2, PAD:PAD + S],
                                            ps[:, bank_of[("u", l, 0, h)], :].rearrange("p (a b) -> p a b", a=2),
                                            conv[:, 2 * h:2 * h + 2, :], ALU.mult).then_inc(z_ready, 1)
                dve.wait_ge(z_ready, 2 * (l + 1))
                base = CB * TAPS * l
                for j in range(TAPS):
                    for cb in range(CB):
                        col = C_DW + P * l + CB * j + cb
                        w = cols[:, col:col + 1]
                        if j == 0:
                            ins = nc.vector.tensor_scalar(conv[:, cb, :], zp[:, cb, 0:S], w,
                                                          cols[:, C_DWB + CB * l + cb:C_DWB + CB * l + cb + 1],
                                                          ALU.mult, ALU.add)
                        else:
                            dve.wait_ge(conv_step, base + CB * (j - 1) + cb + 1)
                            ins = nc.vector.scalar_tensor_tensor(out=conv[:, cb, :], in0=zp[:, cb, j:j + S], scalar=w,
                                                                 in1=conv[:, cb, :], op0=ALU.mult, op1=ALU.add)
                        ins.then_inc(conv_step, 1)

            def scores(l, g):
                n = 4 * l + g
                if l == 0 and g == 0:
                    dve.wait_ge(sinks_in, 16)
                for i in range(GRP):
                    h = GRP * g + i
                    dve.wait_ge(scores_done, 16 * l + h + 1)
                    if i == 0 and n:
                        dve.wait_ge(probsT_done, 4 * n)
                    slope = 2.0 ** (-8.0 * (h + 1) / HEADS)
                    nc.vector.scalar_tensor_tensor(out=probs[:, 2 * i:2 * i + 2, :].rearrange("p a b -> p (a b)"),
                                                   in0=nd, scalar=slope,
                                                   in1=ps[:, bank_of[("scores", l, g, i)], :],
                                                   op0=ALU.mult, op1=ALU.add).then_inc(biased, 1)
                dve.wait_ge(biased, 4 * (n + 1))
                if n:
                    dve.wait_ge(exp_ready, 9 * n)
                sk = sinks[:, HEADS * l + GRP * g:HEADS * l + GRP * (g + 1)].unsqueeze(2).to_broadcast([P, GRP, TB])
                by_head = lambda v: v[:, :].rearrange("p (a b) -> p a b", a=GRP)
                link(nc.vector.tensor_reduce(st_max[:, :], probs, AX.X, ALU.max))
                link(nc.vector.tensor_tensor(by_head(st_max), by_head(st_max), sk, ALU.max))
                link(nc.vector.tensor_scalar(st_neg[:, :], st_max[:, :], -1.0, None, ALU.mult))
                nc.vector.tensor_tensor(by_head(st_dsink), sk, by_head(st_max), ALU.subtract).then_inc(max_ready, 1)

            def normalise(l, g):
                n = 4 * l + g
                dve.wait_ge(exp_ready, 9 * (n + 1))
                link(nc.vector.tensor_tensor(st_den[:, :], st_den[:, :], st_esink[:, :], ALU.add))
                link(nc.vector.reciprocal(st_rden[:, :], st_den[:, :]))
                for j in range(8):
                    nc.vector.tensor_scalar(probs[:, j, :], probs[:, j, :], st_rden[:, j:j + 1], None,
                                            ALU.mult).then_inc(probs_ready, 1)

            def conv_turn(l, _):
                for t in range(TB):
                    bank = ps[:, bank_of[("convT", l, t)], :]
                    dve.wait_ge(convT_done, 2 * l + t + 1)
                    link(nc.vector.bn_stats(bn[:, t, 0, :], bank))
                    nc.vector.bn_aggr(mv[:, t, :], bn[:, t, 0, :]).then_inc(cvar_ready, 1)
                dve.wait_ge(convT_done, 2 * (l + 1))
                for t in range(TB):
                    dve.wait_ge(csd_ready, 2 * l + t + 1)
                    link(nc.vector.reciprocal(rs[:, t:t + 1], sd[:, t:t + 1]))
                    nc.vector.tensor_scalar(zn[:, t, :], ps[:, bank_of[("convT", l, t)], :], mv[:, t, 0:1], rs[:, t:t + 1],
                                            ALU.subtract, ALU.mult).then_inc(zn_ready, 1)

            def attn_out(l, i):
                weights_done(("attn_out", l, i))
                if i == 0:
                    dve.wait_ge(gate_ready, 8 * (l + 1))
                for h in range(2):
                    kb = KB + 4 * i + 2 * h
                    v = gT[:, kb:kb + 2, :].rearrange("p a b -> p (a b)")
                    nc.vector.tensor_tensor(v, ps[:, bank_of[("attn_out", l, i, h)], :], v, ALU.mult)\
                        .then_inc(gated_attn, 1)

            def conv_out(l, _):
                weights_done(("conv_out", l, 0))
                for j in range(4):
                    v = gT[:, 2 * j:2 * j + 2, :].rearrange("p a b -> p (a b)")
                    nc.vector.tensor_tensor(v, ps[:, bank_of[("conv_out", l, j)], :], v, ALU.mult)\
                        .then_inc(gated_conv, 1)
                dve.wait_ge(gated_attn, 4 * (l + 1))
                for j in range(4):
                    dve.wait_ge(gated_conv, 4 * l + j + 1)
                    v = gT[:, 2 * j:2 * j + 2, :]
                    nc.vector.tensor_tensor(v, v, gT[:, KB + 2 * j:KB + 2 * j + 2, :], ALU.add).then_inc(merged, 1)

            def residual(s):
                dve.wait_ge(gains_ready, 2 * (s + 1))
                if s:
                    dve.wait_ge(x_ready, 2 * s)
                for t in range(TB):
                    for h in range(2):
                        y = y_sum[:, t, 512 * h:512 * h + 512] if s == 3 else ps[:, bank_of[("y", s, t, h)], :]
                        nc.vector.tensor_tensor(xn[:, t, 512 * h:512 * h + 512], y,
                                                gains[:, 512 * h:512 * h + 512], ALU.mult).then_inc(y_gained, 1)
                    dve.wait_ge(y_gained, 4 * s + 2 * t + 2)
                    link(nc.vector.scalar_tensor_tensor(out=x_tok[:, t, :], in0=x_tok[:, t, :], scalar=ALPHA,
                                                        in1=xn[:, t, :], op0=ALU.mult, op1=ALU.add))
                    nc.vector.bn_stats(bn[:, t, 0, :], x_tok[:, t, 0:512])
                    link(nc.vector.bn_stats(bn[:, t, 1, :], x_tok[:, t, 512:1024]))
                    nc.vector.bn_aggr(mv[:, t, :], bn[:, t, :, :].rearrange("p a b -> p (a b)")).then_inc(var_ready, 1)
                dve.wait_ge(var_ready, 2 * (s + 1))
                for t in range(TB):
                    dve.wait_ge(sd_ready, 2 * s + t + 1)
                    link(nc.vector.reciprocal(rs[:, t:t + 1], sd[:, t:t + 1]))
                    nc.vector.tensor_scalar(xn[:, t, :], x_tok[:, t, :], mv[:, t, 0:1], rs[:, t:t + 1],
                                            ALU.subtract, ALU.mult).then_inc(xn_ready, 1)

            def out_proj(l, i):
                if i == 1:
                    weights_done(("w_o", l, 1))
                    residual(2 * l)

            def ffn_up(l, f):
                weights_done(("ffn_up", 0, f))
                dve.wait_ge(silu_ready, f + 1)
                if f >= 2:
                    if f % 2 == 1:
                        weights_done(("ffn_down", 0, (f - 2) // 2))
                    else:
                        dve.wait_ge(ffn_half, (f - 2) // 2 + 1)
                nc.vector.tensor_tensor(hid[:, f % 2, :], ps[:, bank_of[("ffn_up", f, 1)], :], gated[:, f % 2, :],
                                        ALU.mult).then_inc(hid_ready, 1)

            def ffn_down(l, f):
                if f == NFT - 1:
                    weights_done(("ffn_down", 0, (NFT - 1) // 2))
                    residual(1)

            def router(l, _):
                r = lambda n: route[:, n, :].rearrange("p (t e) -> p t e", t=TB)
                pair = lambda n: route[:, n, 0:2]
                wide = lambda n: route[:, n, 0:2].unsqueeze(2).to_broadcast([P, TB, E])
                dve.wait_ge(router_done, 1)
                dve.wait_ge(consts, 5)
                lg, rev = ps[:, bank_of[("router", 0)], 0:TB * E].rearrange("p (t e) -> p t e", t=TB), e_rev
                link(nc.vector.tensor_copy(r(1), lg))
                src = 1
                for n, (best, onehot, key, keymax) in enumerate(((2, 3, 4, 5), (6, 7, 4, 5))):
                    link(nc.vector.tensor_reduce(pair(best), r(src), AX.X, ALU.max))
                    link(nc.vector.tensor_tensor(r(key), r(src), wide(best), ALU.is_equal))
                    link(nc.vector.tensor_tensor(r(key), r(key), rev, ALU.mult))
                    link(nc.vector.tensor_reduce(pair(keymax), r(key), AX.X, ALU.max))
                    link(nc.vector.tensor_tensor(r(onehot), rev, wide(keymax), ALU.is_equal))
                    if n == 0:
                        link(nc.vector.scalar_tensor_tensor(out=route[:, 8, :], in0=route[:, 3, :], scalar=-3e38,
                                                            in1=route[:, 1, :], op0=ALU.mult, op1=ALU.add))
                        src = 8
                nc.vector.tensor_tensor(route[:, 0, :], route[:, 3, :], route[:, 7, :], ALU.add).then_inc(mask_ready, 1)
                nc.vector.tensor_tensor(pair(9), pair(6), pair(2), ALU.subtract).then_inc(gap_ready, 1)
                dve.wait_ge(gap_exp, 1)
                link(nc.vector.tensor_scalar(pair(10), pair(11), 1.0, None, ALU.add))
                link(nc.vector.reciprocal(pair(12), pair(10)))
                link(nc.vector.tensor_tensor(pair(13), pair(12), pair(11), ALU.mult))
                link(nc.vector.tensor_tensor(r(3), r(3), wide(12), ALU.mult))
                link(nc.vector.tensor_tensor(r(7), r(7), wide(13), ALU.mult))
                link(nc.vector.tensor_tensor(r(14), r(3), r(7), ALU.add))

            def ranks(l, _):
                r = lambda n: route[:, n, :].rearrange("p (t e) -> p t e", t=TB)
                bank = ps[:, bank_of[("ranks", 0)], :]
                dve.wait_ge(ranks_done, 1)
                dve.wait_ge(mask_ready, 1)
                link(nc.vector.tensor_scalar(route[:, 1, :], bank[:, 0:TB * E], 1.0, None, ALU.add))
                link(nc.vector.tensor_tensor(route[:, 1, :], route[:, 1, :], route[:, 0, :], ALU.mult))
                link(nc.vector.tensor_scalar(route[:, 1, :], route[:, 1, :], -1.0, None, ALU.add))
                big, ahead = route[:, 2, 0:E], route[:, 2, E:2 * E]
                link(nc.vector.tensor_scalar(big, bank[:, 2 * E:3 * E], float(P), None, ALU.is_gt))
                link(nc.vector.memset(ahead[:, 0:1], 0.0))
                for e in range(1, E):
                    link(nc.vector.tensor_tensor(ahead[:, e:e + 1], ahead[:, e - 1:e], big[:, e - 1:e], ALU.add))
                link(nc.vector.tensor_tensor(items_f[:, 0:1], ahead[:, E - 1:E], big[:, E - 1:E], ALU.add))
                link(nc.vector.tensor_scalar(items_f[:, 0:1], items_f[:, 0:1], float(E), None, ALU.add))
                link(nc.vector.memset(item_pos[:, :, MAX_ITEMS:], -1.0))
                link(nc.vector.tensor_copy(item_pos[:, :, 0:E], r(1)))
                link(nc.vector.tensor_copy(item_gate[:, :, 0:E], r(14)))
                for m in range(MAX_ITEMS - E):
                    pick = route[:, 3, 0:E]
                    link(nc.vector.tensor_scalar(pick, ahead, float(m), None, ALU.is_equal))
                    link(nc.vector.tensor_tensor(pick, pick, big, ALU.mult))
                    link(nc.vector.tensor_tensor(route[:, 4, 0:E], pick, e_idx, ALU.mult))
                    link(nc.vector.tensor_reduce(items_f[:, 1 + m:2 + m], route[:, 4, 0:E], AX.X, ALU.add))
                    for t in range(TB):
                        link(nc.vector.tensor_tensor(route[:, 4, 0:E], pick, route[:, 1, E * t:E * t + E], ALU.mult))
                        link(nc.vector.tensor_reduce(route[:, 5, 0:1], route[:, 4, 0:E], AX.X, ALU.add))
                        link(nc.vector.tensor_scalar(item_pos[:, t, E + m:E + m + 1], route[:, 5, 0:1], -float(P),
                                                     None, ALU.add))
                        link(nc.vector.tensor_tensor(route[:, 4, 0:E], pick, route[:, 14, E * t:E * t + E], ALU.mult))
                        link(nc.vector.tensor_reduce(item_gate[:, t, E + m:E + m + 1], route[:, 4, 0:E], AX.X, ALU.add))
                nc.vector.tensor_copy(items_i[:, :], items_f[:, :]).then_inc(items_ready, 1)
                nc.vector.memset(y_sum, 0.0).then_inc(y_added, 1)

            do = {"turn": turn_stream, "u": u, "scores": scores, "probsT": normalise, "convT": conv_turn,
                  "attn_out": attn_out, "conv_out": conv_out, "w_o": out_proj, "ffn_up": ffn_up,
                  "ffn_down": ffn_down, "router": router, "ranks": ranks}
            for kind, l, i in steps:
                if kind in do:
                    do[kind](l, i)

            def place(col):
                for t in range(TB):
                    nc.vector.tensor_scalar(put[:, t, :], slot_no, item_pos[:, t, bass.ds(col, 1)] if not isinstance(col, int)
                                            else item_pos[:, t, col:col + 1], None, ALU.is_equal).then_inc(put_ready, 1)

            def gathered():
                for j in range(4, 8):
                    nc.vector.tensor_scalar(hTi[:, j, :], ps[:, 7, P * (j - 4):P * (j - 4) + P],
                                            scale_c[:, 3, j:j + 1], shift_c[:, 3, j:j + 1],
                                            ALU.mult, ALU.add).then_inc(hTi_ready, 1)

            place(0)
            dve.wait_ge(gather_done, 1)
            gathered()
            n_items = dve.value_load(items_i[0:1, 0:1], min_val=E, max_val=MAX_ITEMS)
            with dve.Fori(0, n_items) as it:
                dve.wait_ge(gather_done, it + 1)
                place(it + 1)
                dve.wait_ge(putT_done, it + 1)
                for t in range(TB):
                    nc.vector.tensor_scalar(put_g[:, t, :], slot_no, item_pos[:, t, bass.ds(it, 1)],
                                            item_gate[:, t, bass.ds(it, 1)], ALU.is_equal, ALU.mult)\
                        .then_inc(put_g_ready, 1)
                for f in range(NET):
                    dve.wait_ge(wts_used, it * ITEM_BLOCKS + (N0 + w3_place(f) + 1))
                    dve.wait_ge(silu_ready, it * NET + (NFT + f + 1))
                    if f >= 2:
                        dve.wait_ge(wts_used, it * ITEM_BLOCKS + (N0 + w2_place(f - 2) + 1))
                    nc.vector.tensor_tensor(hid[:, f % 2, :], ps[:, 2 * (f % 2) + 1, :], gated[:, f % 2, :],
                                            ALU.mult).then_inc(hid_ready, 1)
                dve.wait_ge(gather_done, it + 2)
                gathered()
                for t in range(TB):
                    for h in range(2):
                        dve.wait_ge(scatter_done, it * 4 + (2 * t + h + 2))
                        if t == 0 and h == 0:
                            dve.wait_ge(y_added, it * 4 + 1)
                        y = y_sum[:, t, 512 * h:512 * h + 512]
                        nc.vector.tensor_tensor(y, ps[:, 6 + h, :], y, ALU.add).then_inc(y_added, 1)
            link(nc.vector.memset(st_max[:, :], 0.0))
            residual(3)
            dve.wait_ge(fin_in, 32)
            dve.wait_ge(xn_ready, 8)
            for t in range(TB):
                link(nc.vector.tensor_tensor(xn[:, t, :], xn[:, t, :], fin_g, ALU.mult))
                nc.vector.tensor_tensor(xn[:, t, :], xn[:, t, :], fin_b, ALU.add).then_inc(out_ready, 1)

        @block.gpsimd
        def _(pool):
            count = [0]

            def link(ins):
                count[0] += 1
                ins.then_inc(pool_chain, 1)
                pool.wait_ge(pool_chain, count[0])

            nc.gpsimd.memset(rows, 0.0).then_inc(rows_zero, 1)
            link(nc.gpsimd.memset(ident[:, :], 0.0))
            nc.gpsimd.affine_select(out=ident[:, :], in_=ident[:, :], compare_op=ALU.not_equal, fill=1.0, base=0,
                                    pattern=[[-1, P]], channel_multiplier=1).then_inc(consts, 1)
            nc.gpsimd.memset(ones[:, :], 1.0).then_inc(consts, 1)
            nc.gpsimd.iota(iota_i.rearrange("p (a b) -> p a b", a=TB), pattern=[[P, TB], [-1, S]], base=0,
                           channel_multiplier=1).then_inc(consts, 1)
            nc.gpsimd.memset(epsc[:, :], EPS)
            link(nc.gpsimd.memset(pick4[:, :], 0.0))
            for j in range(4):
                link(nc.gpsimd.memset(pick4[32 * j:32 * j + 1, :], 1.0))
            link(nc.gpsimd.memset(before[:, :], 1.0))
            link(nc.gpsimd.affine_select(out=before[:, :], in_=before[:, :], compare_op=ALU.is_gt, fill=0.0, base=0,
                                         pattern=[[1, P]], channel_multiplier=-1))
            nc.gpsimd.memset(st_den[:, :], 0.0).then_inc(consts, 1)

            def bias_c(l, i):
                return cols[:, C_BADA + 48 * l + i * KB:C_BADA + 48 * l + (i + 1) * KB]

            def scales(s):
                l, base = s // 2, 3 * (s % 2)
                pool.wait_ge(cols_ready, 4)
                pool.wait_ge(mod_raw_ready, 12 * l + (4 if s % 2 == 0 else 10))
                raw = lambda i: mod_raw[:, l, i * KB:(i + 1) * KB]
                link(nc.gpsimd.tensor_tensor(tiny[:, 0, :], raw(base + 1), bias_c(l, base + 1), ALU.add))
                if s == 0:
                    link(nc.gpsimd.tensor_scalar(scale_c[:, 0, :], tiny[:, 0, :], 1.0, None, ALU.add))
                    nc.gpsimd.tensor_tensor(shift_c[:, 0, :], raw(0), bias_c(l, 0), ALU.add).then_inc(scales_ready, 1)
                    return
                gam = cols[:, C_LNG + KB * (s - 1):C_LNG + KB * s]
                bet = cols[:, C_LNB + KB * (s - 1):C_LNB + KB * s]
                link(nc.gpsimd.tensor_scalar(tiny[:, 0, :], tiny[:, 0, :], 1.0, None, ALU.add))
                link(nc.gpsimd.tensor_tensor(scale_c[:, s, :], tiny[:, 0, :], gam, ALU.mult))
                link(nc.gpsimd.tensor_tensor(tiny[:, 1, :], raw(base), bias_c(l, base), ALU.add))
                link(nc.gpsimd.tensor_tensor(tiny[:, 2, :], tiny[:, 0, :], bet, ALU.mult))
                nc.gpsimd.tensor_tensor(shift_c[:, s, :], tiny[:, 1, :], tiny[:, 2, :], ALU.add).then_inc(scales_ready, 1)

            def diagonal(s):
                l, i = s // 2, 2 + 3 * (s % 2)
                pool.wait_ge(mod_raw_ready, 12 * l + (6 if s % 2 == 0 else 12))
                link(nc.gpsimd.tensor_tensor(tiny[:, 3, :], mod_raw[:, l, i * KB:(i + 1) * KB], bias_c(l, i), ALU.add))
                for kb in range(KB):
                    ins = nc.gpsimd.tensor_scalar(lnbuf[:, P * kb:P * kb + P], ident[:, :], tiny[:, 3, kb:kb + 1],
                                                  None, ALU.mult)
                    if kb == KB - 1:
                        ins.then_inc(diag_ready, 1)

            def update(s):
                for n, par in enumerate((post_ln_g, post_ln_b)):
                    if n == 0:
                        pool.wait_ge(gains_done, s + 1)
                    pool.dma_start(lnbuf[:, :], par[s // 2, s % 2].partition_broadcast(P)).then_inc(ln_in, 16)
                    pool.wait_ge(ln_in, 16 * (2 * s + n + 1))
                    if n == 0:
                        pool.wait_ge(xn_ready, 2 * (s + 1))
                    for t in range(TB):
                        ins = nc.gpsimd.tensor_tensor(x_tok[:, t, :], xn[:, t, :] if n == 0 else x_tok[:, t, :],
                                                      lnbuf[:, :], ALU.mult if n == 0 else ALU.add)
                        if n == 0:
                            link(ins)
                        else:
                            ins.then_inc(x_ready, 1)

            def expert_constants():
                pool.wait_ge(xn_ready, 6)
                link(nc.gpsimd.iota(slot_no, pattern=[[1, P]], base=0, channel_multiplier=0,
                                    allow_small_or_imprecise_dtypes=True))
                link(nc.gpsimd.iota(e_rev, pattern=[[0, TB], [-1, E]], base=E, channel_multiplier=0,
                                    allow_small_or_imprecise_dtypes=True))
                nc.gpsimd.iota(e_idx, pattern=[[1, E]], base=0, channel_multiplier=0,
                               allow_small_or_imprecise_dtypes=True).then_inc(consts, 1)
                pool.dma_start(fin_g, post_ln_g[1, 1].partition_broadcast(P)).then_inc(fin_in, 16)
                pool.dma_start(fin_b, post_ln_b[1, 1].partition_broadcast(P)).then_inc(fin_in, 16)

            scales(0)
            for s in range(4):
                diagonal(s)
                if s < 3:
                    scales(s + 1)
                    if s == 2:
                        expert_constants()
                    update(s)
                    pool.wait_ge(x_ready, 2 * (s + 1))
        @block.sync
        def _(sp):
            for n, b in enumerate(load):
                if n >= SLOTS:
                    sp.wait_ge(wts_used, used_place[load[n - SLOTS]] + 1)
                dst, srcs = ring_slot(b), sources(b)
                for j, src in enumerate(srcs):
                    to = dst[:, j] if b[0] == "ffn_up" else dst[:, 0:src.shape[1]]
                    sp.dma_start(to, src).then_inc(slot_in[slot_of[b]], 16)

            def item(it, e):
                order = [None] * ITEM_BLOCKS
                for f in range(NET):
                    cut = slice(ET * f, ET * f + ET)
                    order[w1_place(f)] = (moe1, f)
                    order[w3_place(f)] = (moe3, f)
                    order[w2_place(f)] = (moe2, f)
                for place, (w, f) in enumerate(order):
                    s = (N0 + place) % SLOTS
                    sp.wait_ge(wts_used, it * ITEM_BLOCKS + (N0 + place - SLOTS + 1))
                    if w is moe2:
                        src = w[bass.ds(e, 1), :, 4 * f:4 * f + 4, :]
                        dst = ring[:, s, :].rearrange("p (k n) -> p k n", k=4)
                    else:
                        src = w[bass.ds(e, 1), :, :, ET * f:ET * f + ET]
                        dst = ring[:, s, :].rearrange("p (k n) -> p k n", k=KB)
                    sp.dma_start(dst, src.rearrange("a p k n -> (a p) k n")).then_inc(slot_in[s], 16)

            with sp.Fori(0, E) as it:
                item(it, it)
            sp.wait_ge(items_ready, 1)
            n_items = sp.value_load(items_i[0:1, 0:1], min_val=E, max_val=MAX_ITEMS)
            with sp.If(n_items > E):
                with sp.Fori(E, n_items) as it:
                    e = sp.value_load(items_i[0:1, bass.ds(it - (E - 1), 1)], min_val=0, max_val=E - 1)
                    item(it, e)
            for t in range(TB):
                sp.wait_ge(out_ready, t + 1)
                sp.dma_start(out[0, P * t:P * t + P, :], xn[:, t, :]).then_inc(out_done, 16)
            sp.wait_ge(out_done, 16 * TB)


_INS = ['x', 'c', 'w_ada', 'b_ada', 'w_in', 'conv_dw_w', 'conv_dw_b', 'conv_ln_g', 'conv_ln_b', 'w_conv_out',
        'w_attn_out', 'attn_sinks', 'w_o', 'post_ln_g', 'post_ln_b', 'ffn_w1', 'ffn_w3', 'ffn_w2', 'moe_router',
        'moe_w1', 'moe_w3', 'moe_w2']
_OUTS = [((1, 256, 1024), 'float32')]


def kernel(**inputs):
    import numpy as _np
    import concourse.bacc as _bacc
    from concourse import mybir as _mybir
    from concourse.bass_utils import run_bass_kernel_spmd as _run

    nc = _bacc.Bacc("TRN2", target_bir_lowering=False, num_devices=1)
    arrays, args = {}, []
    for name in _INS:
        a = _np.ascontiguousarray(inputs[name])
        arrays[f"in_{name}_dram"] = a
        args.append(nc.dram_tensor(f"in_{name}_dram", a.shape, _mybir.dt.from_np(a.dtype), kind="ExternalInput").ap())
    for i, (shape, dtype) in enumerate(_OUTS):
        dt = _mybir.dt.from_np(_np.dtype(dtype))
        args.append(nc.dram_tensor(f"out_{i}_dram", shape, dt, kind="ExternalOutput").ap())
    trunk(nc, *args)
    r = _run(nc, [arrays], core_ids=[0])
    got = tuple(r.results[0][f"out_{i}_dram"] for i in range(len(_OUTS)))
    return got[0]
```

```python
from contextlib import ExitStack

import concourse.bass as bass
from concourse import mybir

F32 = mybir.dt.float32
F32R = mybir.dt.float32r
I32 = mybir.dt.int32
ALU = mybir.AluOpType
ACT = mybir.ActivationFunctionType
AX = mybir.AxisListType

P = 128
D = 1024
KB = D // P
S = 256
TB = S // P
DEPTH = 2
HEADS, KV_HEADS, HD = 16, 4, 64
GRP = HEADS // KV_HEADS
CHUNK = 64
CONV = 512
CB = CONV // P
TAPS = 31
PAD = TAPS - 1
DFF = 2816
FT = 256
NFT = DFF // FT
E = 8
DFFE = 3584
ET = 512
NET = DFFE // ET
ALPHA = (2.0 * DEPTH) ** 0.25
EPS = 1e-5
FAR = -1e38
SLOTS = 7
GRAIN = 2048
AHEAD = 3
ITEM_GRAINS = 6 * NET
TAPS_STEP = 8
MAX_ITEMS = E + 3

C_BADA, C_LNG, C_LNB, C_C, C_CG, C_CB, C_DWB, C_DW = 0, 96, 128, 160, 168, 176, 184, 256


def mixing_steps(l):
    ada = [(0, i) for i in range(4, 12)] if l == 0 else [(1, i) for i in range(9, 12)]
    main = [("u", l, 0), ("u", l, 1), ("q", l, 0), ("q", l, 1), ("kv", l, 0), ("scores", l, 0),
            ("gate", l, 0), ("probsT", l, 0), ("pv", l, 0), ("scores", l, 1),
            ("gate", l, 1), ("probsT", l, 1), ("pv", l, 1), ("scores", l, 2),
            ("gate", l, 2), ("probsT", l, 2), ("pv", l, 2), ("scores", l, 3),
            ("gate", l, 3), ("probsT", l, 3), ("pv", l, 3), ("attn_out", l, 0), ("convT", l, 0),
            ("attn_out", l, 1), ("normT", l, 0), ("gains", 2 * l, 0), ("conv_out", l, 0),
            ("w_o", l, 0), ("w_o", l, 1)]
    out = []
    for n, step in enumerate(main):
        fill = n >= 1 and step[0] in ("u", "q", "kv", "gate") and ada
        if fill:
            al, ai = ada.pop(0)
            out += [("ada", al, ai), step, ("ada_cols", al, ai)]
        else:
            out.append(step)
    assert not ada
    return out


def all_steps():
    steps = []
    for i in range(4):
        steps += [("ada", 0, i), ("ada_cols", 0, i)]
    steps += [("turn", 0, 0)] + mixing_steps(0)
    steps += [("turn", 1, 0), ("ffn_up", 0, 0), ("ffn_up", 0, 1), ("ffn_down", 0, 0)]
    for f in range(2, NFT):
        steps += [("ada", 1, f - 2), ("ffn_up", 0, f), ("ada_cols", 1, f - 2), ("ffn_down", 0, f - 1)]
    steps += [("gains", 1, 0), ("ffn_down", 0, NFT - 1)]
    steps += [("turn", 2, 0)] + mixing_steps(1)
    steps += [("turn", 3, 0), ("router", 1, 0), ("ranks", 1, 0), ("gains", 3, 0)]
    return steps


SPLIT_STEPS = ("u", "q", "kv", "gate", "conv_out", "attn_out", "w_o", "ffn_up", "ffn_down")


def granules(steps):
    load = []
    for kind, l, i in steps:
        if kind == "ada" or kind in SPLIT_STEPS:
            load += [(kind, l, i, g) for g in range(1 if kind == "ffn_down" else 2)]
    return load


def up_at(f):
    return 0 if f == 0 else 6 * f - 2


def down_at(f):
    return 6 * f + 8 if f < NET - 1 else ITEM_GRAINS - 2


def trunk(nc, x, c, w_ada, b_ada, w_in, conv_dw_w, conv_dw_b, conv_ln_g, conv_ln_b, w_conv_out,
          w_attn_out, attn_sinks, w_o, post_ln_g, post_ln_b, ffn_w1, ffn_w3, ffn_w2, moe_router,
          moe_w1, moe_w3, moe_w2, out):
    steps = all_steps()
    load = granules(steps)
    ring_no = {g: n for n, g in enumerate(load)}
    split_no = {g: n for n, g in enumerate(g for g in load if g[0] != "ada")}
    ada_no = {g: n for n, g in enumerate(g for g in load if g[0] == "ada")}
    R0, K0 = len(load), len(split_no)

    def landed(n):
        return n % SLOTS, 16 * (n // SLOTS + 1)

    with ExitStack() as ctx:
        def sb(name, shape, dt=F32):
            return ctx.enter_context(nc.sbuf_tensor(name, shape, dt))

        def sem(name):
            return ctx.enter_context(nc.semaphore(name))

        ring = sb("ring", [P, SLOTS, GRAIN])
        w_hi = sb("w_hi", [P, AHEAD, GRAIN], F32R)
        w_lo = sb("w_lo", [P, AHEAD, GRAIN], F32R)
        in_hi = sb("in_hi", [P, KB, S], F32R)
        in_lo = sb("in_lo", [P, KB, S], F32R)
        mid_hi = sb("mid_hi", [P, KB, S], F32R)
        mid_lo = sb("mid_lo", [P, KB, S], F32R)
        x_tok = sb("x_tok", [P, TB, D])
        xn = sb("xn", [P, TB, D])
        arena = sb("arena", [P, 13432])
        cols = sb("cols", [P, 512])
        mod_raw = sb("mod_raw", [P, DEPTH, 48])
        scale_c = sb("scale_c", [P, 4, KB])
        shift_c = sb("shift_c", [P, 4, KB])
        tiny = sb("tiny", [P, 4, KB])
        mod_part = sb("mod_part", [P, 512])
        neg_dist = sb("neg_dist", [P, TB, S])
        ident = sb("ident", [P, P])
        ones = sb("ones", [P, P])
        before = sb("before", [P, P])
        pick4 = sb("pick4", [P, 1])
        c_wide = sb("c_wide", [P, KB, 32])
        c_act = sb("c_act", [P, KB])
        sinks = sb("sinks", [P, DEPTH * HEADS])
        w_router = sb("w_router", [P, KB, E])
        router_hi = sb("router_hi", [P, KB, E], F32R)
        router_lo = sb("router_lo", [P, KB, E], F32R)
        epsc = sb("epsc", [P, 1])
        st_max = sb("st_max", [P, 8])
        st_neg = sb("st_neg", [P, 8])
        st_dsink = sb("st_dsink", [P, 8])
        st_den = sb("st_den", [P, 8])
        st_esink = sb("st_esink", [P, 8])
        st_rden = sb("st_rden", [P, 8])
        bn = sb("bn", [P, 2, 2, 6])
        mv = sb("mv", [P, 2, 2])
        sd = sb("sd", [P, 2])
        rs = sb("rs", [P, 2])
        item_pos = sb("item_pos", [P, TB, MAX_ITEMS + 1])
        item_gate = sb("item_gate", [P, TB, MAX_ITEMS + 1])
        items_f = sb("items_f", [P, 4])
        items_i = sb("items_i", [P, 4], I32)
        ps = ctx.enter_context(nc.psum_tensor("ps", [P, 8, 512], F32))

        at = [0]

        def part(*shape):
            n = 1
            for k in shape:
                n *= k
            v = arena[:, at[0]:at[0] + n]
            at[0] += n
            if len(shape) == 2:
                v = v.rearrange("p (a b) -> p a b", a=shape[0])
            if len(shape) == 3:
                v = v.rearrange("p (a b c) -> p a b c", a=shape[0], b=shape[1])
            return v

        qT = part(KB, S)
        kT = part(KV_HEADS, S)
        v_tok = part(TB, KV_HEADS * HD)
        zp = part(CB, S + PAD)
        conv = part(CB, S)
        gT = part(2 * KB, S)
        probs = part(8, S)
        pT = part(GRP, 3 * P)
        zn = conv.rearrange("p a b -> p (a b)").rearrange("p (a b) -> p a b", a=TB)
        zT = qT[:, 0:CB, :]
        hT = gT[:, 0:KB, :]
        gains = probs[:, 0:4, :].rearrange("p a b -> p (a b)")
        lnbuf = probs[:, 4:8, :].rearrange("p a b -> p (a b)")
        assert at[0] == 13432
        at[0] = 0
        gated_d = part(2, 512)
        hid_d = part(2, 512)
        at[0] = 0
        fin_g = part(D)
        fin_b = part(D)
        y_sum = part(TB, D)
        hid = part(ET)
        gated = part(ET)
        put = part(TB, P)
        put_g = part(TB, P)
        at[0] = 5752
        hTi = part(KB, P)
        y_item = part(D)
        put_gT = part(S)
        at[0] = 11896
        slot_no = part(P)
        e_rev = part(TB, E)
        e_idx = part(E)
        route = part(16, 16)
        hTi_hi, hTi_lo = (m[:, 0:4, :].rearrange("p a b -> p (a b)").rearrange("p (k n) -> p k n", k=KB)
                          for m in (mid_hi, mid_lo))
        hidT_hi, hidT_lo = (m[:, 4:6, :].rearrange("p a b -> p (a b)") for m in (mid_hi, mid_lo))
        at[0] = 0
        rows = part(4, P)
        at[0] = 12000
        iota_i = arena[:, 12000:12000 + 512].bitcast(I32)

        slot_in = [sem(f"slot_in{i}") for i in range(SLOTS)]
        rows_in = sem("rows_in")
        x_in = sem("x_in")
        sinks_in = sem("sinks_in")
        router_in = sem("router_in")
        router_split = sem("router_split")
        consts = sem("consts")
        cols_t = sem("cols_t")
        cols_ready = sem("cols_ready")
        c_ready = sem("c_ready")
        cw_ready = sem("cw_ready")
        dist_ready = sem("dist_ready")
        hi_ready = sem("hi_ready")
        lo_ready = sem("lo_ready")
        wts_used = sem("wts_used")
        ada_used = sem("ada_used")
        ada_cols_done = sem("ada_cols_done")
        mod_part_ready = sem("mod_part_ready")
        mod_raw_ready = sem("mod_raw_ready")
        scales_ready = sem("scales_ready")
        turn_done = sem("turn_done")
        hT_act = sem("hT_act")
        hT_dve = sem("hT_dve")
        in_hi_ready = sem("in_hi_ready")
        in_lo_ready = sem("in_lo_ready")
        o_hi_ready = sem("o_hi_ready")
        zT_hi_ready = sem("zT_hi_ready")
        zT_lo_ready = sem("zT_lo_ready")
        mg_hi_ready = sem("mg_hi_ready")
        mg_lo_ready = sem("mg_lo_ready")
        hid_hi_ready = sem("hid_hi_ready")
        hid_lo_ready = sem("hid_lo_ready")
        hidT_done = sem("hidT_done")
        hTi_hi_ready = sem("hTi_hi_ready")
        hTi_lo_ready = sem("hTi_lo_ready")
        sg_ready = sem("sg_ready")
        z_ready = sem("z_ready")
        pad_ready = sem("pad_ready")
        conv_step = sem("conv_step")
        q_ready = sem("q_ready")
        kv_ready = sem("kv_ready")
        gate_ready = sem("gate_ready")
        scores_done = sem("scores_done")
        biased = sem("biased")
        max_ready = sem("max_ready")
        exp_ready = sem("exp_ready")
        probs_ready = sem("probs_ready")
        probsT_done = sem("probsT_done")
        pT_ready = sem("pT_ready")
        pv_done = sem("pv_done")
        oT_ready = sem("oT_ready")
        convT_done = sem("convT_done")
        cvar_ready = sem("cvar_ready")
        csd_ready = sem("csd_ready")
        zn_ready = sem("zn_ready")
        normT_done = sem("normT_done")
        zT_ready = sem("zT_ready")
        gated_conv = sem("gated_conv")
        gated_attn = sem("gated_attn")
        merged = sem("merged")
        diag_ready = sem("diag_ready")
        gains_done = sem("gains_done")
        gains_ready = sem("gains_ready")
        y_gained = sem("y_gained")
        summed = sem("summed")
        stats = sem("stats")
        var_ready = sem("var_ready")
        sd_ready = sem("sd_ready")
        xn_ready = sem("xn_ready")
        ln_in = sem("ln_in")
        x_ready = sem("x_ready")
        silu_ready = sem("silu_ready")
        hid_ready = sem("hid_ready")
        gap_ready = sem("gap_ready")
        gap_exp = sem("gap_exp")
        router_done = sem("router_done")
        mask_ready = sem("mask_ready")
        ranks_done = sem("ranks_done")
        items_ready = sem("items_ready")
        put_ready = sem("put_ready")
        put_g_ready = sem("put_g_ready")
        gather_done = sem("gather_done")
        hTi_ready = sem("hTi_ready")
        putT_done = sem("putT_done")
        putT_ready = sem("putT_ready")
        y_item_ready = sem("y_item_ready")
        scatter_done = sem("scatter_done")
        y_added = sem("y_added")
        fin_in = sem("fin_in")
        out_ready = sem("out_ready")
        out_done = sem("out_done")
        dve_chain = sem("dve_chain")
        pool_chain = sem("pool_chain")

        def source(g):
            kind, l, i, h = g
            first = {"q": 0, "kv": 2, "u": 3, "gate": 5}
            if kind == "ffn_up":
                return (ffn_w1, ffn_w3)[h][0].rearrange("(kb p) n -> p kb n", p=P)[:, :, FT * i:FT * i + FT]
            if kind == "ffn_down":
                return ffn_w2[0, FT * i:FT * i + FT].rearrange("(kb p) n -> p kb n", p=P)
            if kind == "conv_out":
                return w_conv_out[l, 256 * h:256 * h + 256].rearrange("(kb p) n -> p kb n", p=P)
            w, j = {"ada": (w_ada, i), "attn_out": (w_attn_out, i), "w_o": (w_o, i)}.get(
                kind, (w_in, first.get(kind, 0) + i))
            return w[l, 512 * h:512 * h + 512].rearrange("(kb p) n -> p kb n", p=P)[:, :, 512 * j:512 * j + 512]

        def rows_of(kind):
            return {"ffn_up": KB, "ffn_down": 2, "conv_out": 2}.get(kind, 4)

        def cut_in(v, k):
            return v.rearrange("p (k n) -> p k n", k=k)

        moe1 = moe_w1.rearrange("a e (kb p) n -> (a e) p kb n", p=P)
        moe3 = moe_w3.rearrange("a e (kb p) n -> (a e) p kb n", p=P)
        moe2 = moe_w2.rearrange("a e (kb p) n -> (a e) p kb n", p=P)

        def used(step):
            kind, l, i = step
            return split_no[(kind, l, i, 0 if kind == "ffn_down" else 1)] + 1

        bank_of = {}
        block = ctx.enter_context(nc.Block())

        @block.tensor
        def _(pe):
            holder = [None] * 8
            turn, size = [0], [8]

            def take(key, freed_by, banks=None):
                if banks is None:
                    b = turn[0] % size[0]
                    turn[0] += 1
                else:
                    b = banks
                if holder[b] is not None:
                    pe.wait_ge(*holder[b])
                holder[b] = freed_by
                bank_of[key] = b
                return b

            def split(g):
                k = split_no[g]
                pe.wait_ge(lo_ready, k + 1)
                n = rows_of(g[0])
                return cut_in(w_hi[:, k % AHEAD, :], n), cut_in(w_lo[:, k % AHEAD, :], n)

            def product(to, stat, stat_at, mov, mov_at, start, stop):
                (sh, sl), (mh, ml) = stat, mov
                nc.tensor.matmul(to, sh[stat_at], mh[mov_at], start=start, stop=False, skip_group_check=True)
                nc.tensor.matmul(to, sh[stat_at], ml[mov_at], start=False, stop=False, skip_group_check=True)
                return nc.tensor.matmul(to, sl[stat_at], mh[mov_at], start=False, stop=stop, skip_group_check=True)

            whole = slice(None)
            layer_in, inner = (in_hi, in_lo), (mid_hi, mid_lo)

            def block(n, k=P):
                return slice(k * n, k * n + k)

            pe.wait_ge(rows_in, 16 * 11)
            pe.wait_ge(consts, 1)
            b = take(("cols", 0), (cols_ready, 4))
            for j, r in enumerate((128, 64, 124, 124)):
                mm = nc.tensor.transpose(ps[:, b, 128 * j:128 * j + r], rows[0:r, j, :], ident[0:r, 0:r])
            mm.then_inc(cols_t, 1)
            pe.wait_ge(cw_ready, 1)
            pe.wait_ge(consts, 4)

            def ada(l, i):
                b = take(("ada", l, i), (mod_part_ready, 12 * l + i + 1))
                for r in range(2):
                    n = ring_no[("ada", l, i, r)]
                    pe.wait_ge(slot_in[landed(n)[0]], landed(n)[1])
                    w = cut_in(ring[:, n % SLOTS, :], 4)
                    for j in range(4):
                        mm = nc.tensor.matmul(ps[32 * j:32 * j + 32, b, :], c_wide[:, 4 * r + j, :], w[:, j, :],
                                              start=(r == 0), stop=(r == 1), tile_position=(0, 32 * j))
                    mm.then_inc(ada_used, 1)

            def ada_cols(l, i):
                n = 12 * l + i
                b = take(("ada_cols", l, i), (mod_raw_ready, n + 1))
                pe.wait_ge(mod_part_ready, n + 1)
                for j in range(4):
                    mm = nc.tensor.matmul(ps[:, b, j:j + 1], mod_part[:, P * j:P * j + P], pick4[:, :],
                                          start=True, stop=True)
                mm.then_inc(ada_cols_done, 1)

            def turn_stream(s, _):
                src = x_tok if s == 0 else xn
                if s == 0:
                    pe.wait_ge(x_in, 16)
                else:
                    pe.wait_ge(xn_ready, 2 * s)
                for j in range(4):
                    b = take(("turn", s, j), (hT_dve if j % 2 else hT_act, 4 * s + 2 * (j // 2) + 2))
                    for kb in (2 * j, 2 * j + 1):
                        for t in range(TB):
                            mm = nc.tensor.transpose(
                                ps[:, b, S * (kb % 2) + P * t:S * (kb % 2) + P * t + P],
                                src[:, t, P * kb:P * kb + P], ident[:, :])
                    mm.then_inc(turn_done, 1)

            def input_ready(l, kind, kb):
                if kind == "u":
                    pe.wait_ge(in_lo_ready, 8 * l + kb // 2 + 1)

            def project(kind, freed_by, act=layer_in):
                def run(l, i):
                    banks = [take((kind, l, i, h), freed_by(l, i, h)) for h in range(2)]
                    for g in range(2):
                        w = split((kind, l, i, g))
                        for j in range(4):
                            for k in range(4):
                                if j == 0:
                                    input_ready(l, kind, 4 * g + k)
                                mm = product(ps[:, banks[j // 2], block(j % 2, S)], w, (whole, k, block(j)),
                                             act, (whole, 4 * g + k),
                                             start=(g == 0 and k == 0 and j % 2 == 0), stop=(g == 1 and k == 3))
                        mm.then_inc(wts_used, 1)
                return run

            def kv(l, _):
                bk = take(("kv", l, 0), (kv_ready, 5 * l + 4))
                bv = take(("kv", l, 1), (kv_ready, 5 * l + 5))
                for g in range(2):
                    w = split(("kv", l, 0, g))
                    for j in range(2):
                        for k in range(4):
                            first, last = g == 0 and k == 0 and j == 0, g == 1 and k == 3
                            product(ps[:, bk, block(j, S)], w, (whole, k, block(j)), layer_in, (whole, 4 * g + k),
                                    start=first, stop=last)
                            mm = product(ps[:, bv, block(j, S)], layer_in, (whole, 4 * g + k, block(j)),
                                         w, (whole, k, slice(256, 512)), start=first, stop=last)
                    mm.then_inc(wts_used, 1)

            def scores(l, g):
                if g == 0:
                    pe.wait_ge(q_ready, 4 * (l + 1))
                    pe.wait_ge(kv_ready, 5 * (l + 1))
                for i in range(GRP):
                    h = GRP * g + i
                    half = HD * (h % 2)
                    b = take(("scores", l, g, i), (biased, 16 * l + h + 1))
                    for t in range(TB):
                        mm = nc.tensor.matmul(ps[:, b, S * t:S * t + S],
                                              qT[half:half + HD, h // 2, P * t:P * t + P],
                                              kT[half:half + HD, g, :], start=True, stop=True)
                    mm.then_inc(scores_done, 1)

            def probs_turn(l, g):
                pe.wait_ge(probs_ready, 8 * (4 * l + g + 1))
                for i in range(GRP):
                    b = take(("probsT", l, g, i), (pT_ready, 16 * l + GRP * g + i + 1))
                    for n, (t, kb) in enumerate(((0, 0), (1, 0), (1, 1))):
                        mm = nc.tensor.transpose(ps[:, b, P * n:P * n + P],
                                                 probs[:, 2 * i + t, P * kb:P * kb + P], ident[:, :])
                    mm.then_inc(probsT_done, 1)

            def pv(l, g):
                pe.wait_ge(pT_ready, 16 * l + GRP * (g + 1))
                b = take(("pv", l, g), (oT_ready, 4 * l + g + 1))
                for i in range(GRP):
                    half, c0 = HD * (i % 2), S * (i // 2)
                    for n, (t, kb) in enumerate(((0, 0), (1, 0), (1, 1))):
                        mm = nc.tensor.matmul(ps[half:half + HD, b, c0 + P * t:c0 + P * t + P],
                                              v_tok[:, kb, HD * g:HD * g + HD], pT[:, i, P * n:P * n + P],
                                              start=(n != 2), stop=(n != 1), tile_position=(0, half))
                mm.then_inc(pv_done, 1)

            def conv_turn(l, _):
                pe.wait_ge(conv_step, CB * TAPS * (l + 1))
                for t in range(TB):
                    b = take(("convT", l, t), (zn_ready, 2 * l + t + 1))
                    for cb in range(CB):
                        mm = nc.tensor.transpose(ps[:, b, P * cb:P * cb + P],
                                                 conv[:, cb, P * t:P * t + P], ident[:, :])
                    mm.then_inc(convT_done, 1)

            def norm_turn(l, _):
                pe.wait_ge(zn_ready, 2 * (l + 1))
                for j in range(2):
                    b = take(("normT", l, j), (zT_ready, 4 * l + 2 * j + 2))
                    for cb in (2 * j, 2 * j + 1):
                        for t in range(TB):
                            mm = nc.tensor.transpose(
                                ps[:, b, S * (cb % 2) + P * t:S * (cb % 2) + P * t + P],
                                zn[:, t, P * cb:P * cb + P], ident[:, :])
                    mm.then_inc(normT_done, 1)

            def conv_out(l, _):
                pe.wait_ge(zT_lo_ready, l + 1)
                banks = [take(("conv_out", l, j), (gated_conv, 4 * l + j + 1)) for j in range(4)]
                for g in range(2):
                    w = split(("conv_out", l, 0, g))
                    for j in range(8):
                        for k in range(2):
                            mm = product(ps[:, banks[j // 2], block(j % 2, S)], w, (whole, k, block(j)),
                                         layer_in, (whole, 2 * g + k),
                                         start=(g == 0 and k == 0 and j % 2 == 0), stop=(g == 1 and k == 1))
                    mm.then_inc(wts_used, 1)

            def attn_out(l, i):
                if i == 0:
                    pe.wait_ge(oT_ready, 4 * (l + 1))
                project("attn_out", lambda l, i, h: (gated_attn, 4 * l + 2 * i + h + 1), inner)(l, i)

            def out_proj(l, i):
                if i == 0:
                    pe.wait_ge(mg_lo_ready, 4 * (l + 1))
                banks = [take(("y", 2 * l, t, i), (y_gained, 8 * l + 2 * i + t + 1)) for t in range(TB)]
                for g in range(2):
                    w = split(("w_o", l, i, g))
                    for t in range(TB):
                        for k in range(4):
                            mm = product(ps[:, banks[t], :], inner, (whole, 4 * g + k, block(t)), w, (whole, k),
                                         start=(g == 0 and k == 0), stop=(g == 1 and k == 3))
                    mm.then_inc(wts_used, 1)

            def spread_gains(s, _):
                pe.wait_ge(diag_ready, s + 1)
                for h in range(2):
                    b = take(("gains", s, h), (gains_ready, 2 * s + h + 1))
                    mm = nc.tensor.matmul(ps[:, b, :], ones[:, :], lnbuf[:, 512 * h:512 * h + 512],
                                          start=True, stop=True)
                mm.then_inc(gains_done, 1)

            def ffn_up(l, f):
                if f == 0:
                    pe.wait_ge(in_lo_ready, 8)
                for h in range(2):
                    b = take(("ffn_up", f, h), (hid_ready, f + 1))
                    w = split(("ffn_up", 0, f, h))
                    for j in range(2):
                        for kb in range(KB):
                            mm = product(ps[:, b, block(j, S)], w, (whole, kb, block(j)), layer_in, (whole, kb),
                                         start=(kb == 0), stop=(kb == KB - 1))
                    mm.then_inc(wts_used, 1)

            def ffn_down(l, f):
                w = split(("ffn_down", 0, f, 0))
                if f == 0:
                    for h in range(2):
                        for t in range(TB):
                            take(("y", 1, t, h), (y_gained, 4 + 2 * h + t + 1), 4 + 2 * t + h)
                pe.wait_ge(hid_lo_ready, f + 1)
                for h in range(2):
                    for t in range(TB):
                        for j in range(2):
                            mm = product(ps[:, 4 + 2 * t + h, :], inner, (whole, 2 * (f % 2) + j, block(t)),
                                         w, (whole, j, block(h, 512)),
                                         start=(f == 0 and j == 0), stop=(f == NFT - 1 and j == 1))
                mm.then_inc(wts_used, 1)

            def router(l, _):
                pe.wait_ge(router_split, 2)
                pe.wait_ge(in_lo_ready, 16)
                b = take(("router", 0), (mask_ready, 1))
                for t in range(TB):
                    for kb in range(KB):
                        mm = product(ps[:, b, block(t, E)], layer_in, (whole, kb, block(t)),
                                     (router_hi, router_lo), (whole, kb), start=(kb == 0), stop=(kb == KB - 1))
                mm.then_inc(router_done, 1)

            def ranks(l, _):
                pe.wait_ge(mask_ready, 1)
                b = take(("ranks", 0), (items_ready, 1))
                m0, m1 = route[:, 0, 0:E], route[:, 0, E:2 * E]
                nc.tensor.matmul(ps[:, b, 0:E], before[:, :], m0, start=True, stop=True)
                nc.tensor.matmul(ps[:, b, E:2 * E], ones[:, :], m0, start=True, stop=False)
                nc.tensor.matmul(ps[:, b, E:2 * E], before[:, :], m1, start=False, stop=True)
                nc.tensor.matmul(ps[:, b, 2 * E:3 * E], ones[:, :], m0, start=True, stop=False)
                nc.tensor.matmul(ps[:, b, 2 * E:3 * E], ones[:, :], m1, start=False, stop=True)\
                    .then_inc(ranks_done, 1)

            do = {"ada": ada, "ada_cols": ada_cols, "turn": turn_stream,
                  "u": project("u", lambda l, i, h: (z_ready, 2 * l + h + 1)),
                  "q": project("q", lambda l, i, h: (q_ready, 4 * l + 2 * i + h + 1)),
                  "gate": project("gate", lambda l, i, h: (gate_ready, 8 * l + 2 * i + h + 1)),
                  "kv": kv, "scores": scores, "probsT": probs_turn, "pv": pv, "convT": conv_turn,
                  "normT": norm_turn, "conv_out": conv_out, "attn_out": attn_out, "w_o": out_proj,
                  "gains": spread_gains, "ffn_up": ffn_up, "ffn_down": ffn_down, "router": router,
                  "ranks": ranks}
            for kind, l, i in steps:
                if kind == "ffn_up" and i == 0:
                    turn[0], size[0] = 0, 4
                if kind == "turn":
                    turn[0], size[0] = 0, 8
                do[kind](l, i)

            for b in range(8):
                if holder[b] is not None:
                    pe.wait_ge(*holder[b])

            def gather(n):
                pe.wait_ge(put_ready, 2 * n)
                for h in range(2):
                    for j in range(4):
                        kb = 4 * h + j
                        for t in range(TB):
                            mm = nc.tensor.matmul(ps[:, 5 + h, P * j:P * j + P], xn[:, t, P * kb:P * kb + P],
                                                  put[:, t, :], start=(t == 0), stop=(t == TB - 1))
                mm.then_inc(gather_done, 1)

            gather(1)
            pe.sem_inc(putT_done, 1)
            pe.sem_inc(scatter_done, 1)
            n_items = pe.value_load(items_i[0:1, 0:1], min_val=E, max_val=MAX_ITEMS)
            with pe.Fori(0, n_items) as it:
                def item_split(j, k):
                    pe.wait_ge(lo_ready, it * ITEM_GRAINS + (K0 + j + 1))
                    n = (K0 + j) % AHEAD
                    return cut_in(w_hi[:, n, :], k), cut_in(w_lo[:, n, :], k)

                def up(f):
                    for h in range(2):
                        for g in range(2):
                            w = item_split(up_at(f) + 2 * h + g, 4)
                            for k in range(4):
                                mm = product(ps[:, h, :], (hTi_hi, hTi_lo), (whole, 4 * g + k), w, (whole, k),
                                             start=(g == 0 and k == 0), stop=(g == 1 and k == 3))
                            mm.then_inc(wts_used, 1)

                def turn_hidden(f):
                    pe.wait_ge(hid_ready, it * NET + (NFT + f + 1))
                    for j in range(4):
                        mm = nc.tensor.transpose(ps[:, 2, block(j)], hid[:, block(j)], ident[:, :])
                    mm.then_inc(hidT_done, 1)

                def down(f):
                    pe.wait_ge(hid_lo_ready, it * NET + (NFT + f + 1))
                    if f == 0:
                        pe.wait_ge(y_item_ready, it * 2 + 1)
                    for g in range(2):
                        w = item_split(down_at(f) + g, 2)
                        for h in range(2):
                            for k in range(2):
                                mm = product(ps[:, 3 + h, :], (hidT_hi, hidT_lo), (whole, block(2 * g + k)),
                                             w, (whole, k, block(h, 512)),
                                             start=(f == 0 and g == 0 and k == 0),
                                             stop=(f == NET - 1 and g == 1 and k == 1))
                        mm.then_inc(wts_used, 1)

                pe.wait_ge(hTi_lo_ready, it + 1)
                for f in range(NET):
                    up(f)
                    if f == 0:
                        pe.wait_ge(y_added, it * 4 + 1)
                        pe.wait_ge(put_g_ready, it * 2 + 2)
                        for t in range(TB):
                            mm = nc.tensor.transpose(ps[:, 7, block(t)], put_g[:, t, :], ident[:, :])
                        mm.then_inc(putT_done, 1)
                    else:
                        down(f - 1)
                    turn_hidden(f)
                gather(it + 2)
                down(NET - 1)
                pe.wait_ge(putT_ready, it + 1)
                for n, (h, t) in enumerate(((0, 0), (0, 1), (1, 0), (1, 1))):
                    b = (7, 5, 6, 7)[n]
                    if t == 0:
                        pe.wait_ge(y_item_ready, it * 2 + (h + 2))
                    if n == 1:
                        pe.wait_ge(hTi_ready, it * 8 + 16)
                    if n == 3:
                        pe.wait_ge(y_added, it * 4 + 2)
                    nc.tensor.matmul(ps[:, b, :], put_gT[:, block(t)], y_item[:, block(h, 512)],
                                     start=True, stop=True).then_inc(scatter_done, 1)

        @block.scalar
        def _(act):
            act.dma_start(sinks[:, :], attn_sinks.rearrange("l h -> (l h)").partition_broadcast(P)).then_inc(sinks_in, 16)
            act.dma_start(w_router[:, :, :], moe_router[0].rearrange("(kb p) e -> p kb e", p=P)).then_inc(router_in, 16)

            act.wait_ge(cols_t, 1)
            act.wait_ge(consts, 4)
            b = bank_of[("cols", 0)]
            for j, r in enumerate((128, 64, 124, 124)):
                nc.scalar.copy(cols[:, P * j:P * j + r], ps[:, b, P * j:P * j + r]).then_inc(cols_ready, 1)
            act.wait_ge(cols_ready, 4)
            nc.scalar.activation(c_act[:, :], cols[:, C_C:C_C + KB], ACT.Silu).then_inc(c_ready, 1)

            def weights_done(step):
                act.wait_ge(wts_used, used(step))

            split_order = [g for g in load if g[0] != "ada"]

            def high(k):
                if k >= K0:
                    slot, value = landed(R0 + k - K0)
                else:
                    slot, value = landed(ring_no[split_order[k]])
                act.wait_ge(slot_in[slot], value)
                if k >= AHEAD:
                    act.wait_ge(wts_used, k - AHEAD + 1)
                nc.scalar.copy(w_hi[:, k % AHEAD, :], ring[:, slot, :]).then_inc(hi_ready, 1)

            def ada(l, i):
                n = 12 * l + i
                act.wait_ge(ada_used, 2 * (n + 1))
                if n:
                    act.wait_ge(ada_cols_done, n)
                nc.scalar.copy(mod_part[:, :], ps[:, bank_of[("ada", l, i)], :]).then_inc(mod_part_ready, 1)

            def ada_cols(l, i):
                act.wait_ge(ada_cols_done, 12 * l + i + 1)
                nc.scalar.copy(mod_raw[:, l, 4 * i:4 * i + 4], ps[:, bank_of[("ada_cols", l, i)], 0:4])\
                    .then_inc(mod_raw_ready, 1)

            def turn_stream(s, _):
                act.wait_ge(scales_ready, s + 1)
                for j in range(4):
                    if j % 2 == 0:
                        act.wait_ge(turn_done, 4 * s + j + 1)
                        for kb in (2 * j, 2 * j + 1):
                            nc.scalar.activation(hT[:, kb, :], ps[:, bank_of[("turn", s, j)], S * (kb % 2):S * (kb % 2) + S],
                                                 ACT.Identity, bias=shift_c[:, s, kb:kb + 1],
                                                 scale=scale_c[:, s, kb:kb + 1]).then_inc(hT_act, 1)
                        act.wait_ge(hT_act, 4 * s + j + 2)
                    else:
                        act.wait_ge(hT_dve, 4 * s + j + 1)
                    nc.scalar.copy(in_hi[:, 2 * j:2 * j + 2, :], hT[:, 2 * j:2 * j + 2, :]).then_inc(in_hi_ready, 1)

            def u(l, i):
                if i == 1:
                    weights_done(("u", l, 1))
                    for h in range(2):
                        nc.scalar.activation(conv[:, 2 * h:2 * h + 2, :].rearrange("p a b -> p (a b)"),
                                             ps[:, bank_of[("u", l, 1, h)], :], ACT.Sigmoid).then_inc(sg_ready, 1)

            def q(l, i):
                weights_done(("q", l, i))
                for h in range(2):
                    kb = 4 * i + 2 * h
                    nc.scalar.mul(qT[:, kb:kb + 2, :].rearrange("p a b -> p (a b)"),
                                  ps[:, bank_of[("q", l, i, h)], :], HD ** -0.5).then_inc(q_ready, 1)

            def kv(l, _):
                weights_done(("kv", l, 0))
                src = ps[:, bank_of[("kv", l, 0)], :].rearrange("p (a b) -> p a b", a=2)
                for half in range(2):
                    for to in range(2):
                        nc.scalar.copy(kT[HD * to:HD * to + HD, half::2, :],
                                       src[HD * half:HD * half + HD, :, :]).then_inc(kv_ready, 1)
                nc.scalar.copy(v_tok.rearrange("p a b -> p (a b)"), ps[:, bank_of[("kv", l, 1)], :])\
                    .then_inc(kv_ready, 1)

            def gate(l, i):
                weights_done(("gate", l, i))
                for h in range(2):
                    kb = 4 * i + 2 * h
                    nc.scalar.activation(gT[:, kb:kb + 2, :].rearrange("p a b -> p (a b)"),
                                         ps[:, bank_of[("gate", l, i, h)], :], ACT.Sigmoid).then_inc(gate_ready, 1)

            def scores(l, g):
                n = 4 * l + g
                act.wait_ge(max_ready, n + 1)
                nc.scalar.activation(st_esink[:, :], st_dsink[:, :], ACT.Exp).then_inc(exp_ready, 1)
                for j in range(8):
                    nc.scalar.activation(probs[:, j, :], probs[:, j, :], ACT.Exp, bias=st_neg[:, j:j + 1],
                                         accum_out=st_den[:, j:j + 1]).then_inc(exp_ready, 1)

            def probs_turn(l, g):
                for i in range(GRP):
                    act.wait_ge(probsT_done, 16 * l + GRP * g + i + 1)
                    if i == 0 and 4 * l + g:
                        act.wait_ge(pv_done, 4 * l + g)
                    nc.scalar.copy(pT[:, i, :], ps[:, bank_of[("probsT", l, g, i)], 0:3 * P]).then_inc(pT_ready, 1)

            def pv(l, g):
                act.wait_ge(pv_done, 4 * l + g + 1)
                nc.scalar.copy(mid_hi[:, 2 * g:2 * g + 2, :].rearrange("p a b -> p (a b)"),
                               ps[:, bank_of[("pv", l, g)], :]).then_inc(o_hi_ready, 1)

            def conv_turn(l, _):
                for t in range(TB):
                    act.wait_ge(cvar_ready, 2 * l + t + 1)
                    nc.scalar.activation(sd[:, t:t + 1], mv[:, t, 1:2], ACT.Sqrt, bias=epsc[:, 0:1]).then_inc(csd_ready, 1)

            def norm_turn(l, _):
                for j in range(2):
                    act.wait_ge(normT_done, 2 * l + j + 1)
                    for cb in (2 * j, 2 * j + 1):
                        nc.scalar.activation(zT[:, cb, :], ps[:, bank_of[("normT", l, j)], S * (cb % 2):S * (cb % 2) + S],
                                             ACT.Silu, bias=cols[:, C_CB + CB * l + cb:C_CB + CB * l + cb + 1],
                                             scale=cols[:, C_CG + CB * l + cb:C_CG + CB * l + cb + 1]).then_inc(zT_ready, 1)
                act.wait_ge(zT_ready, 4 * (l + 1))
                nc.scalar.copy(in_hi[:, 0:CB, :], zT).then_inc(zT_hi_ready, 1)

            def conv_out(l, _):
                for j in range(4):
                    act.wait_ge(merged, 4 * l + j + 1)
                    nc.scalar.copy(mid_hi[:, 2 * j:2 * j + 2, :], gT[:, 2 * j:2 * j + 2, :]).then_inc(mg_hi_ready, 1)

            def spread_gains(s, _):
                act.wait_ge(gains_done, s + 1)
                if s:
                    act.wait_ge(y_gained, 4 * s)
                for h in range(2):
                    nc.scalar.copy(gains[:, 512 * h:512 * h + 512], ps[:, bank_of[("gains", s, h)], :])\
                        .then_inc(gains_ready, 1)

            def residual(s):
                for t in range(TB):
                    act.wait_ge(var_ready, 2 * s + t + 1)
                    nc.scalar.activation(sd[:, t:t + 1], mv[:, t, 1:2], ACT.Sqrt, bias=epsc[:, 0:1]).then_inc(sd_ready, 1)

            def out_proj(l, i):
                if i == 1:
                    residual(2 * l)

            def ffn_up(l, f):
                weights_done(("ffn_up", 0, f))
                if f >= 2:
                    act.wait_ge(hid_ready, f - 1)
                nc.scalar.activation(gated_d[:, f % 2, :], ps[:, bank_of[("ffn_up", f, 0)], :], ACT.Silu)\
                    .then_inc(silu_ready, 1)
                act.wait_ge(hid_ready, f + 1)
                if f >= 2:
                    weights_done(("ffn_down", 0, f - 2))
                nc.scalar.copy(mid_hi[:, 2 * (f % 2):2 * (f % 2) + 2, :].rearrange("p a b -> p (a b)"),
                               hid_d[:, f % 2, :]).then_inc(hid_hi_ready, 1)

            def ffn_down(l, f):
                if f == NFT - 1:
                    residual(1)

            def router(l, _):
                act.wait_ge(gap_ready, 1)
                nc.scalar.activation(route[:, 11, 0:2], route[:, 9, 0:2], ACT.Exp).then_inc(gap_exp, 1)

            do = {"ada": ada, "ada_cols": ada_cols, "turn": turn_stream, "u": u, "q": q, "kv": kv,
                  "gate": gate, "scores": scores, "probsT": probs_turn, "pv": pv, "convT": conv_turn,
                  "normT": norm_turn, "conv_out": conv_out, "gains": spread_gains, "w_o": out_proj,
                  "ffn_up": ffn_up, "ffn_down": ffn_down, "router": router}
            for kind, l, i in steps:
                if kind == "turn" and l == 0:
                    for k in range(AHEAD):
                        high(k)
                mine = [k for g, k in split_no.items() if g[:3] == (kind, l, i)]
                for k in mine[:-1]:
                    high(k + AHEAD)
                if kind in do:
                    do[kind](l, i)
                for k in mine[-1:]:
                    high(k + AHEAD)

            def gathered():
                for j in range(4):
                    nc.scalar.activation(hTi[:, j, :], ps[:, 5, P * j:P * j + P], ACT.Identity,
                                         bias=shift_c[:, 3, j:j + 1], scale=scale_c[:, 3, j:j + 1]).then_inc(hTi_ready, 1)

            act.sem_inc(y_item_ready, 1)
            act.wait_ge(gather_done, 1)
            gathered()
            act.wait_ge(hTi_ready, 8)
            nc.scalar.copy(hTi_hi, hTi).then_inc(hTi_hi_ready, 1)
            n_items = act.value_load(items_i[0:1, 0:1], min_val=E, max_val=MAX_ITEMS)
            with act.Fori(0, n_items) as it:
                def item_high(j):
                    slot, value = landed(R0 + j)
                    act.wait_ge(slot_in[slot], it * (16 * ITEM_GRAINS // SLOTS) + value)
                    act.wait_ge(wts_used, it * ITEM_GRAINS + (K0 + j - AHEAD + 1))
                    nc.scalar.copy(w_hi[:, (K0 + j) % AHEAD, :], ring[:, slot, :]).then_inc(hi_ready, 1)

                for f in range(NET):
                    for g in range(3):
                        item_high(up_at(f) + g + AHEAD)
                    act.wait_ge(wts_used, it * ITEM_GRAINS + (K0 + up_at(f) + 4))
                    act.wait_ge(hid_ready, it * NET + (NFT + f))
                    nc.scalar.activation(gated, ps[:, 0, :], ACT.Silu).then_inc(silu_ready, 1)
                    item_high(up_at(f) + 3 + AHEAD)
                    if f == 0:
                        act.wait_ge(putT_done, it + 2)
                        act.wait_ge(scatter_done, it * 4 + 1)
                        nc.scalar.copy(put_gT[:, :], ps[:, 7, 0:S]).then_inc(putT_ready, 1)
                    else:
                        for g in range(2):
                            item_high(down_at(f - 1) + g + AHEAD)
                    act.wait_ge(hidT_done, it * NET + (f + 1))
                    nc.scalar.copy(hidT_hi, ps[:, 2, :]).then_inc(hid_hi_ready, 1)
                act.wait_ge(gather_done, it + 2)
                gathered()
                act.wait_ge(hTi_ready, it * 8 + 16)
                nc.scalar.copy(hTi_hi, hTi).then_inc(hTi_hi_ready, 1)
                item_high(down_at(NET - 1) + AHEAD)
                act.wait_ge(wts_used, it * ITEM_GRAINS + (K0 + ITEM_GRAINS))
                for h in range(2):
                    nc.scalar.copy(y_item[:, 512 * h:512 * h + 512], ps[:, 3 + h, :]).then_inc(y_item_ready, 1)
                item_high(down_at(NET - 1) + 1 + AHEAD)
            residual(3)

        @block.vector
        def _(dve):
            count = [0]

            def link(ins):
                count[0] += 1
                ins.then_inc(dve_chain, 1)
                dve.wait_ge(dve_chain, count[0])

            dve.wait_ge(c_ready, 1)
            dve.wait_ge(consts, 3)
            for kb in range(KB):
                ins = nc.vector.tensor_scalar(c_wide[:, kb, :], ones[:, 0:32], c_act[:, kb:kb + 1], None, ALU.mult)
            ins.then_inc(cw_ready, 1)
            nd = neg_dist[:, :, :].rearrange("p a b -> p (a b)")
            link(nc.vector.tensor_copy(nd, iota_i))
            link(nc.vector.scalar_tensor_tensor(out=nd, in0=nd, scalar=-1.0, in1=nd, op0=ALU.mult, op1=ALU.min))
            for p0, t, a, z in ((0, 0, CHUNK, S), (CHUNK, 0, 2 * CHUNK, S), (0, 1, 0, CHUNK),
                                (0, 1, 3 * CHUNK, S), (CHUNK, 1, 0, 2 * CHUNK)):
                link(nc.vector.memset(neg_dist[p0:p0 + CHUNK, t, a:z], FAR))

            def weights_done(step):
                dve.wait_ge(wts_used, used(step))

            split_order = [g for g in load if g[0] != "ada"]

            def low(k):
                slot, _ = landed(R0 + k - K0 if k >= K0 else ring_no[split_order[k]])
                dve.wait_ge(hi_ready, k + 1)
                nc.vector.tensor_tensor(w_lo[:, k % AHEAD, :], ring[:, slot, :], w_hi[:, k % AHEAD, :].bitcast(F32),
                                        ALU.subtract).then_inc(lo_ready, 1)

            def turn_stream(s, _):
                dve.wait_ge(scales_ready, s + 1)
                for j in range(4):
                    if j % 2:
                        dve.wait_ge(turn_done, 4 * s + j + 1)
                        for kb in (2 * j, 2 * j + 1):
                            nc.vector.tensor_scalar(hT[:, kb, :], ps[:, bank_of[("turn", s, j)], S * (kb % 2):S * (kb % 2) + S],
                                                    scale_c[:, s, kb:kb + 1], shift_c[:, s, kb:kb + 1],
                                                    ALU.mult, ALU.add).then_inc(hT_dve, 1)
                for j in range(4):
                    dve.wait_ge(in_hi_ready, 4 * s + j + 1)
                    v = slice(2 * j, 2 * j + 2)
                    nc.vector.tensor_tensor(in_lo[:, v, :], hT[:, v, :], in_hi[:, v, :].bitcast(F32),
                                            ALU.subtract).then_inc(in_lo_ready, 1)

            def u(l, i):
                if i == 0:
                    link(nc.vector.memset(zp[:, :, 0:PAD], 0.0))
                    return
                for h in range(2):
                    dve.wait_ge(sg_ready, 2 * l + h + 1)
                    nc.vector.tensor_tensor(zp[:, 2 * h:2 * h + 2, PAD:PAD + S],
                                            ps[:, bank_of[("u", l, 0, h)], :].rearrange("p (a b) -> p a b", a=2),
                                            conv[:, 2 * h:2 * h + 2, :], ALU.mult).then_inc(z_ready, 1)
                dve.wait_ge(z_ready, 2 * (l + 1))

            def taps(l, a, z):
                base = CB * TAPS * l
                for n in range(a, z):
                    j, cb = n // CB, n % CB
                    col = C_DW + P * l + n
                    w = cols[:, col:col + 1]
                    if j == 0:
                        ins = nc.vector.tensor_scalar(conv[:, cb, :], zp[:, cb, 0:S], w,
                                                      cols[:, C_DWB + CB * l + cb:C_DWB + CB * l + cb + 1],
                                                      ALU.mult, ALU.add)
                    else:
                        dve.wait_ge(conv_step, base + n - CB + 1)
                        ins = nc.vector.scalar_tensor_tensor(out=conv[:, cb, :], in0=zp[:, cb, j:j + S], scalar=w,
                                                             in1=conv[:, cb, :], op0=ALU.mult, op1=ALU.add)
                    ins.then_inc(conv_step, 1)

            def scores(l, g):
                n = 4 * l + g
                if l == 0 and g == 0:
                    dve.wait_ge(sinks_in, 16)
                for i in range(GRP):
                    h = GRP * g + i
                    dve.wait_ge(scores_done, 16 * l + h + 1)
                    if i == 0 and n:
                        dve.wait_ge(probsT_done, 4 * n)
                    if i == 0 and l and g == 0:
                        dve.wait_ge(x_ready, 4)
                    slope = 2.0 ** (-8.0 * (h + 1) / HEADS)
                    nc.vector.scalar_tensor_tensor(out=probs[:, 2 * i:2 * i + 2, :].rearrange("p a b -> p (a b)"),
                                                   in0=nd, scalar=slope,
                                                   in1=ps[:, bank_of[("scores", l, g, i)], :],
                                                   op0=ALU.mult, op1=ALU.add).then_inc(biased, 1)
                dve.wait_ge(biased, 4 * (n + 1))
                if n:
                    dve.wait_ge(exp_ready, 9 * n)
                sk = sinks[:, HEADS * l + GRP * g:HEADS * l + GRP * (g + 1)].unsqueeze(2).to_broadcast([P, GRP, TB])
                by_head = lambda v: v[:, :].rearrange("p (a b) -> p a b", a=GRP)
                link(nc.vector.tensor_reduce(st_max[:, :], probs, AX.X, ALU.max))
                link(nc.vector.tensor_tensor(by_head(st_max), by_head(st_max), sk, ALU.max))
                link(nc.vector.tensor_scalar(st_neg[:, :], st_max[:, :], -1.0, None, ALU.mult))
                nc.vector.tensor_tensor(by_head(st_dsink), sk, by_head(st_max), ALU.subtract).then_inc(max_ready, 1)

            def normalise(l, g):
                n = 4 * l + g
                dve.wait_ge(exp_ready, 9 * (n + 1))
                link(nc.vector.tensor_tensor(st_den[:, :], st_den[:, :], st_esink[:, :], ALU.add))
                link(nc.vector.reciprocal(st_rden[:, :], st_den[:, :]))
                for j in range(8):
                    nc.vector.tensor_scalar(probs[:, j, :], probs[:, j, :], st_rden[:, j:j + 1], None,
                                            ALU.mult).then_inc(probs_ready, 1)

            def pv(l, g):
                dve.wait_ge(o_hi_ready, 4 * l + g + 1)
                v = slice(2 * g, 2 * g + 2)
                nc.vector.tensor_tensor(mid_lo[:, v, :].rearrange("p a b -> p (a b)"), ps[:, bank_of[("pv", l, g)], :],
                                        mid_hi[:, v, :].bitcast(F32).rearrange("p a b -> p (a b)"),
                                        ALU.subtract).then_inc(oT_ready, 1)

            def norm_turn(l, _):
                dve.wait_ge(zT_hi_ready, l + 1)
                nc.vector.tensor_tensor(in_lo[:, 0:CB, :], zT, in_hi[:, 0:CB, :].bitcast(F32),
                                        ALU.subtract).then_inc(zT_lo_ready, 1)

            def conv_turn(l, _):
                for t in range(TB):
                    bank = ps[:, bank_of[("convT", l, t)], :]
                    dve.wait_ge(convT_done, 2 * l + t + 1)
                    link(nc.vector.bn_stats(bn[:, t, 0, :], bank))
                    nc.vector.bn_aggr(mv[:, t, :], bn[:, t, 0, :]).then_inc(cvar_ready, 1)
                dve.wait_ge(convT_done, 2 * (l + 1))
                for t in range(TB):
                    dve.wait_ge(csd_ready, 2 * l + t + 1)
                    link(nc.vector.reciprocal(rs[:, t:t + 1], sd[:, t:t + 1]))
                    nc.vector.tensor_scalar(zn[:, t, :], ps[:, bank_of[("convT", l, t)], :], mv[:, t, 0:1], rs[:, t:t + 1],
                                            ALU.subtract, ALU.mult).then_inc(zn_ready, 1)

            def attn_out(l, i):
                weights_done(("attn_out", l, i))
                if i == 0:
                    dve.wait_ge(gate_ready, 8 * (l + 1))
                for h in range(2):
                    kb = KB + 4 * i + 2 * h
                    v = gT[:, kb:kb + 2, :].rearrange("p a b -> p (a b)")
                    nc.vector.tensor_tensor(v, ps[:, bank_of[("attn_out", l, i, h)], :], v, ALU.mult)\
                        .then_inc(gated_attn, 1)

            def conv_out(l, _):
                weights_done(("conv_out", l, 0))
                for j in range(4):
                    v = gT[:, 2 * j:2 * j + 2, :].rearrange("p a b -> p (a b)")
                    nc.vector.tensor_tensor(v, ps[:, bank_of[("conv_out", l, j)], :], v, ALU.mult)\
                        .then_inc(gated_conv, 1)
                dve.wait_ge(gated_attn, 4 * (l + 1))
                for j in range(4):
                    dve.wait_ge(gated_conv, 4 * l + j + 1)
                    v = gT[:, 2 * j:2 * j + 2, :]
                    nc.vector.tensor_tensor(v, v, gT[:, KB + 2 * j:KB + 2 * j + 2, :], ALU.add).then_inc(merged, 1)
                for j in range(4):
                    dve.wait_ge(mg_hi_ready, 4 * l + j + 1)
                    v = slice(2 * j, 2 * j + 2)
                    nc.vector.tensor_tensor(mid_lo[:, v, :], gT[:, v, :], mid_hi[:, v, :].bitcast(F32),
                                            ALU.subtract).then_inc(mg_lo_ready, 1)

            def add_y(s, h):
                if h == 0:
                    dve.wait_ge(gains_ready, 2 * (s + 1))
                    if s:
                        dve.wait_ge(x_ready, 2 * s)
                c0 = slice(512 * h, 512 * h + 512)
                for t in range(TB):
                    y = y_sum[:, t, c0] if s == 3 else ps[:, bank_of[("y", s, t, h)], :]
                    nc.vector.tensor_tensor(xn[:, t, c0], y, gains[:, c0], ALU.mult).then_inc(y_gained, 1)
                for t in range(TB):
                    dve.wait_ge(y_gained, 4 * s + 2 * h + t + 1)
                    nc.vector.scalar_tensor_tensor(out=x_tok[:, t, c0], in0=x_tok[:, t, c0], scalar=ALPHA,
                                                   in1=xn[:, t, c0], op0=ALU.mult, op1=ALU.add).then_inc(summed, 1)
                for t in range(TB):
                    dve.wait_ge(summed, 4 * s + 2 * h + t + 1)
                    ins = nc.vector.bn_stats(bn[:, t, h, :], x_tok[:, t, c0])
                    ins.then_inc(stats, 1)

            def normalise_x(s):
                for t in range(TB):
                    dve.wait_ge(stats, 4 * s + 3 + t)
                    nc.vector.bn_aggr(mv[:, t, :], bn[:, t, :, :].rearrange("p a b -> p (a b)")).then_inc(var_ready, 1)
                dve.wait_ge(var_ready, 2 * (s + 1))
                for t in range(TB):
                    dve.wait_ge(sd_ready, 2 * s + t + 1)
                    link(nc.vector.reciprocal(rs[:, t:t + 1], sd[:, t:t + 1]))
                    nc.vector.tensor_scalar(xn[:, t, :], x_tok[:, t, :], mv[:, t, 0:1], rs[:, t:t + 1],
                                            ALU.subtract, ALU.mult).then_inc(xn_ready, 1)

            def out_proj(l, i):
                weights_done(("w_o", l, i))
                add_y(2 * l, i)
                if i == 1:
                    normalise_x(2 * l)

            def ffn_up(l, f):
                weights_done(("ffn_up", 0, f))
                dve.wait_ge(silu_ready, f + 1)
                if f >= 2:
                    dve.wait_ge(hid_lo_ready, f - 1)
                nc.vector.tensor_tensor(hid_d[:, f % 2, :], ps[:, bank_of[("ffn_up", f, 1)], :], gated_d[:, f % 2, :],
                                        ALU.mult).then_inc(hid_ready, 1)
                dve.wait_ge(hid_hi_ready, f + 1)
                v = slice(2 * (f % 2), 2 * (f % 2) + 2)
                nc.vector.tensor_tensor(mid_lo[:, v, :].rearrange("p a b -> p (a b)"), hid_d[:, f % 2, :],
                                        mid_hi[:, v, :].bitcast(F32).rearrange("p a b -> p (a b)"),
                                        ALU.subtract).then_inc(hid_lo_ready, 1)

            def ffn_down(l, f):
                if f == NFT - 1:
                    weights_done(("ffn_down", 0, NFT - 1))
                    add_y(1, 0)
                    add_y(1, 1)
                    normalise_x(1)

            def router(l, _):
                r = lambda n: route[:, n, :].rearrange("p (t e) -> p t e", t=TB)
                pair = lambda n: route[:, n, 0:2]
                wide = lambda n: route[:, n, 0:2].unsqueeze(2).to_broadcast([P, TB, E])
                dve.wait_ge(router_in, 16)
                link(nc.vector.tensor_copy(router_hi[:, :, :], w_router[:, :, :]))
                link(nc.vector.tensor_tensor(router_lo[:, :, :], w_router[:, :, :], router_hi[:, :, :].bitcast(F32),
                                             ALU.subtract))
                nc.vector.memset(st_max[:, :], 0.0).then_inc(router_split, 2)
                dve.wait_ge(router_done, 1)
                dve.wait_ge(consts, 5)
                lg, rev = ps[:, bank_of[("router", 0)], 0:TB * E].rearrange("p (t e) -> p t e", t=TB), e_rev
                link(nc.vector.tensor_copy(r(1), lg))
                src = 1
                for n, (best, onehot, key, keymax) in enumerate(((2, 3, 4, 5), (6, 7, 4, 5))):
                    link(nc.vector.tensor_reduce(pair(best), r(src), AX.X, ALU.max))
                    link(nc.vector.tensor_tensor(r(key), r(src), wide(best), ALU.is_equal))
                    link(nc.vector.tensor_tensor(r(key), r(key), rev, ALU.mult))
                    link(nc.vector.tensor_reduce(pair(keymax), r(key), AX.X, ALU.max))
                    link(nc.vector.tensor_tensor(r(onehot), rev, wide(keymax), ALU.is_equal))
                    if n == 0:
                        link(nc.vector.scalar_tensor_tensor(out=route[:, 8, :], in0=route[:, 3, :], scalar=-3e38,
                                                            in1=route[:, 1, :], op0=ALU.mult, op1=ALU.add))
                        src = 8
                nc.vector.tensor_tensor(route[:, 0, :], route[:, 3, :], route[:, 7, :], ALU.add).then_inc(mask_ready, 1)
                nc.vector.tensor_tensor(pair(9), pair(6), pair(2), ALU.subtract).then_inc(gap_ready, 1)
                dve.wait_ge(gap_exp, 1)
                link(nc.vector.tensor_scalar(pair(10), pair(11), 1.0, None, ALU.add))
                link(nc.vector.reciprocal(pair(12), pair(10)))
                link(nc.vector.tensor_tensor(pair(13), pair(12), pair(11), ALU.mult))
                link(nc.vector.tensor_tensor(r(3), r(3), wide(12), ALU.mult))
                link(nc.vector.tensor_tensor(r(7), r(7), wide(13), ALU.mult))
                link(nc.vector.tensor_tensor(r(14), r(3), r(7), ALU.add))

            def ranks(l, _):
                r = lambda n: route[:, n, :].rearrange("p (t e) -> p t e", t=TB)
                bank = ps[:, bank_of[("ranks", 0)], :]
                dve.wait_ge(ranks_done, 1)
                dve.wait_ge(mask_ready, 1)
                link(nc.vector.tensor_scalar(route[:, 1, :], bank[:, 0:TB * E], 1.0, None, ALU.add))
                link(nc.vector.tensor_tensor(route[:, 1, :], route[:, 1, :], route[:, 0, :], ALU.mult))
                link(nc.vector.tensor_scalar(route[:, 1, :], route[:, 1, :], -1.0, None, ALU.add))
                big, ahead = route[:, 2, 0:E], route[:, 2, E:2 * E]
                link(nc.vector.tensor_scalar(big, bank[:, 2 * E:3 * E], float(P), None, ALU.is_gt))
                link(nc.vector.memset(ahead[:, 0:1], 0.0))
                for e in range(1, E):
                    link(nc.vector.tensor_tensor(ahead[:, e:e + 1], ahead[:, e - 1:e], big[:, e - 1:e], ALU.add))
                link(nc.vector.tensor_tensor(items_f[:, 0:1], ahead[:, E - 1:E], big[:, E - 1:E], ALU.add))
                link(nc.vector.tensor_scalar(items_f[:, 0:1], items_f[:, 0:1], float(E), None, ALU.add))
                link(nc.vector.memset(item_pos[:, :, MAX_ITEMS:], -1.0))
                link(nc.vector.tensor_copy(item_pos[:, :, 0:E], r(1)))
                link(nc.vector.tensor_copy(item_gate[:, :, 0:E], r(14)))
                for m in range(MAX_ITEMS - E):
                    pick = route[:, 3, 0:E]
                    link(nc.vector.tensor_scalar(pick, ahead, float(m), None, ALU.is_equal))
                    link(nc.vector.tensor_tensor(pick, pick, big, ALU.mult))
                    link(nc.vector.tensor_tensor(route[:, 4, 0:E], pick, e_idx, ALU.mult))
                    link(nc.vector.tensor_reduce(items_f[:, 1 + m:2 + m], route[:, 4, 0:E], AX.X, ALU.add))
                    for t in range(TB):
                        link(nc.vector.tensor_tensor(route[:, 4, 0:E], pick, route[:, 1, E * t:E * t + E], ALU.mult))
                        link(nc.vector.tensor_reduce(route[:, 5, 0:1], route[:, 4, 0:E], AX.X, ALU.add))
                        link(nc.vector.tensor_scalar(item_pos[:, t, E + m:E + m + 1], route[:, 5, 0:1], -float(P),
                                                     None, ALU.add))
                        link(nc.vector.tensor_tensor(route[:, 4, 0:E], pick, route[:, 14, E * t:E * t + E], ALU.mult))
                        link(nc.vector.tensor_reduce(item_gate[:, t, E + m:E + m + 1], route[:, 4, 0:E], AX.X, ALU.add))
                nc.vector.tensor_copy(items_i[:, :], items_f[:, :]).then_inc(items_ready, 1)
                nc.vector.memset(y_sum, 0.0).then_inc(y_added, 1)

            do = {"turn": turn_stream, "u": u, "scores": scores, "probsT": normalise, "pv": pv,
                  "convT": conv_turn, "normT": norm_turn, "attn_out": attn_out, "conv_out": conv_out,
                  "w_o": out_proj, "ffn_up": ffn_up, "ffn_down": ffn_down, "router": router, "ranks": ranks}
            tap = [0]
            for kind, l, i in steps:
                if kind == "turn" and l == 0:
                    for k in range(AHEAD):
                        low(k)
                mine = [k for g, k in split_no.items() if g[:3] == (kind, l, i)]

                def ahead(k):
                    low(k + AHEAD)
                    if kind in ("q", "kv", "gate", "attn_out") and (kind, i) != ("attn_out", 1):
                        n = min(tap[0] + TAPS_STEP, CB * TAPS)
                        taps(l, tap[0], n)
                        tap[0] = n
                for k in mine[:-1]:
                    ahead(k)
                if kind in do:
                    do[kind](l, i)
                for k in mine[-1:]:
                    ahead(k)
                if kind == "w_o":
                    assert tap[0] in (0, CB * TAPS)
                    tap[0] = 0

            def place(col):
                for t in range(TB):
                    nc.vector.tensor_scalar(put[:, t, :], slot_no, item_pos[:, t, bass.ds(col, 1)] if not isinstance(col, int)
                                            else item_pos[:, t, col:col + 1], None, ALU.is_equal).then_inc(put_ready, 1)

            def gathered():
                for j in range(4, 8):
                    nc.vector.tensor_scalar(hTi[:, j, :], ps[:, 6, P * (j - 4):P * (j - 4) + P],
                                            scale_c[:, 3, j:j + 1], shift_c[:, 3, j:j + 1],
                                            ALU.mult, ALU.add).then_inc(hTi_ready, 1)

            def gathered_low():
                nc.vector.tensor_tensor(hTi_lo, hTi, hTi_hi.bitcast(F32), ALU.subtract).then_inc(hTi_lo_ready, 1)

            place(0)
            dve.wait_ge(gather_done, 1)
            gathered()
            dve.wait_ge(hTi_hi_ready, 1)
            gathered_low()
            n_items = dve.value_load(items_i[0:1, 0:1], min_val=E, max_val=MAX_ITEMS)
            with dve.Fori(0, n_items) as it:
                def item_low(j):
                    slot = (R0 + j) % SLOTS
                    n = (K0 + j) % AHEAD
                    dve.wait_ge(hi_ready, it * ITEM_GRAINS + (K0 + j + 1))
                    nc.vector.tensor_tensor(w_lo[:, n, :], ring[:, slot, :], w_hi[:, n, :].bitcast(F32),
                                            ALU.subtract).then_inc(lo_ready, 1)

                dve.wait_ge(gather_done, it + 1)
                place(it + 1)
                dve.wait_ge(putT_done, it + 1)
                for t in range(TB):
                    nc.vector.tensor_scalar(put_g[:, t, :], slot_no, item_pos[:, t, bass.ds(it, 1)],
                                            item_gate[:, t, bass.ds(it, 1)], ALU.is_equal, ALU.mult)\
                        .then_inc(put_g_ready, 1)
                for f in range(NET):
                    for g in range(3):
                        item_low(up_at(f) + g + AHEAD)
                    dve.wait_ge(wts_used, it * ITEM_GRAINS + (K0 + up_at(f) + 4))
                    dve.wait_ge(silu_ready, it * NET + (NFT + f + 1))
                    if f:
                        dve.wait_ge(hidT_done, it * NET + f)
                    nc.vector.tensor_tensor(hid, ps[:, 1, :], gated, ALU.mult).then_inc(hid_ready, 1)
                    item_low(up_at(f) + 3 + AHEAD)
                    if f:
                        for g in range(2):
                            item_low(down_at(f - 1) + g + AHEAD)
                    dve.wait_ge(hid_hi_ready, it * NET + (NFT + f + 1))
                    nc.vector.tensor_tensor(hidT_lo, ps[:, 2, :], hidT_hi.bitcast(F32), ALU.subtract)\
                        .then_inc(hid_lo_ready, 1)
                dve.wait_ge(gather_done, it + 2)
                gathered()
                dve.wait_ge(hTi_hi_ready, it + 2)
                gathered_low()
                item_low(down_at(NET - 1) + AHEAD)
                item_low(down_at(NET - 1) + 1 + AHEAD)
                for n, (h, t) in enumerate(((0, 0), (0, 1), (1, 0), (1, 1))):
                    dve.wait_ge(scatter_done, it * 4 + (n + 2))
                    if n == 0:
                        dve.wait_ge(y_added, it * 4 + 1)
                    y = y_sum[:, t, 512 * h:512 * h + 512]
                    nc.vector.tensor_tensor(y, ps[:, (7, 5, 6, 7)[n], :], y, ALU.add).then_inc(y_added, 1)
            link(nc.vector.memset(st_max[:, :], 0.0))
            add_y(3, 0)
            add_y(3, 1)
            normalise_x(3)
            dve.wait_ge(fin_in, 32)
            dve.wait_ge(xn_ready, 8)
            for t in range(TB):
                link(nc.vector.tensor_tensor(xn[:, t, :], xn[:, t, :], fin_g, ALU.mult))
                nc.vector.tensor_tensor(xn[:, t, :], xn[:, t, :], fin_b, ALU.add).then_inc(out_ready, 1)

        @block.gpsimd
        def _(pool):
            count = [0]

            def link(ins):
                count[0] += 1
                ins.then_inc(pool_chain, 1)
                pool.wait_ge(pool_chain, count[0])

            link(nc.gpsimd.memset(ident[:, :], 0.0))
            nc.gpsimd.affine_select(out=ident[:, :], in_=ident[:, :], compare_op=ALU.not_equal, fill=1.0, base=0,
                                    pattern=[[-1, P]], channel_multiplier=1).then_inc(consts, 1)
            nc.gpsimd.memset(ones[:, :], 1.0).then_inc(consts, 1)
            nc.gpsimd.iota(iota_i.rearrange("p (a b) -> p a b", a=TB), pattern=[[P, TB], [-1, S]], base=0,
                           channel_multiplier=1).then_inc(consts, 1)
            nc.gpsimd.memset(epsc[:, :], EPS)
            link(nc.gpsimd.memset(pick4[:, :], 0.0))
            for j in range(4):
                link(nc.gpsimd.memset(pick4[32 * j:32 * j + 1, :], 1.0))
            link(nc.gpsimd.memset(before[:, :], 1.0))
            link(nc.gpsimd.affine_select(out=before[:, :], in_=before[:, :], compare_op=ALU.is_gt, fill=0.0, base=0,
                                         pattern=[[1, P]], channel_multiplier=-1))
            nc.gpsimd.memset(st_den[:, :], 0.0).then_inc(consts, 1)

            def bias_c(l, i):
                return cols[:, C_BADA + 48 * l + i * KB:C_BADA + 48 * l + (i + 1) * KB]

            def scales(s):
                l, base = s // 2, 3 * (s % 2)
                pool.wait_ge(cols_ready, 4)
                pool.wait_ge(mod_raw_ready, 12 * l + (4 if s % 2 == 0 else 10))
                raw = lambda i: mod_raw[:, l, i * KB:(i + 1) * KB]
                link(nc.gpsimd.tensor_tensor(tiny[:, 0, :], raw(base + 1), bias_c(l, base + 1), ALU.add))
                if s == 0:
                    link(nc.gpsimd.tensor_scalar(scale_c[:, 0, :], tiny[:, 0, :], 1.0, None, ALU.add))
                    nc.gpsimd.tensor_tensor(shift_c[:, 0, :], raw(0), bias_c(l, 0), ALU.add).then_inc(scales_ready, 1)
                    return
                gam = cols[:, C_LNG + KB * (s - 1):C_LNG + KB * s]
                bet = cols[:, C_LNB + KB * (s - 1):C_LNB + KB * s]
                link(nc.gpsimd.tensor_scalar(tiny[:, 0, :], tiny[:, 0, :], 1.0, None, ALU.add))
                link(nc.gpsimd.tensor_tensor(scale_c[:, s, :], tiny[:, 0, :], gam, ALU.mult))
                link(nc.gpsimd.tensor_tensor(tiny[:, 1, :], raw(base), bias_c(l, base), ALU.add))
                link(nc.gpsimd.tensor_tensor(tiny[:, 2, :], tiny[:, 0, :], bet, ALU.mult))
                nc.gpsimd.tensor_tensor(shift_c[:, s, :], tiny[:, 1, :], tiny[:, 2, :], ALU.add).then_inc(scales_ready, 1)

            def diagonal(s):
                l, i = s // 2, 2 + 3 * (s % 2)
                pool.wait_ge(mod_raw_ready, 12 * l + (6 if s % 2 == 0 else 12))
                if s % 2 == 0:
                    pool.wait_ge(probsT_done, 16 * (l + 1))
                link(nc.gpsimd.tensor_tensor(tiny[:, 3, :], mod_raw[:, l, i * KB:(i + 1) * KB], bias_c(l, i), ALU.add))
                for kb in range(KB):
                    ins = nc.gpsimd.tensor_scalar(lnbuf[:, P * kb:P * kb + P], ident[:, :], tiny[:, 3, kb:kb + 1],
                                                  None, ALU.mult)
                    if kb == KB - 1:
                        ins.then_inc(diag_ready, 1)

            def update(s):
                for n, par in enumerate((post_ln_g, post_ln_b)):
                    if n == 0:
                        pool.wait_ge(gains_done, s + 1)
                    pool.dma_start(lnbuf[:, :], par[s // 2, s % 2].partition_broadcast(P)).then_inc(ln_in, 16)
                    pool.wait_ge(ln_in, 16 * (2 * s + n + 1))
                    if n == 0:
                        pool.wait_ge(xn_ready, 2 * (s + 1))
                    for t in range(TB):
                        ins = nc.gpsimd.tensor_tensor(x_tok[:, t, :], xn[:, t, :] if n == 0 else x_tok[:, t, :],
                                                      lnbuf[:, :], ALU.mult if n == 0 else ALU.add)
                        if n == 0:
                            link(ins)
                        else:
                            ins.then_inc(x_ready, 1)

            def expert_constants():
                pool.wait_ge(xn_ready, 6)
                link(nc.gpsimd.iota(slot_no, pattern=[[1, P]], base=0, channel_multiplier=0,
                                    allow_small_or_imprecise_dtypes=True))
                link(nc.gpsimd.iota(e_rev, pattern=[[0, TB], [-1, E]], base=E, channel_multiplier=0,
                                    allow_small_or_imprecise_dtypes=True))
                nc.gpsimd.iota(e_idx, pattern=[[1, E]], base=0, channel_multiplier=0,
                               allow_small_or_imprecise_dtypes=True).then_inc(consts, 1)
                pool.dma_start(fin_g, post_ln_g[1, 1].partition_broadcast(P)).then_inc(fin_in, 16)
                pool.dma_start(fin_b, post_ln_b[1, 1].partition_broadcast(P)).then_inc(fin_in, 16)

            scales(0)
            for s in range(4):
                diagonal(s)
                if s < 3:
                    scales(s + 1)
                    if s == 2:
                        expert_constants()
                    update(s)
                    pool.wait_ge(x_ready, 2 * (s + 1))
        @block.sync
        def _(sp):
            sp.dma_start(rows[0:96, 0, :], b_ada.rearrange("l (r p) -> (l r) p", p=P)).then_inc(rows_in, 16)
            sp.dma_start(rows[96:128, 0, :], post_ln_g.rearrange("l s (r p) -> (l s r) p", p=P)).then_inc(rows_in, 16)
            sp.dma_start(rows[0:32, 1, :], post_ln_b.rearrange("l s (r p) -> (l s r) p", p=P)).then_inc(rows_in, 16)
            sp.dma_start(rows[32:40, 1, :], c.rearrange("a (r p) -> (a r) p", p=P)).then_inc(rows_in, 16)
            sp.dma_start(rows[40:48, 1, :], conv_ln_g.rearrange("l (r p) -> (l r) p", p=P)).then_inc(rows_in, 16)
            sp.dma_start(rows[48:56, 1, :], conv_ln_b.rearrange("l (r p) -> (l r) p", p=P)).then_inc(rows_in, 16)
            sp.dma_start(rows[56:64, 1, :], conv_dw_b.rearrange("l (r p) -> (l r) p", p=P)).then_inc(rows_in, 16)
            for l in range(DEPTH):
                for h in range(2):
                    r = conv_dw_w[l].rearrange("j (r p) -> (j r) p", p=P)[62 * h:62 * h + 62, :]
                    sp.dma_start(rows[62 * h:62 * h + 62, 2 + l, :], r).then_inc(rows_in, 16)

            for n, g in enumerate(load):
                if n >= SLOTS:
                    old = load[n - SLOTS]
                    if old[0] == "ada":
                        sp.wait_ge(ada_used, ada_no[old] + 1)
                    else:
                        sp.wait_ge(lo_ready, split_no[old] + 1)
                if n == 6:
                    sp.dma_start(x_tok[:, :, :], x[0].rearrange("(t p) d -> p t d", p=P)).then_inc(x_in, 16)
                sp.dma_start(cut_in(ring[:, n % SLOTS, :], rows_of(g[0])), source(g)).then_inc(slot_in[n % SLOTS], 16)

            order = [None] * ITEM_GRAINS
            for f in range(NET):
                for g in range(2):
                    order[up_at(f) + g] = (moe1, f, g)
                    order[up_at(f) + 2 + g] = (moe3, f, g)
                    order[down_at(f) + g] = (moe2, f, g)

            def fetch(it, e, j):
                w, f, g = order[j % ITEM_GRAINS]
                sp.wait_ge(lo_ready, it * ITEM_GRAINS + (K0 + j - SLOTS + 1))
                if w is moe2:
                    src = w[bass.ds(e, 1), :, 4 * f + 2 * g:4 * f + 2 * g + 2, :]
                else:
                    src = w[bass.ds(e, 1), :, 4 * g:4 * g + 4, ET * f:ET * f + ET]
                slot = (R0 + j) % SLOTS
                sp.dma_start(cut_in(ring[:, slot, :], 2 if w is moe2 else 4),
                             src.rearrange("a p k n -> (a p) k n")).then_inc(slot_in[slot], 16)

            with sp.Fori(0, E) as it:
                for j in range(ITEM_GRAINS):
                    fetch(it, it, j)
            sp.wait_ge(items_ready, 1)
            n_items = sp.value_load(items_i[0:1, 0:1], min_val=E, max_val=MAX_ITEMS)
            with sp.If(n_items > E):
                with sp.Fori(E, n_items) as it:
                    e = sp.value_load(items_i[0:1, bass.ds(it - (E - 1), 1)], min_val=0, max_val=E - 1)
                    for j in range(ITEM_GRAINS):
                        fetch(it, e, j)
            for j in range(AHEAD):
                fetch(n_items, 0, j)
            for t in range(TB):
                sp.wait_ge(out_ready, t + 1)
                sp.dma_start(out[0, P * t:P * t + P, :], xn[:, t, :]).then_inc(out_done, 16)
            sp.wait_ge(out_done, 16 * TB)


_INS = ['x', 'c', 'w_ada', 'b_ada', 'w_in', 'conv_dw_w', 'conv_dw_b', 'conv_ln_g', 'conv_ln_b', 'w_conv_out',
        'w_attn_out', 'attn_sinks', 'w_o', 'post_ln_g', 'post_ln_b', 'ffn_w1', 'ffn_w3', 'ffn_w2', 'moe_router',
        'moe_w1', 'moe_w3', 'moe_w2']
_OUTS = [((1, 256, 1024), 'float32')]


def kernel(**inputs):
    import numpy as _np
    import concourse.bacc as _bacc
    from concourse import mybir as _mybir
    from concourse.bass_utils import run_bass_kernel_spmd as _run

    nc = _bacc.Bacc("TRN2", target_bir_lowering=False, num_devices=1, dynamic_dma_scratch_size=4096)
    arrays, args = {}, []
    for name in _INS:
        a = _np.ascontiguousarray(inputs[name])
        arrays[f"in_{name}_dram"] = a
        args.append(nc.dram_tensor(f"in_{name}_dram", a.shape, _mybir.dt.from_np(a.dtype), kind="ExternalInput").ap())
    for i, (shape, dtype) in enumerate(_OUTS):
        dt = _mybir.dt.from_np(_np.dtype(dtype))
        args.append(nc.dram_tensor(f"out_{i}_dram", shape, dt, kind="ExternalOutput").ap())
    trunk(nc, *args)
    r = _run(nc, [arrays], core_ids=[0])
    got = tuple(r.results[0][f"out_{i}_dram"] for i in range(len(_OUTS)))
    return got[0]
```

```python
from contextlib import ExitStack

import concourse.bass as bass
from concourse import mybir

F32 = mybir.dt.float32
F32R = mybir.dt.float32r
I32 = mybir.dt.int32
ALU = mybir.AluOpType
ACT = mybir.ActivationFunctionType
AX = mybir.AxisListType

P = 128
D = 1024
KB = D // P
S = 256
TB = S // P
DEPTH = 2
HEADS, KV_HEADS, HD = 16, 4, 64
GRP = HEADS // KV_HEADS
CHUNK = 64
CONV = 512
CB = CONV // P
TAPS = 31
PAD = TAPS - 1
DFF = 2816
FT = 256
NFT = DFF // FT
E = 8
DFFE = 3584
ET = 512
NET = DFFE // ET
ALPHA = (2.0 * DEPTH) ** 0.25
EPS = 1e-5
FAR = -1e38
SLOTS = 7
GRAIN = 2048
AHEAD = 3
ITEM_GRAINS = 6 * NET
TAPS_STEP = 10
MAX_ITEMS = E + 3

C_BADA, C_LNG, C_LNB, C_C, C_CG, C_CB, C_DWB, C_DW = 0, 96, 128, 160, 168, 176, 184, 256


def mixing_steps(l):
    ada = [(0, i) for i in range(4, 10)] if l == 0 else [(1, 6), (1, 7)]
    main = [("u", l, 0), ("u", l, 1), ("kv", l, 0), ("q", l, 0), ("scores", l, 0), ("q", l, 1),
            ("scores", l, 1), ("probsT", l, 0), ("gate", l, 0), ("pv", l, 0),
            ("scores", l, 2), ("probsT", l, 1), ("gate", l, 1), ("pv", l, 1),
            ("scores", l, 3), ("probsT", l, 2), ("gate", l, 2), ("pv", l, 2),
            ("probsT", l, 3), ("gate", l, 3), ("pv", l, 3), ("convT", l, 0), ("attn_out", l, 0),
            ("normT", l, 0), ("attn_out", l, 1), ("gains", 2 * l, 0), ("conv_out", l, 0),
            ("w_o", l, 0), ("w_o", l, 1)]
    out = []
    for n, step in enumerate(main):
        fill = ada and step[0] in ("u", "kv", "q", "gate") and n >= 2
        if fill:
            al, ai = ada.pop(0)
            out += [("ada", al, ai), step, ("ada_cols", al, ai)]
        else:
            out.append(step)
    assert not ada
    return out


def all_steps():
    steps = []
    for i in range(4):
        steps += [("ada", 0, i), ("ada_cols", 0, i)]
    steps += [("turn", 0, 0)] + mixing_steps(0)
    steps += [("ada", 0, 10), ("ada", 0, 11), ("ada_cols", 0, 10), ("turn", 1, 0), ("ada_cols", 0, 11)]
    steps += [("ffn_up", 0, 0), ("ffn_up", 0, 1), ("ffn_down", 0, 0)]
    for f in range(2, NFT):
        if f < 6:
            steps += [("ada", 1, f - 2), ("ffn_up", 0, f), ("ada_cols", 1, f - 2), ("ffn_down", 0, f - 1)]
        else:
            steps += [("ffn_up", 0, f), ("ffn_down", 0, f - 1)]
    steps += [("gains", 1, 0), ("ffn_down", 0, NFT - 1)]
    steps += [("ada", 1, 4), ("ada", 1, 5), ("ada_cols", 1, 4), ("turn", 2, 0), ("ada_cols", 1, 5)]
    steps += mixing_steps(1)
    steps += [("ada", 1, 8), ("ada", 1, 9), ("ada_cols", 1, 8), ("ada_cols", 1, 9), ("turn", 3, 0),
              ("router", 1, 0), ("ada", 1, 10), ("ranks", 1, 0), ("ada", 1, 11), ("ada_cols", 1, 10),
              ("ada_cols", 1, 11)]
    return steps


NORMALISE_IN = {("q", 1): 0, ("gate", 0): 1, ("gate", 1): 2, ("gate", 2): 3}
HOLD = {("w_o", 0, 1): "turn", ("ffn_down", 0, NFT - 1): "turn"}
HOLD_VECTOR = {**HOLD, **{(kind, l, i): "scores" for l in range(DEPTH) for kind in ("q", "gate") for i in range(2)}}
SPLIT_STEPS = ("u", "q", "kv", "gate", "conv_out", "attn_out", "w_o", "ffn_up", "ffn_down")


def granules(steps):
    load = []
    for kind, l, i in steps:
        if kind == "ada" or kind in SPLIT_STEPS:
            load += [(kind, l, i, g) for g in range(1 if kind == "ffn_down" else 2)]
    return load


def up_at(f):
    return 0 if f == 0 else 6 * f - 2


def down_at(f):
    return 6 * f + 8 if f < NET - 1 else ITEM_GRAINS - 2


def trunk(nc, x, c, w_ada, b_ada, w_in, conv_dw_w, conv_dw_b, conv_ln_g, conv_ln_b, w_conv_out,
          w_attn_out, attn_sinks, w_o, post_ln_g, post_ln_b, ffn_w1, ffn_w3, ffn_w2, moe_router,
          moe_w1, moe_w3, moe_w2, out):
    steps = all_steps()
    load = granules(steps)
    ring_no = {g: n for n, g in enumerate(load)}
    split_no = {g: n for n, g in enumerate(g for g in load if g[0] != "ada")}
    ada_no = {g: n for n, g in enumerate(g for g in load if g[0] == "ada")}
    R0, K0 = len(load), len(split_no)

    def landed(n):
        return n % SLOTS, 16 * (n // SLOTS + 1)

    with ExitStack() as ctx:
        def sb(name, shape, dt=F32):
            return ctx.enter_context(nc.sbuf_tensor(name, shape, dt))

        def sem(name):
            return ctx.enter_context(nc.semaphore(name))

        ring = sb("ring", [P, SLOTS, GRAIN])
        w_hi = sb("w_hi", [P, AHEAD, GRAIN], F32R)
        w_lo = sb("w_lo", [P, AHEAD, GRAIN], F32R)
        in_hi = sb("in_hi", [P, KB, S], F32R)
        in_lo = sb("in_lo", [P, KB, S], F32R)
        mid_hi = sb("mid_hi", [P, KB, S], F32R)
        mid_lo = sb("mid_lo", [P, KB, S], F32R)
        x_tok = sb("x_tok", [P, TB, D])
        xn = sb("xn", [P, TB, D])
        arena = sb("arena", [P, 13432])
        cols = sb("cols", [P, 512])
        mod_raw = sb("mod_raw", [P, DEPTH, 48])
        scale_c = sb("scale_c", [P, 4, KB])
        shift_c = sb("shift_c", [P, 4, KB])
        tiny = sb("tiny", [P, 4, KB])
        mod_part = sb("mod_part", [P, 512])
        neg_dist = sb("neg_dist", [P, TB, S])
        ident = sb("ident", [P, P])
        ones = sb("ones", [P, P])
        before = sb("before", [P, P])
        pick4 = sb("pick4", [P, 1])
        c_wide = sb("c_wide", [P, KB, 32])
        c_act = sb("c_act", [P, KB])
        sinks = sb("sinks", [P, DEPTH * HEADS])
        w_router = sb("w_router", [P, KB, E])
        extra_no = sb("extra_no", [P, MAX_ITEMS - E, E])
        extra_of = sb("extra_of", [P, MAX_ITEMS - E, E])
        extra = sb("extra", [P, TB, MAX_ITEMS - E, E])
        prefix = sb("prefix", [P, 3, 2 * E])
        epsc = sb("epsc", [P, 1])
        st_max, st_neg, st_dsink, st_den, st_esink, st_rden = (
            sb(f"st_{name}", [P, 2, 8]) for name in ("max", "neg", "dsink", "den", "esink", "rden"))
        bn = sb("bn", [P, 2, 2, 6])
        mv = sb("mv", [P, 2, 2])
        sd = sb("sd", [P, 2])
        rs = sb("rs", [P, 2])
        item_pos = sb("item_pos", [P, TB, MAX_ITEMS + 1])
        item_gate = sb("item_gate", [P, TB, MAX_ITEMS + 1])
        items_f = sb("items_f", [P, 4])
        items_i = sb("items_i", [P, 4], I32)
        ps = ctx.enter_context(nc.psum_tensor("ps", [P, 8, 512], F32))

        at = [0]

        def part(*shape):
            n = 1
            for k in shape:
                n *= k
            v = arena[:, at[0]:at[0] + n]
            at[0] += n
            if len(shape) == 2:
                v = v.rearrange("p (a b) -> p a b", a=shape[0])
            if len(shape) == 3:
                v = v.rearrange("p (a b c) -> p a b c", a=shape[0], b=shape[1])
            return v

        qT = part(KB, S)
        kT = part(KV_HEADS, S)
        v_tok = part(TB, KV_HEADS * HD)
        zp = part(CB, S + PAD)
        conv = part(CB, S)
        gT = part(2 * KB, S)
        probs = part(8, S)
        pT = part(GRP, 3 * P)
        zn = conv.rearrange("p a b -> p (a b)").rearrange("p (a b) -> p a b", a=TB)
        zT = qT[:, 0:CB, :]
        hT = gT[:, 0:KB, :]
        probs_of = (probs, xn.rearrange("p t (a b) -> p (t a) b", b=S))
        gains = probs[:, 0:4, :].rearrange("p a b -> p (a b)")
        lnbuf = probs[:, 4:8, :].rearrange("p a b -> p (a b)")
        assert at[0] == 13432
        at[0] = 0
        gated_d = part(2, 512)
        hid_d = part(2, 512)
        at[0] = 0
        fin_g = part(D)
        fin_b = part(D)
        y_sum = part(TB, D)
        hid = part(ET)
        gated = part(ET)
        put = part(TB, P)
        put_g = part(TB, P)
        at[0] = 5752
        hTi = part(KB, P)
        y_item = part(D)
        put_gT = part(S)
        at[0] = 11896
        slot_no = part(P)
        e_rev = part(TB, E)
        e_idx = part(E)
        route = part(16, 16)
        hTi_hi, hTi_lo = (m[:, 0:4, :].rearrange("p a b -> p (a b)").rearrange("p (k n) -> p k n", k=KB)
                          for m in (mid_hi, mid_lo))
        hidT_hi, hidT_lo = (m[:, 4:6, :].rearrange("p a b -> p (a b)") for m in (mid_hi, mid_lo))
        at[0] = 0
        rows = part(4, P)
        at[0] = 12000
        iota_i = arena[:, 12000:12000 + 512].bitcast(I32)

        slot_in = [sem(f"slot_in{i}") for i in range(SLOTS)]
        rows_in = sem("rows_in")
        x_in = sem("x_in")
        sinks_in = sem("sinks_in")
        router_in = sem("router_in")
        consts = sem("consts")
        cols_t = sem("cols_t")
        cols_ready = sem("cols_ready")
        c_ready = sem("c_ready")
        cw_ready = sem("cw_ready")
        hi_ready = sem("hi_ready")
        lo_ready = sem("lo_ready")
        wts_used = sem("wts_used")
        ada_used = sem("ada_used")
        ada_cols_done = sem("ada_cols_done")
        mod_part_ready = sem("mod_part_ready")
        mod_raw_ready = sem("mod_raw_ready")
        scales_ready = sem("scales_ready")
        turn_done = sem("turn_done")
        hT_act = sem("hT_act")
        hT_dve = sem("hT_dve")
        in_hi_ready = sem("in_hi_ready")
        in_lo_ready = sem("in_lo_ready")
        o_hi_ready = sem("o_hi_ready")
        zT_hi_ready = sem("zT_hi_ready")
        zT_lo_ready = sem("zT_lo_ready")
        mg_hi_ready = sem("mg_hi_ready")
        mg_lo_ready = sem("mg_lo_ready")
        hid_hi_ready = sem("hid_hi_ready")
        hid_lo_ready = sem("hid_lo_ready")
        hidT_done = sem("hidT_done")
        hTi_hi_ready = sem("hTi_hi_ready")
        hTi_lo_ready = sem("hTi_lo_ready")
        sg_ready = sem("sg_ready")
        z_ready = sem("z_ready")
        conv_step = sem("conv_step")
        q_ready = sem("q_ready")
        kv_ready = sem("kv_ready")
        gate_ready = sem("gate_ready")
        scores_done = sem("scores_done")
        biased = sem("biased")
        max_ready = sem("max_ready")
        exp_ready = sem("exp_ready")
        probs_ready = sem("probs_ready")
        probsT_done = sem("probsT_done")
        pT_ready = sem("pT_ready")
        pv_done = sem("pv_done")
        oT_ready = sem("oT_ready")
        convT_done = sem("convT_done")
        cvar_ready = sem("cvar_ready")
        csd_ready = sem("csd_ready")
        zn_ready = sem("zn_ready")
        normT_done = sem("normT_done")
        zT_ready = sem("zT_ready")
        rden_ready = sem("rden_ready")
        conv_bank = sem("conv_bank")
        attn_bank = sem("attn_bank")
        y_part = sem("y_part")
        gated_conv = sem("gated_conv")
        gated_attn = sem("gated_attn")
        merged = sem("merged")
        diag_ready = sem("diag_ready")
        gains_done = sem("gains_done")
        gains_ready = sem("gains_ready")
        y_gained = sem("y_gained")
        summed = sem("summed")
        stats = sem("stats")
        var_ready = sem("var_ready")
        sd_ready = sem("sd_ready")
        xn_ready = sem("xn_ready")
        ln_in = sem("ln_in")
        x_ready = sem("x_ready")
        silu_ready = sem("silu_ready")
        hid_ready = sem("hid_ready")
        gap_ready = sem("gap_ready")
        gap_exp = sem("gap_exp")
        router_done = sem("router_done")
        mask_ready = sem("mask_ready")
        ranks_done = sem("ranks_done")
        items_ready = sem("items_ready")
        put_ready = sem("put_ready")
        put_g_ready = sem("put_g_ready")
        gather_done = sem("gather_done")
        hTi_ready = sem("hTi_ready")
        putT_done = sem("putT_done")
        putT_ready = sem("putT_ready")
        y_item_ready = sem("y_item_ready")
        scatter_done = sem("scatter_done")
        y_added = sem("y_added")
        fin_in = sem("fin_in")
        out_ready = sem("out_ready")
        out_done = sem("out_done")
        dve_chain = sem("dve_chain")
        pool_chain = sem("pool_chain")

        def source(g):
            kind, l, i, h = g
            first = {"q": 0, "kv": 2, "u": 3, "gate": 5}
            if kind == "ffn_up":
                return (ffn_w1, ffn_w3)[h][0].rearrange("(kb p) n -> p kb n", p=P)[:, :, FT * i:FT * i + FT]
            if kind == "ffn_down":
                return ffn_w2[0, FT * i:FT * i + FT].rearrange("(kb p) n -> p kb n", p=P)
            if kind == "conv_out":
                return w_conv_out[l, 256 * h:256 * h + 256].rearrange("(kb p) n -> p kb n", p=P)
            w, j = {"ada": (w_ada, i), "attn_out": (w_attn_out, i), "w_o": (w_o, i)}.get(
                kind, (w_in, first.get(kind, 0) + i))
            return w[l, 512 * h:512 * h + 512].rearrange("(kb p) n -> p kb n", p=P)[:, :, 512 * j:512 * j + 512]

        def rows_of(kind):
            return {"ffn_up": KB, "ffn_down": 2, "conv_out": 2}.get(kind, 4)

        def cut_in(v, k):
            return v.rearrange("p (k n) -> p k n", k=k)

        moe1 = moe_w1.rearrange("a e (kb p) n -> (a e) p kb n", p=P)
        moe3 = moe_w3.rearrange("a e (kb p) n -> (a e) p kb n", p=P)
        moe2 = moe_w2.rearrange("a e (kb p) n -> (a e) p kb n", p=P)

        def used(step):
            kind, l, i = step
            return split_no[(kind, l, i, 0 if kind == "ffn_down" else 1)] + 1

        def merged_at(kb):
            return (kb + CB) % KB

        bank_of = {}
        block = ctx.enter_context(nc.Block())

        @block.tensor
        def _(pe):
            holder = [None] * 8
            turn, size = [0], [8]

            def take(key, freed_by, banks=None):
                if banks is None:
                    b = turn[0] % size[0]
                    turn[0] += 1
                else:
                    b = banks
                if holder[b] is not None:
                    pe.wait_ge(*holder[b])
                holder[b] = freed_by
                bank_of[key] = b
                return b

            def split(g):
                k = split_no[g]
                pe.wait_ge(lo_ready, k + 1)
                n = rows_of(g[0])
                return cut_in(w_hi[:, k % AHEAD, :], n), cut_in(w_lo[:, k % AHEAD, :], n)

            def product(to, stat, stat_at, mov, mov_at, start, stop):
                (sh, sl), (mh, ml) = stat, mov
                nc.tensor.matmul(to, sh[stat_at], mh[mov_at], start=start, stop=False, skip_group_check=True)
                nc.tensor.matmul(to, sh[stat_at], ml[mov_at], start=False, stop=False, skip_group_check=True)
                return nc.tensor.matmul(to, sl[stat_at], mh[mov_at], start=False, stop=stop, skip_group_check=True)

            whole = slice(None)
            layer_in, inner = (in_hi, in_lo), (mid_hi, mid_lo)

            def block(n, k=P):
                return slice(k * n, k * n + k)

            pe.wait_ge(rows_in, 16 * 11)
            pe.wait_ge(consts, 1)
            b = take(("cols", 0), (cols_ready, 4))
            for j, r in enumerate((128, 64, 124, 124)):
                mm = nc.tensor.transpose(ps[:, b, 128 * j:128 * j + r], rows[0:r, j, :], ident[0:r, 0:r])
            mm.then_inc(cols_t, 1)
            pe.wait_ge(cw_ready, 1)
            pe.wait_ge(consts, 4)

            def ada(l, i):
                b = take(("ada", l, i), (mod_part_ready, 12 * l + i + 1))
                for r in range(2):
                    n = ring_no[("ada", l, i, r)]
                    pe.wait_ge(slot_in[landed(n)[0]], landed(n)[1])
                    w = cut_in(ring[:, n % SLOTS, :], 4)
                    for j in range(4):
                        mm = nc.tensor.matmul(ps[32 * j:32 * j + 32, b, :], c_wide[:, 4 * r + j, :], w[:, j, :],
                                              start=(r == 0), stop=(r == 1), tile_position=(0, 32 * j))
                    mm.then_inc(ada_used, 1)

            def ada_cols(l, i):
                n = 12 * l + i
                b = take(("ada_cols", l, i), (mod_raw_ready, n + 1))
                pe.wait_ge(mod_part_ready, n + 1)
                for j in range(4):
                    mm = nc.tensor.matmul(ps[:, b, j:j + 1], mod_part[:, P * j:P * j + P], pick4[:, :],
                                          start=True, stop=True)
                mm.then_inc(ada_cols_done, 1)

            def turn_stream(s, _):
                src = x_tok if s == 0 else xn
                if s == 0:
                    pe.wait_ge(x_in, 16)
                else:
                    pe.wait_ge(xn_ready, 2 * s)
                for j in range(4):
                    b = take(("turn", s, j), (hT_dve if j % 2 else hT_act, 4 * s + 2 * (j // 2) + 2))
                    for kb in (2 * j, 2 * j + 1):
                        for t in range(TB):
                            mm = nc.tensor.transpose(
                                ps[:, b, S * (kb % 2) + P * t:S * (kb % 2) + P * t + P],
                                src[:, t, P * kb:P * kb + P], ident[:, :])
                    mm.then_inc(turn_done, 1)

            def input_ready(l, kind, kb):
                if kind == "u":
                    pe.wait_ge(in_lo_ready, 8 * l + kb // 2 + 1)
                if kind == "attn_out":
                    pe.wait_ge(oT_ready, 4 * l + kb // 2 + 1)

            def project(kind, freed_by, act=layer_in):
                def run(l, i):
                    banks = [take((kind, l, i, h), freed_by(l, i, h)) for h in range(2)]
                    for g in range(2):
                        w = split((kind, l, i, g))
                        for j in range(4):
                            for k in range(4):
                                if j == 0:
                                    input_ready(l, kind, 4 * g + k)
                                mm = product(ps[:, banks[j // 2], block(j % 2, S)], w, (whole, k, block(j)),
                                             act, (whole, 4 * g + k),
                                             start=(g == 0 and k == 0 and j % 2 == 0), stop=(g == 1 and k == 3))
                            if kind == "attn_out" and g == 1 and j == 1:
                                mm.then_inc(attn_bank, 1)
                        mm.then_inc(wts_used, 1)
                return run

            def kv(l, _):
                bk = take(("kv", l, 0), (kv_ready, 5 * l + 4))
                bv = take(("kv", l, 1), (kv_ready, 5 * l + 5))
                for g in range(2):
                    w = split(("kv", l, 0, g))
                    for j in range(2):
                        for k in range(4):
                            first, last = g == 0 and k == 0 and j == 0, g == 1 and k == 3
                            product(ps[:, bk, block(j, S)], w, (whole, k, block(j)), layer_in, (whole, 4 * g + k),
                                    start=first, stop=last)
                            mm = product(ps[:, bv, block(j, S)], layer_in, (whole, 4 * g + k, block(j)),
                                         w, (whole, k, slice(256, 512)), start=first, stop=last)
                    mm.then_inc(wts_used, 1)

            def scores(l, g):
                if g == 0:
                    pe.wait_ge(kv_ready, 5 * (l + 1))
                if g % 2 == 0:
                    pe.wait_ge(q_ready, 4 * l + g + 2)
                for i in range(GRP):
                    h = GRP * g + i
                    half = HD * (h % 2)
                    b = take(("scores", l, g, i), (biased, 16 * l + h + 1))
                    for t in range(TB):
                        mm = nc.tensor.matmul(ps[:, b, S * t:S * t + S],
                                              qT[half:half + HD, h // 2, P * t:P * t + P],
                                              kT[half:half + HD, g, :], start=True, stop=True)
                    mm.then_inc(scores_done, 1)

            def probs_turn(l, g):
                pe.wait_ge(probs_ready, 8 * (4 * l + g + 1))
                for i in range(GRP):
                    b = take(("probsT", l, g, i), (pT_ready, 16 * l + GRP * g + i + 1))
                    for n, (t, kb) in enumerate(((0, 0), (1, 0), (1, 1))):
                        mm = nc.tensor.transpose(ps[:, b, P * n:P * n + P],
                                                 probs_of[g % 2][:, 2 * i + t, P * kb:P * kb + P], ident[:, :])
                    mm.then_inc(probsT_done, 1)

            def pv(l, g):
                pe.wait_ge(pT_ready, 16 * l + GRP * (g + 1))
                b = take(("pv", l, g), (oT_ready, 4 * l + g + 1))
                for i in range(GRP):
                    half, c0 = HD * (i % 2), S * (i // 2)
                    for n, (t, kb) in enumerate(((0, 0), (1, 0), (1, 1))):
                        mm = nc.tensor.matmul(ps[half:half + HD, b, c0 + P * t:c0 + P * t + P],
                                              v_tok[:, kb, HD * g:HD * g + HD], pT[:, i, P * n:P * n + P],
                                              start=(n != 2), stop=(n != 1), tile_position=(0, half))
                mm.then_inc(pv_done, 1)

            def conv_turn(l, _):
                pe.wait_ge(conv_step, CB * TAPS * (l + 1))
                for t in range(TB):
                    b = take(("convT", l, t), (zn_ready, 2 * l + t + 1))
                    for cb in range(CB):
                        mm = nc.tensor.transpose(ps[:, b, P * cb:P * cb + P],
                                                 conv[:, cb, P * t:P * t + P], ident[:, :])
                    mm.then_inc(convT_done, 1)

            def norm_turn(l, _):
                pe.wait_ge(zn_ready, 2 * (l + 1))
                for j in range(2):
                    b = take(("normT", l, j), (zT_ready, 4 * l + 2 * j + 2))
                    for cb in (2 * j, 2 * j + 1):
                        for t in range(TB):
                            mm = nc.tensor.transpose(
                                ps[:, b, S * (cb % 2) + P * t:S * (cb % 2) + P * t + P],
                                zn[:, t, P * cb:P * cb + P], ident[:, :])
                    mm.then_inc(normT_done, 1)

            def conv_out(l, _):
                banks = [take(("conv_out", l, j), (gated_conv, 4 * l + j + 1)) for j in range(4)]
                for g in range(2):
                    pe.wait_ge(zT_lo_ready, 2 * l + g + 1)
                    w = split(("conv_out", l, 0, g))
                    for j in range(8):
                        for k in range(2):
                            mm = product(ps[:, banks[j // 2], block(j % 2, S)], w, (whole, k, block(j)),
                                         layer_in, (whole, 2 * g + k),
                                         start=(g == 0 and k == 0 and j % 2 == 0), stop=(g == 1 and k == 1))
                        if g == 1 and j % 2 and j < 7:
                            mm.then_inc(conv_bank, 1)
                    mm.then_inc(wts_used, 1)

            def attn_out(l, i):
                project("attn_out", lambda l, i, h: (gated_attn, 4 * l + 2 * i + h + 1), inner)(l, i)

            def out_proj(l, i):
                banks = [take(("y", 2 * l, t, i), (y_gained, 8 * l + 2 * i + t + 1)) for t in range(TB)]
                for g in range(2):
                    w = split(("w_o", l, i, g))
                    for t in range(TB):
                        for k in range(4):
                            if i == 0 and t == 0:
                                pe.wait_ge(mg_lo_ready, 4 * l + (4 * g + k) // 2 + 1)
                            mm = product(ps[:, banks[t], :], layer_in, (whole, merged_at(4 * g + k), block(t)),
                                         w, (whole, k), start=(g == 0 and k == 0), stop=(g == 1 and k == 3))
                        if g == 1 and t == 0:
                            mm.then_inc(y_part, 1)
                    mm.then_inc(wts_used, 1)

            def spread_gains(s, _):
                pe.wait_ge(diag_ready, s + 1)
                for h in range(2):
                    b = take(("gains", s, h), (gains_ready, 2 * s + h + 1))
                    mm = nc.tensor.matmul(ps[:, b, :], ones[:, :], lnbuf[:, 512 * h:512 * h + 512],
                                          start=True, stop=True)
                mm.then_inc(gains_done, 1)

            def ffn_up(l, f):
                for h in range(2):
                    b = take(("ffn_up", f, h), (hid_ready, f + 1))
                    w = split(("ffn_up", 0, f, h))
                    for j in range(2):
                        for kb in range(KB):
                            if (f, h, j) == (0, 0, 0):
                                pe.wait_ge(in_lo_ready, 4 + kb // 2 + 1)
                            mm = product(ps[:, b, block(j, S)], w, (whole, kb, block(j)), layer_in, (whole, kb),
                                         start=(kb == 0), stop=(kb == KB - 1))
                    mm.then_inc(wts_used, 1)

            def ffn_down(l, f):
                w = split(("ffn_down", 0, f, 0))
                if f == 0:
                    for h in range(2):
                        for t in range(TB):
                            take(("y", 1, t, h), (y_gained, 4 + 2 * h + t + 1), 4 + 2 * t + h)
                pe.wait_ge(hid_lo_ready, f + 1)
                for h in range(2):
                    for t in range(TB):
                        for j in range(2):
                            mm = product(ps[:, 4 + 2 * t + h, :], inner, (whole, 2 * (f % 2) + j, block(t)),
                                         w, (whole, j, block(h, 512)),
                                         start=(f == 0 and j == 0), stop=(f == NFT - 1 and j == 1))
                        if f == NFT - 1 and (h, t) != (1, 1):
                            mm.then_inc(y_part, 1)
                mm.then_inc(wts_used, 1)

            def router(l, _):
                pe.wait_ge(router_in, 16)
                pe.wait_ge(hT_act, 16)
                pe.wait_ge(hT_dve, 16)
                b = take(("router", 0), (mask_ready, 1))
                for t in range(TB):
                    for kb in range(KB):
                        mm = nc.tensor.matmul(ps[:, b, block(t, E)], hT[:, kb, block(t)], w_router[:, kb, :],
                                              start=(kb == 0), stop=(kb == KB - 1))
                mm.then_inc(router_done, 1)

            def ranks(l, _):
                pe.wait_ge(mask_ready, 1)
                b = take(("ranks", 0), (items_ready, 1))
                m0, m1 = route[:, 0, 0:E], route[:, 0, E:2 * E]
                nc.tensor.matmul(ps[:, b, 0:E], before[:, :], m0, start=True, stop=True)
                nc.tensor.matmul(ps[:, b, E:2 * E], ones[:, :], m0, start=True, stop=False)
                nc.tensor.matmul(ps[:, b, E:2 * E], before[:, :], m1, start=False, stop=True)
                nc.tensor.matmul(ps[:, b, 2 * E:3 * E], ones[:, :], m0, start=True, stop=False)
                nc.tensor.matmul(ps[:, b, 2 * E:3 * E], ones[:, :], m1, start=False, stop=True)\
                    .then_inc(ranks_done, 1)

            do = {"ada": ada, "ada_cols": ada_cols, "turn": turn_stream,
                  "u": project("u", lambda l, i, h: (z_ready, 2 * l + h + 1)),
                  "q": project("q", lambda l, i, h: (q_ready, 4 * l + 2 * i + h + 1)),
                  "gate": project("gate", lambda l, i, h: (gate_ready, 8 * l + 2 * i + h + 1)),
                  "kv": kv, "scores": scores, "probsT": probs_turn, "pv": pv, "convT": conv_turn,
                  "normT": norm_turn, "conv_out": conv_out, "attn_out": attn_out, "w_o": out_proj,
                  "gains": spread_gains, "ffn_up": ffn_up, "ffn_down": ffn_down, "router": router,
                  "ranks": ranks}
            for kind, l, i in steps:
                if kind == "ffn_up" and i == 0:
                    turn[0], size[0] = 0, 4
                if kind == "turn":
                    turn[0], size[0] = 0, 8
                do[kind](l, i)

            for b in range(8):
                if holder[b] is not None:
                    pe.wait_ge(*holder[b])

            def gather(n):
                pe.wait_ge(put_ready, 2 * n)
                for h in range(2):
                    for j in range(4):
                        kb = 4 * h + j
                        for t in range(TB):
                            mm = nc.tensor.matmul(ps[:, 5 + h, P * j:P * j + P], xn[:, t, P * kb:P * kb + P],
                                                  put[:, t, :], start=(t == 0), stop=(t == TB - 1))
                mm.then_inc(gather_done, 1)

            gather(1)
            turn[0] = 3
            spread_gains(3, 0)
            pe.sem_inc(putT_done, 1)
            pe.sem_inc(scatter_done, 1)
            n_items = pe.value_load(items_i[0:1, 0:1], min_val=E, max_val=MAX_ITEMS)
            with pe.Fori(0, n_items) as it:
                def item_split(j, k):
                    pe.wait_ge(lo_ready, it * ITEM_GRAINS + (K0 + j + 1))
                    n = (K0 + j) % AHEAD
                    return cut_in(w_hi[:, n, :], k), cut_in(w_lo[:, n, :], k)

                def up(f, halves=(0, 1)):
                    for h in halves:
                        for g in range(2):
                            w = item_split(up_at(f) + 2 * h + g, 4)
                            for k in range(4):
                                mm = product(ps[:, h, :], (hTi_hi, hTi_lo), (whole, 4 * g + k), w, (whole, k),
                                             start=(g == 0 and k == 0), stop=(g == 1 and k == 3))
                            mm.then_inc(wts_used, 1)

                def turn_hidden(f):
                    pe.wait_ge(hid_ready, it * NET + (NFT + f + 1))
                    for j in range(4):
                        mm = nc.tensor.transpose(ps[:, 2, block(j)], hid[:, block(j)], ident[:, :])
                    mm.then_inc(hidT_done, 1)

                def down(f):
                    pe.wait_ge(hid_lo_ready, it * NET + (NFT + f + 1))
                    if f == 0:
                        pe.wait_ge(y_item_ready, it * 2 + 1)
                        pe.wait_ge(gains_ready, 8)
                    for g in range(2):
                        w = item_split(down_at(f) + g, 2)
                        for h in range(2):
                            for k in range(2):
                                mm = product(ps[:, 3 + h, :], (hidT_hi, hidT_lo), (whole, block(2 * g + k)),
                                             w, (whole, k, block(h, 512)),
                                             start=(f == 0 and g == 0 and k == 0),
                                             stop=(f == NET - 1 and g == 1 and k == 1))
                        mm.then_inc(wts_used, 1)

                pe.wait_ge(hTi_lo_ready, it + 1)
                for f in range(NET):
                    up(f, (1,) if f == 1 else (0, 1))
                    if f == 0:
                        pe.wait_ge(y_added, it * 4 + 1)
                        pe.wait_ge(put_g_ready, it * 2 + 2)
                        for t in range(TB):
                            mm = nc.tensor.transpose(ps[:, 7, block(t)], put_g[:, t, :], ident[:, :])
                        mm.then_inc(putT_done, 1)
                        pe.wait_ge(silu_ready, it * NET + (NFT + 1))
                        up(1, (0,))
                    else:
                        down(f - 1)
                    turn_hidden(f)
                gather(it + 2)
                down(NET - 1)
                pe.wait_ge(putT_ready, it + 1)
                for n, (h, t) in enumerate(((0, 0), (0, 1), (1, 0), (1, 1))):
                    b = (7, 5, 6, 2)[n]
                    if t == 0:
                        pe.wait_ge(y_item_ready, it * 2 + (h + 2))
                    if n == 1:
                        pe.wait_ge(hTi_ready, it * 8 + 16)
                    nc.tensor.matmul(ps[:, b, :], put_gT[:, block(t)], y_item[:, block(h, 512)],
                                     start=True, stop=True).then_inc(scatter_done, 1)

        @block.scalar
        def _(act):
            act.dma_start(sinks[:, :], attn_sinks.rearrange("l h -> (l h)").partition_broadcast(P)).then_inc(sinks_in, 16)
            act.dma_start(w_router[:, :, :], moe_router[0].rearrange("(kb p) e -> p kb e", p=P)).then_inc(router_in, 16)

            act.wait_ge(cols_t, 1)
            act.wait_ge(consts, 4)
            b = bank_of[("cols", 0)]
            for j, r in enumerate((128, 64, 124, 124)):
                nc.scalar.copy(cols[:, P * j:P * j + r], ps[:, b, P * j:P * j + r]).then_inc(cols_ready, 1)
            act.wait_ge(cols_ready, 4)
            nc.scalar.activation(c_act[:, :], cols[:, C_C:C_C + KB], ACT.Silu).then_inc(c_ready, 1)

            def weights_done(step):
                act.wait_ge(wts_used, used(step))

            split_order = [g for g in load if g[0] != "ada"]

            def high(k):
                slot, value = landed(R0 + k - K0 if k >= K0 else ring_no[split_order[k]])
                act.wait_ge(slot_in[slot], value)
                if k >= AHEAD:
                    act.wait_ge(wts_used, k - AHEAD + 1)
                nc.scalar.copy(w_hi[:, k % AHEAD, :], ring[:, slot, :]).then_inc(hi_ready, 1)

            def ada(l, i):
                n = 12 * l + i
                act.wait_ge(ada_used, 2 * (n + 1))
                if n:
                    act.wait_ge(ada_cols_done, n)
                nc.scalar.copy(mod_part[:, :], ps[:, bank_of[("ada", l, i)], :]).then_inc(mod_part_ready, 1)

            def ada_cols(l, i):
                act.wait_ge(ada_cols_done, 12 * l + i + 1)
                nc.scalar.copy(mod_raw[:, l, 4 * i:4 * i + 4], ps[:, bank_of[("ada_cols", l, i)], 0:4])\
                    .then_inc(mod_raw_ready, 1)

            def turn_stream(s, _):
                act.wait_ge(scales_ready, s + 1)
                for j in range(4):
                    if j % 2 == 0:
                        act.wait_ge(turn_done, 4 * s + j + 1)
                        for kb in (2 * j, 2 * j + 1):
                            nc.scalar.activation(hT[:, kb, :], ps[:, bank_of[("turn", s, j)], S * (kb % 2):S * (kb % 2) + S],
                                                 ACT.Identity, bias=shift_c[:, s, kb:kb + 1],
                                                 scale=scale_c[:, s, kb:kb + 1]).then_inc(hT_act, 1)
                        act.wait_ge(hT_act, 4 * s + j + 2)
                    else:
                        act.wait_ge(hT_dve, 4 * s + j + 1)
                    nc.scalar.copy(in_hi[:, 2 * j:2 * j + 2, :], hT[:, 2 * j:2 * j + 2, :]).then_inc(in_hi_ready, 1)

            def u(l, i):
                if i == 1:
                    weights_done(("u", l, 1))
                    for h in range(2):
                        nc.scalar.activation(conv[:, 2 * h:2 * h + 2, :].rearrange("p a b -> p (a b)"),
                                             ps[:, bank_of[("u", l, 1, h)], :], ACT.Sigmoid).then_inc(sg_ready, 1)

            def q(l, i):
                weights_done(("q", l, i))
                for h in range(2):
                    kb = 4 * i + 2 * h
                    nc.scalar.mul(qT[:, kb:kb + 2, :].rearrange("p a b -> p (a b)"),
                                  ps[:, bank_of[("q", l, i, h)], :], HD ** -0.5).then_inc(q_ready, 1)

            def kv(l, _):
                weights_done(("kv", l, 0))
                src = ps[:, bank_of[("kv", l, 0)], :].rearrange("p (a b) -> p a b", a=2)
                for half in range(2):
                    for to in range(2):
                        nc.scalar.copy(kT[HD * to:HD * to + HD, half::2, :],
                                       src[HD * half:HD * half + HD, :, :]).then_inc(kv_ready, 1)
                nc.scalar.copy(v_tok.rearrange("p a b -> p (a b)"), ps[:, bank_of[("kv", l, 1)], :])\
                    .then_inc(kv_ready, 1)

            def gate(l, i):
                weights_done(("gate", l, i))
                for h in range(2):
                    kb = 4 * i + 2 * h
                    nc.scalar.activation(gT[:, kb:kb + 2, :].rearrange("p a b -> p (a b)"),
                                         ps[:, bank_of[("gate", l, i, h)], :], ACT.Sigmoid).then_inc(gate_ready, 1)

            def scores(l, g):
                n = 4 * l + g
                pr = probs_of[g % 2]
                act.wait_ge(max_ready, n + 1)
                nc.scalar.activation(st_esink[:, g % 2, :], st_dsink[:, g % 2, :], ACT.Exp).then_inc(exp_ready, 1)
                for j in range(8):
                    nc.scalar.activation(pr[:, j, :], pr[:, j, :], ACT.Exp, bias=st_neg[:, g % 2, j:j + 1],
                                         accum_out=st_den[:, g % 2, j:j + 1]).then_inc(exp_ready, 1)

            def normalise(l, g):
                pr = probs_of[g % 2]
                act.wait_ge(rden_ready, 4 * l + g + 1)
                for j in range(8):
                    nc.scalar.mul(pr[:, j, :], pr[:, j, :], st_rden[:, g % 2, j:j + 1]).then_inc(probs_ready, 1)

            def probs_turn(l, g):
                n = 4 * l + g
                for i in range(GRP):
                    act.wait_ge(probsT_done, 4 * n + i + 1)
                    if i == 0 and n:
                        act.wait_ge(pv_done, n)
                    nc.scalar.copy(pT[:, i, :], ps[:, bank_of[("probsT", l, g, i)], 0:3 * P]).then_inc(pT_ready, 1)

            def pv(l, g):
                act.wait_ge(pv_done, 4 * l + g + 1)
                nc.scalar.copy(mid_hi[:, 2 * g:2 * g + 2, :].rearrange("p a b -> p (a b)"),
                               ps[:, bank_of[("pv", l, g)], :]).then_inc(o_hi_ready, 1)

            def conv_turn(l, _):
                for t in range(TB):
                    act.wait_ge(cvar_ready, 2 * l + t + 1)
                    nc.scalar.activation(sd[:, t:t + 1], mv[:, t, 1:2], ACT.Sqrt, bias=epsc[:, 0:1]).then_inc(csd_ready, 1)

            def norm_turn(l, _):
                for j in range(2):
                    act.wait_ge(normT_done, 2 * l + j + 1)
                    for cb in (2 * j, 2 * j + 1):
                        nc.scalar.activation(zT[:, cb, :], ps[:, bank_of[("normT", l, j)], S * (cb % 2):S * (cb % 2) + S],
                                             ACT.Silu, bias=cols[:, C_CB + CB * l + cb:C_CB + CB * l + cb + 1],
                                             scale=cols[:, C_CG + CB * l + cb:C_CG + CB * l + cb + 1]).then_inc(zT_ready, 1)
                    act.wait_ge(zT_ready, 4 * l + 2 * j + 2)
                    nc.scalar.copy(in_hi[:, 2 * j:2 * j + 2, :], zT[:, 2 * j:2 * j + 2, :]).then_inc(zT_hi_ready, 1)

            def conv_out(l, _):
                for j in range(4):
                    act.wait_ge(merged, 4 * l + j + 1)
                    to = merged_at(2 * j)
                    nc.scalar.copy(in_hi[:, to:to + 2, :], gT[:, 2 * j:2 * j + 2, :]).then_inc(mg_hi_ready, 1)

            def spread_gains(s, _):
                act.wait_ge(gains_done, s + 1)
                if s:
                    act.wait_ge(y_gained, 4 * s)
                for h in range(2):
                    nc.scalar.copy(gains[:, 512 * h:512 * h + 512], ps[:, bank_of[("gains", s, h)], :])\
                        .then_inc(gains_ready, 1)

            def residual(s):
                for t in range(TB):
                    act.wait_ge(var_ready, 2 * s + t + 1)
                    nc.scalar.activation(sd[:, t:t + 1], mv[:, t, 1:2], ACT.Sqrt, bias=epsc[:, 0:1]).then_inc(sd_ready, 1)

            def out_proj(l, i):
                if i == 1:
                    residual(2 * l)

            def ffn_up(l, f):
                weights_done(("ffn_up", 0, f))
                if f >= 2:
                    act.wait_ge(hid_ready, f - 1)
                nc.scalar.activation(gated_d[:, f % 2, :], ps[:, bank_of[("ffn_up", f, 0)], :], ACT.Silu)\
                    .then_inc(silu_ready, 1)
                act.wait_ge(hid_ready, f + 1)
                if f >= 2:
                    weights_done(("ffn_down", 0, f - 2))
                nc.scalar.copy(mid_hi[:, 2 * (f % 2):2 * (f % 2) + 2, :].rearrange("p a b -> p (a b)"),
                               hid_d[:, f % 2, :]).then_inc(hid_hi_ready, 1)

            def ffn_down(l, f):
                if f == NFT - 1:
                    residual(1)

            def router(l, _):
                act.wait_ge(gap_ready, 1)
                nc.scalar.activation(route[:, 11, 0:2], route[:, 9, 0:2], ACT.Exp).then_inc(gap_exp, 1)

            do = {"ada": ada, "ada_cols": ada_cols, "turn": turn_stream, "u": u, "q": q, "kv": kv,
                  "gate": gate, "scores": scores, "probsT": probs_turn, "pv": pv, "convT": conv_turn,
                  "normT": norm_turn, "conv_out": conv_out, "gains": spread_gains, "w_o": out_proj,
                  "ffn_up": ffn_up, "ffn_down": ffn_down, "router": router}
            held = ()
            for kind, l, i in steps:
                mine = [k for g, k in split_no.items() if g[:3] == (kind, l, i) and k + AHEAD < K0]
                if (kind, i) in NORMALISE_IN:
                    normalise(l, NORMALISE_IN[kind, i])
                for k in mine[:-1]:
                    high(k + AHEAD)
                if kind in do:
                    do[kind](l, i)
                last = mine[-1:] if (kind, l) != ("turn", 0) else range(-AHEAD, 0)
                if (kind, l, i) in HOLD:
                    held = last
                    continue
                for k in last:
                    high(k + AHEAD)
                if held and kind == "turn":
                    for k in held:
                        high(k + AHEAD)
                    held = ()
                if (kind, l, i) == ("ada_cols", 1, 11):
                    for k in range(K0, K0 + AHEAD):
                        high(k)

            def gathered():
                for j in range(4):
                    nc.scalar.activation(hTi[:, j, :], ps[:, 5, P * j:P * j + P], ACT.Identity,
                                         bias=shift_c[:, 3, j:j + 1], scale=scale_c[:, 3, j:j + 1]).then_inc(hTi_ready, 1)

            act.sem_inc(y_item_ready, 1)
            act.wait_ge(gather_done, 1)
            gathered()
            act.wait_ge(hTi_ready, 8)
            nc.scalar.copy(hTi_hi, hTi).then_inc(hTi_hi_ready, 1)
            spread_gains(3, 0)
            nc.scalar.activation(mod_part[:, 0:KB], c_act[:, :], ACT.Silu)
            n_items = act.value_load(items_i[0:1, 0:1], min_val=E, max_val=MAX_ITEMS)
            with act.Fori(0, n_items) as it:
                def item_high(j):
                    slot, value = landed(R0 + j)
                    act.wait_ge(slot_in[slot], it * (16 * ITEM_GRAINS // SLOTS) + value)
                    act.wait_ge(wts_used, it * ITEM_GRAINS + (K0 + j - AHEAD + 1))
                    nc.scalar.copy(w_hi[:, (K0 + j) % AHEAD, :], ring[:, slot, :]).then_inc(hi_ready, 1)

                for f in range(NET):
                    for g in range(1 if f == 1 else 0, 3):
                        item_high(up_at(f) + g + AHEAD)
                    act.wait_ge(wts_used, it * ITEM_GRAINS + (K0 + up_at(f) + 4))
                    act.wait_ge(hid_ready, it * NET + (NFT + f))
                    nc.scalar.activation(gated, ps[:, 0, :], ACT.Silu).then_inc(silu_ready, 1)
                    item_high(up_at(f) + 3 + AHEAD)
                    if f == 0:
                        act.wait_ge(putT_done, it + 2)
                        act.wait_ge(scatter_done, it * 4 + 1)
                        nc.scalar.copy(put_gT[:, :], ps[:, 7, 0:S]).then_inc(putT_ready, 1)
                        item_high(up_at(1) + AHEAD)
                    else:
                        for g in range(2):
                            item_high(down_at(f - 1) + g + AHEAD)
                    act.wait_ge(hidT_done, it * NET + (f + 1))
                    nc.scalar.copy(hidT_hi, ps[:, 2, :]).then_inc(hid_hi_ready, 1)
                act.wait_ge(gather_done, it + 2)
                gathered()
                act.wait_ge(hTi_ready, it * 8 + 16)
                nc.scalar.copy(hTi_hi, hTi).then_inc(hTi_hi_ready, 1)
                item_high(down_at(NET - 1) + AHEAD)
                act.wait_ge(wts_used, it * ITEM_GRAINS + (K0 + ITEM_GRAINS))
                for h in range(2):
                    nc.scalar.copy(y_item[:, 512 * h:512 * h + 512], ps[:, 3 + h, :]).then_inc(y_item_ready, 1)
                item_high(down_at(NET - 1) + 1 + AHEAD)
            residual(3)

        @block.vector
        def _(dve):
            count = [0]

            def link(ins):
                count[0] += 1
                ins.then_inc(dve_chain, 1)
                dve.wait_ge(dve_chain, count[0])

            dve.wait_ge(c_ready, 1)
            dve.wait_ge(consts, 3)
            for kb in range(KB):
                ins = nc.vector.tensor_scalar(c_wide[:, kb, :], ones[:, 0:32], c_act[:, kb:kb + 1], None, ALU.mult)
            ins.then_inc(cw_ready, 1)
            nd = neg_dist[:, :, :].rearrange("p a b -> p (a b)")
            link(nc.vector.tensor_copy(nd, iota_i))
            link(nc.vector.scalar_tensor_tensor(out=nd, in0=nd, scalar=-1.0, in1=nd, op0=ALU.mult, op1=ALU.min))
            for p0, t, a, z in ((0, 0, CHUNK, S), (CHUNK, 0, 2 * CHUNK, S), (0, 1, 0, CHUNK),
                                (0, 1, 3 * CHUNK, S), (CHUNK, 1, 0, 2 * CHUNK)):
                link(nc.vector.memset(neg_dist[p0:p0 + CHUNK, t, a:z], FAR))

            def weights_done(step):
                dve.wait_ge(wts_used, used(step))

            split_order = [g for g in load if g[0] != "ada"]

            def low(k):
                slot, _ = landed(R0 + k - K0 if k >= K0 else ring_no[split_order[k]])
                dve.wait_ge(hi_ready, k + 1)
                nc.vector.tensor_tensor(w_lo[:, k % AHEAD, :], ring[:, slot, :], w_hi[:, k % AHEAD, :].bitcast(F32),
                                        ALU.subtract).then_inc(lo_ready, 1)

            def turn_stream(s, _):
                dve.wait_ge(scales_ready, s + 1)
                for j in range(4):
                    if j % 2:
                        dve.wait_ge(turn_done, 4 * s + j + 1)
                        for kb in (2 * j, 2 * j + 1):
                            nc.vector.tensor_scalar(hT[:, kb, :], ps[:, bank_of[("turn", s, j)], S * (kb % 2):S * (kb % 2) + S],
                                                    scale_c[:, s, kb:kb + 1], shift_c[:, s, kb:kb + 1],
                                                    ALU.mult, ALU.add).then_inc(hT_dve, 1)
                for j in range(4):
                    dve.wait_ge(in_hi_ready, 4 * s + j + 1)
                    v = slice(2 * j, 2 * j + 2)
                    nc.vector.tensor_tensor(in_lo[:, v, :], hT[:, v, :], in_hi[:, v, :].bitcast(F32),
                                            ALU.subtract).then_inc(in_lo_ready, 1)

            def u(l, i):
                if i == 0:
                    link(nc.vector.memset(zp[:, :, 0:PAD], 0.0))
                    return
                for h in range(2):
                    dve.wait_ge(sg_ready, 2 * l + h + 1)
                    nc.vector.tensor_tensor(zp[:, 2 * h:2 * h + 2, PAD:PAD + S],
                                            ps[:, bank_of[("u", l, 0, h)], :].rearrange("p (a b) -> p a b", a=2),
                                            conv[:, 2 * h:2 * h + 2, :], ALU.mult).then_inc(z_ready, 1)
                dve.wait_ge(z_ready, 2 * (l + 1))

            def taps(l, a, z):
                base = CB * TAPS * l
                for n in range(a, z):
                    j, cb = n // CB, n % CB
                    col = C_DW + P * l + n
                    w = cols[:, col:col + 1]
                    if j == 0:
                        ins = nc.vector.tensor_scalar(conv[:, cb, :], zp[:, cb, 0:S], w,
                                                      cols[:, C_DWB + CB * l + cb:C_DWB + CB * l + cb + 1],
                                                      ALU.mult, ALU.add)
                    else:
                        dve.wait_ge(conv_step, base + n - CB + 1)
                        ins = nc.vector.scalar_tensor_tensor(out=conv[:, cb, :], in0=zp[:, cb, j:j + S], scalar=w,
                                                             in1=conv[:, cb, :], op0=ALU.mult, op1=ALU.add)
                    ins.then_inc(conv_step, 1)

            def scores(l, g):
                n = 4 * l + g
                pr = probs_of[g % 2]
                if l == 0 and g == 0:
                    dve.wait_ge(sinks_in, 16)
                for i in range(GRP):
                    h = GRP * g + i
                    dve.wait_ge(scores_done, 16 * l + h + 1)
                    if i == 0 and n >= 2:
                        dve.wait_ge(probsT_done, 4 * (n - 1))
                    if i == 0 and l and g == 0:
                        dve.wait_ge(x_ready, 4)
                    slope = 2.0 ** (-8.0 * (h + 1) / HEADS)
                    nc.vector.scalar_tensor_tensor(out=pr[:, 2 * i:2 * i + 2, :].rearrange("p a b -> p (a b)"),
                                                   in0=nd, scalar=slope,
                                                   in1=ps[:, bank_of[("scores", l, g, i)], :],
                                                   op0=ALU.mult, op1=ALU.add).then_inc(biased, 1)
                dve.wait_ge(biased, 4 * (n + 1))
                sk = sinks[:, HEADS * l + GRP * g:HEADS * l + GRP * (g + 1)].unsqueeze(2).to_broadcast([P, GRP, TB])
                by_head = lambda v: v[:, g % 2, :].rearrange("p (a b) -> p a b", a=GRP)
                link(nc.vector.tensor_reduce(st_max[:, g % 2, :], pr, AX.X, ALU.max))
                link(nc.vector.tensor_tensor(by_head(st_max), by_head(st_max), sk, ALU.max))
                link(nc.vector.tensor_scalar(st_neg[:, g % 2, :], st_max[:, g % 2, :], -1.0, None, ALU.mult))
                nc.vector.tensor_tensor(by_head(st_dsink), sk, by_head(st_max), ALU.subtract).then_inc(max_ready, 1)

            def one_over_sum(l, g):
                n = 4 * l + g
                dve.wait_ge(exp_ready, 9 * (n + 1))
                link(nc.vector.tensor_tensor(st_den[:, g % 2, :], st_den[:, g % 2, :], st_esink[:, g % 2, :], ALU.add))
                nc.vector.reciprocal(st_rden[:, g % 2, :], st_den[:, g % 2, :]).then_inc(rden_ready, 1)

            def pv(l, g):
                dve.wait_ge(o_hi_ready, 4 * l + g + 1)
                v = slice(2 * g, 2 * g + 2)
                nc.vector.tensor_tensor(mid_lo[:, v, :].rearrange("p a b -> p (a b)"), ps[:, bank_of[("pv", l, g)], :],
                                        mid_hi[:, v, :].bitcast(F32).rearrange("p a b -> p (a b)"),
                                        ALU.subtract).then_inc(oT_ready, 1)

            def norm_turn(l, _):
                for j in range(2):
                    v = slice(2 * j, 2 * j + 2)
                    dve.wait_ge(zT_hi_ready, 2 * l + j + 1)
                    nc.vector.tensor_tensor(in_lo[:, v, :], zT[:, v, :], in_hi[:, v, :].bitcast(F32),
                                            ALU.subtract).then_inc(zT_lo_ready, 1)

            def conv_turn(l, _):
                for t in range(TB):
                    bank = ps[:, bank_of[("convT", l, t)], :]
                    dve.wait_ge(convT_done, 2 * l + t + 1)
                    link(nc.vector.bn_stats(bn[:, t, 0, :], bank))
                    nc.vector.bn_aggr(mv[:, t, :], bn[:, t, 0, :]).then_inc(cvar_ready, 1)
                dve.wait_ge(convT_done, 2 * (l + 1))
                for t in range(TB):
                    dve.wait_ge(csd_ready, 2 * l + t + 1)
                    link(nc.vector.reciprocal(rs[:, t:t + 1], sd[:, t:t + 1]))
                    nc.vector.tensor_scalar(zn[:, t, :], ps[:, bank_of[("convT", l, t)], :], mv[:, t, 0:1], rs[:, t:t + 1],
                                            ALU.subtract, ALU.mult).then_inc(zn_ready, 1)

            def attn_out(l, i):
                if i == 0:
                    dve.wait_ge(gate_ready, 8 * (l + 1))
                for h in range(2):
                    if h == 0:
                        dve.wait_ge(attn_bank, 2 * l + i + 1)
                    else:
                        weights_done(("attn_out", l, i))
                    kb = KB + 4 * i + 2 * h
                    v = gT[:, kb:kb + 2, :].rearrange("p a b -> p (a b)")
                    nc.vector.tensor_tensor(v, ps[:, bank_of[("attn_out", l, i, h)], :], v, ALU.mult)\
                        .then_inc(gated_attn, 1)

            def merge(l, j):
                dve.wait_ge(gated_attn, 4 * l + j + 1)
                dve.wait_ge(gated_conv, 4 * l + j + 1)
                v = gT[:, 2 * j:2 * j + 2, :]
                nc.vector.tensor_tensor(v, v, gT[:, KB + 2 * j:KB + 2 * j + 2, :], ALU.add).then_inc(merged, 1)

            def merged_low(l, j):
                dve.wait_ge(mg_hi_ready, 4 * l + j + 1)
                to = merged_at(2 * j)
                nc.vector.tensor_tensor(in_lo[:, to:to + 2, :], gT[:, 2 * j:2 * j + 2, :],
                                        in_hi[:, to:to + 2, :].bitcast(F32), ALU.subtract).then_inc(mg_lo_ready, 1)

            def conv_out(l, _):
                for j in range(4):
                    if j < 3:
                        dve.wait_ge(conv_bank, 3 * l + j + 1)
                    else:
                        weights_done(("conv_out", l, 0))
                    v = gT[:, 2 * j:2 * j + 2, :].rearrange("p a b -> p (a b)")
                    nc.vector.tensor_tensor(v, ps[:, bank_of[("conv_out", l, j)], :], v, ALU.mult)\
                        .then_inc(gated_conv, 1)
                    merge(l, j)
                    if j:
                        merged_low(l, j - 1)
                merged_low(l, 3)

            def add_y(s, h, whole):
                if h == 0:
                    dve.wait_ge(gains_ready, 2 * (s + 1))
                    if s:
                        dve.wait_ge(x_ready, 2 * s)
                c0 = slice(512 * h, 512 * h + 512)
                for t in range(TB):
                    dve.wait_ge(*whole[t])
                    nc.vector.tensor_tensor(xn[:, t, c0], ps[:, bank_of[("y", s, t, h)], :], gains[:, c0], ALU.mult).then_inc(y_gained, 1)
                    dve.wait_ge(y_gained, 4 * s + 2 * h + t + 1)
                    nc.vector.scalar_tensor_tensor(out=x_tok[:, t, c0], in0=x_tok[:, t, c0], scalar=ALPHA,
                                                   in1=xn[:, t, c0], op0=ALU.mult, op1=ALU.add).then_inc(summed, 1)
                for t in range(TB):
                    dve.wait_ge(summed, 4 * s + 2 * h + t + 1)
                    nc.vector.bn_stats(bn[:, t, h, :], x_tok[:, t, c0]).then_inc(stats, 1)

            def normalise_x(s):
                for t in range(TB):
                    dve.wait_ge(stats, 4 * s + 3 + t)
                    nc.vector.bn_aggr(mv[:, t, :], bn[:, t, :, :].rearrange("p a b -> p (a b)")).then_inc(var_ready, 1)
                dve.wait_ge(var_ready, 2 * (s + 1))
                for t in range(TB):
                    dve.wait_ge(sd_ready, 2 * s + t + 1)
                    link(nc.vector.reciprocal(rs[:, t:t + 1], sd[:, t:t + 1]))
                    nc.vector.tensor_scalar(xn[:, t, :], x_tok[:, t, :], mv[:, t, 0:1], rs[:, t:t + 1],
                                            ALU.subtract, ALU.mult).then_inc(xn_ready, 1)

            def out_proj(l, i):
                add_y(2 * l, i, ((y_part, 5 * l + i + 1), (wts_used, used(("w_o", l, i)))))
                if i == 1:
                    normalise_x(2 * l)

            def ffn_up(l, f):
                weights_done(("ffn_up", 0, f))
                dve.wait_ge(silu_ready, f + 1)
                if f >= 2:
                    dve.wait_ge(hid_lo_ready, f - 1)
                nc.vector.tensor_tensor(hid_d[:, f % 2, :], ps[:, bank_of[("ffn_up", f, 1)], :], gated_d[:, f % 2, :],
                                        ALU.mult).then_inc(hid_ready, 1)
                dve.wait_ge(hid_hi_ready, f + 1)
                v = slice(2 * (f % 2), 2 * (f % 2) + 2)
                nc.vector.tensor_tensor(mid_lo[:, v, :].rearrange("p a b -> p (a b)"), hid_d[:, f % 2, :],
                                        mid_hi[:, v, :].bitcast(F32).rearrange("p a b -> p (a b)"),
                                        ALU.subtract).then_inc(hid_lo_ready, 1)

            def ffn_down(l, f):
                if f == NFT - 1:
                    add_y(1, 0, ((y_part, 3), (y_part, 4)))
                    add_y(1, 1, ((y_part, 5), (wts_used, used(("ffn_down", 0, NFT - 1)))))
                    normalise_x(1)

            def router(l, _):
                r = lambda n: route[:, n, :].rearrange("p (t e) -> p t e", t=TB)
                pair = lambda n: route[:, n, 0:2]
                wide = lambda n: route[:, n, 0:2].unsqueeze(2).to_broadcast([P, TB, E])
                nc.vector.memset(prefix[:, :, :], 0.0)
                nc.vector.memset(item_pos[:, :, MAX_ITEMS:], -1.0)
                dve.wait_ge(router_done, 1)
                dve.wait_ge(consts, 5)
                lg, rev = ps[:, bank_of[("router", 0)], 0:TB * E].rearrange("p (t e) -> p t e", t=TB), e_rev
                link(nc.vector.tensor_copy(r(1), lg))
                src = 1
                for n, (best, onehot, key, keymax) in enumerate(((2, 3, 4, 5), (6, 7, 4, 5))):
                    link(nc.vector.tensor_reduce(pair(best), r(src), AX.X, ALU.max))
                    link(nc.vector.tensor_tensor(r(key), r(src), wide(best), ALU.is_equal))
                    link(nc.vector.tensor_tensor(r(key), r(key), rev, ALU.mult))
                    link(nc.vector.tensor_reduce(pair(keymax), r(key), AX.X, ALU.max))
                    link(nc.vector.tensor_tensor(r(onehot), rev, wide(keymax), ALU.is_equal))
                    if n == 0:
                        link(nc.vector.scalar_tensor_tensor(out=route[:, 8, :], in0=route[:, 3, :], scalar=-3e38,
                                                            in1=route[:, 1, :], op0=ALU.mult, op1=ALU.add))
                        src = 8
                nc.vector.tensor_tensor(route[:, 0, :], route[:, 3, :], route[:, 7, :], ALU.add).then_inc(mask_ready, 1)
                nc.vector.tensor_tensor(pair(9), pair(6), pair(2), ALU.subtract).then_inc(gap_ready, 1)
                dve.wait_ge(gap_exp, 1)
                link(nc.vector.tensor_scalar(pair(10), pair(11), 1.0, None, ALU.add))
                link(nc.vector.reciprocal(pair(12), pair(10)))
                link(nc.vector.tensor_tensor(pair(13), pair(12), pair(11), ALU.mult))
                link(nc.vector.tensor_tensor(r(3), r(3), wide(12), ALU.mult))
                link(nc.vector.tensor_tensor(r(7), r(7), wide(13), ALU.mult))
                link(nc.vector.tensor_tensor(r(14), r(3), r(7), ALU.add))

            def ranks(l, _):
                r = lambda n: route[:, n, :].rearrange("p (t e) -> p t e", t=TB)
                bank = ps[:, bank_of[("ranks", 0)], :]
                dve.wait_ge(ranks_done, 1)
                dve.wait_ge(mask_ready, 1)
                link(nc.vector.tensor_scalar(route[:, 1, :], bank[:, 0:TB * E], 1.0, None, ALU.add))
                link(nc.vector.tensor_tensor(route[:, 1, :], route[:, 1, :], route[:, 0, :], ALU.mult))
                link(nc.vector.tensor_scalar(route[:, 1, :], route[:, 1, :], -1.0, None, ALU.add))
                link(nc.vector.tensor_copy(item_pos[:, :, 0:E], r(1)))
                link(nc.vector.tensor_copy(item_gate[:, :, 0:E], r(14)))
                place(0)
                big, ahead, upto = prefix[:, 0, E:], route[:, 2, 0:E], prefix[:, 1, E:]
                link(nc.vector.tensor_scalar(big, bank[:, 2 * E:3 * E], float(P), None, ALU.is_gt))
                for n, (src, to) in enumerate(((0, 1), (1, 2), (2, 1))):
                    link(nc.vector.tensor_tensor(prefix[:, to, E:], prefix[:, src, E:],
                                                 prefix[:, src, E - 2 ** n:2 * E - 2 ** n], ALU.add))
                link(nc.vector.tensor_tensor(ahead, upto, big, ALU.subtract))
                link(nc.vector.tensor_scalar(items_f[:, 0:1], upto[:, E - 1:E], float(E), None, ALU.add))
                M = MAX_ITEMS - E
                each = lambda v: v.unsqueeze(1).to_broadcast([P, M, E])
                link(nc.vector.tensor_tensor(extra_of[:, :, :], each(ahead), extra_no[:, :, :], ALU.is_equal))
                link(nc.vector.tensor_tensor(extra_of[:, :, :], extra_of[:, :, :], each(big), ALU.mult))
                link(nc.vector.tensor_tensor(extra[:, 0], extra_of[:, :, :], each(e_idx), ALU.mult))
                link(nc.vector.tensor_reduce(items_f[:, 1:1 + M], extra[:, 0], AX.X, ALU.add))
                for row, to in ((1, item_pos), (14, item_gate)):
                    for t in range(TB):
                        link(nc.vector.tensor_tensor(extra[:, t], extra_of[:, :, :],
                                                     each(route[:, row, E * t:E * t + E]), ALU.mult))
                        link(nc.vector.tensor_reduce(to[:, t, E:MAX_ITEMS], extra[:, t], AX.X, ALU.add))
                link(nc.vector.tensor_scalar(item_pos[:, :, E:MAX_ITEMS], item_pos[:, :, E:MAX_ITEMS], -float(P),
                                             None, ALU.add))
                nc.vector.tensor_copy(items_i[:, :], items_f[:, :]).then_inc(items_ready, 1)

            def place(col):
                for t in range(TB):
                    nc.vector.tensor_scalar(put[:, t, :], slot_no, item_pos[:, t, bass.ds(col, 1)] if not isinstance(col, int)
                                            else item_pos[:, t, col:col + 1], None, ALU.is_equal).then_inc(put_ready, 1)

            do = {"turn": turn_stream, "u": u, "scores": scores, "pv": pv,
                  "convT": conv_turn, "normT": norm_turn, "attn_out": attn_out, "conv_out": conv_out,
                  "w_o": out_proj, "ffn_up": ffn_up, "ffn_down": ffn_down, "router": router, "ranks": ranks}
            tap, held = [0], None
            for kind, l, i in steps:
                mine = [k for g, k in split_no.items() if g[:3] == (kind, l, i) and k + AHEAD < K0]

                def ahead(k, kind=kind, l=l, i=i, mine=mine):
                    if kind in ("kv", "q", "gate"):
                        n = min(tap[0] + TAPS_STEP, CB * TAPS)
                        taps(l, tap[0], n)
                        tap[0] = n
                    low(k + AHEAD)
                if (kind, i) in NORMALISE_IN:
                    one_over_sum(l, NORMALISE_IN[kind, i])
                if kind == "conv_out":
                    do[kind](l, i)
                for k in mine[:-1]:
                    ahead(k)
                if kind in do and kind != "conv_out":
                    do[kind](l, i)
                last = mine[-1:] if (kind, l) != ("turn", 0) else range(-AHEAD, 0)
                if (kind, l, i) in HOLD_VECTOR:
                    held = HOLD_VECTOR[kind, l, i], last, ahead
                    continue
                for k in last:
                    ahead(k)
                if held and kind == held[0]:
                    for k in held[1]:
                        held[2](k)
                    held = None
                if kind == "w_o":
                    assert tap[0] in (0, CB * TAPS)
                    tap[0] = 0

            def gathered():
                for j in range(4, 8):
                    nc.vector.tensor_scalar(hTi[:, j, :], ps[:, 6, P * (j - 4):P * (j - 4) + P],
                                            scale_c[:, 3, j:j + 1], shift_c[:, 3, j:j + 1],
                                            ALU.mult, ALU.add).then_inc(hTi_ready, 1)

            def gathered_low():
                nc.vector.tensor_tensor(hTi_lo, hTi, hTi_hi.bitcast(F32), ALU.subtract).then_inc(hTi_lo_ready, 1)

            low(K0)
            low(K0 + 1)
            dve.wait_ge(gather_done, 1)
            gathered()
            dve.wait_ge(hTi_hi_ready, 1)
            gathered_low()
            low(K0 + 2)
            n_items = dve.value_load(items_i[0:1, 0:1], min_val=E, max_val=MAX_ITEMS)
            with dve.Fori(0, n_items) as it:
                def item_low(j):
                    slot = (R0 + j) % SLOTS
                    n = (K0 + j) % AHEAD
                    dve.wait_ge(hi_ready, it * ITEM_GRAINS + (K0 + j + 1))
                    nc.vector.tensor_tensor(w_lo[:, n, :], ring[:, slot, :], w_hi[:, n, :].bitcast(F32),
                                            ALU.subtract).then_inc(lo_ready, 1)

                dve.wait_ge(gather_done, it + 1)
                place(it + 1)
                dve.wait_ge(putT_done, it + 1)
                for t in range(TB):
                    nc.vector.tensor_scalar(put_g[:, t, :], slot_no, item_pos[:, t, bass.ds(it, 1)],
                                            item_gate[:, t, bass.ds(it, 1)], ALU.is_equal, ALU.mult)\
                        .then_inc(put_g_ready, 1)
                for f in range(NET):
                    for g in range(1 if f == 1 else 0, 3):
                        item_low(up_at(f) + g + AHEAD)
                    dve.wait_ge(wts_used, it * ITEM_GRAINS + (K0 + up_at(f) + 4))
                    dve.wait_ge(silu_ready, it * NET + (NFT + f + 1))
                    if f:
                        dve.wait_ge(hidT_done, it * NET + f)
                    nc.vector.tensor_tensor(hid, ps[:, 1, :], gated, ALU.mult).then_inc(hid_ready, 1)
                    item_low(up_at(f) + 3 + AHEAD)
                    if f == 0:
                        item_low(up_at(1) + AHEAD)
                    else:
                        for g in range(2):
                            item_low(down_at(f - 1) + g + AHEAD)
                    dve.wait_ge(hid_hi_ready, it * NET + (NFT + f + 1))
                    nc.vector.tensor_tensor(hidT_lo, ps[:, 2, :], hidT_hi.bitcast(F32), ALU.subtract)\
                        .then_inc(hid_lo_ready, 1)
                dve.wait_ge(gather_done, it + 2)
                gathered()
                dve.wait_ge(hTi_hi_ready, it + 2)
                gathered_low()
                item_low(down_at(NET - 1) + AHEAD)
                for n, (h, t) in enumerate(((0, 0), (0, 1), (1, 0), (1, 1))):
                    dve.wait_ge(scatter_done, it * 4 + (n + 2))
                    if n == 0:
                        dve.wait_ge(y_added, it * 4 + 1)
                    y = y_sum[:, t, 512 * h:512 * h + 512]
                    nc.vector.tensor_tensor(y, ps[:, (7, 5, 6, 2)[n], :], y, ALU.add).then_inc(y_added, 1)
                item_low(down_at(NET - 1) + 1 + AHEAD)
            link(nc.vector.memset(st_max[:, 0, :], 0.0))
            dve.wait_ge(gains_ready, 8)
            dve.wait_ge(x_ready, 6)
            for t in range(TB):
                nc.vector.tensor_tensor(xn[:, t, :], y_sum[:, t, :], gains, ALU.mult).then_inc(y_gained, 1)
                dve.wait_ge(y_gained, 12 + t + 1)
                nc.vector.scalar_tensor_tensor(out=x_tok[:, t, :], in0=x_tok[:, t, :], scalar=ALPHA,
                                               in1=xn[:, t, :], op0=ALU.mult, op1=ALU.add).then_inc(summed, 1)
                dve.wait_ge(summed, 12 + t + 1)
                for h in range(2):
                    nc.vector.bn_stats(bn[:, t, h, :], x_tok[:, t, 512 * h:512 * h + 512]).then_inc(stats, 1)
                dve.wait_ge(stats, 12 + 2 * t + 2)
                nc.vector.bn_aggr(mv[:, t, :], bn[:, t, :, :].rearrange("p a b -> p (a b)")).then_inc(var_ready, 1)
            dve.wait_ge(fin_in, 32)
            dve.wait_ge(var_ready, 8)
            for t in range(TB):
                nc.vector.scalar_tensor_tensor(out=xn[:, t, :], in0=x_tok[:, t, :], scalar=mv[:, t, 0:1], in1=fin_g,
                                               op0=ALU.subtract, op1=ALU.mult).then_inc(xn_ready, 1)
                dve.wait_ge(sd_ready, 6 + t + 1)
                link(nc.vector.reciprocal(rs[:, t:t + 1], sd[:, t:t + 1]))
                dve.wait_ge(xn_ready, 6 + t + 1)
                nc.vector.scalar_tensor_tensor(out=xn[:, t, :], in0=xn[:, t, :], scalar=rs[:, t:t + 1], in1=fin_b,
                                               op0=ALU.mult, op1=ALU.add).then_inc(out_ready, 1)

        @block.gpsimd
        def _(pool):
            count = [0]

            def link(ins):
                count[0] += 1
                ins.then_inc(pool_chain, 1)
                pool.wait_ge(pool_chain, count[0])

            link(nc.gpsimd.memset(ident[:, :], 0.0))
            nc.gpsimd.affine_select(out=ident[:, :], in_=ident[:, :], compare_op=ALU.not_equal, fill=1.0, base=0,
                                    pattern=[[-1, P]], channel_multiplier=1).then_inc(consts, 1)
            nc.gpsimd.memset(ones[:, :], 1.0).then_inc(consts, 1)
            nc.gpsimd.iota(iota_i.rearrange("p (a b) -> p a b", a=TB), pattern=[[P, TB], [-1, S]], base=0,
                           channel_multiplier=1).then_inc(consts, 1)
            nc.gpsimd.memset(epsc[:, :], EPS)
            link(nc.gpsimd.memset(pick4[:, :], 0.0))
            for j in range(4):
                link(nc.gpsimd.memset(pick4[32 * j:32 * j + 1, :], 1.0))
            link(nc.gpsimd.memset(before[:, :], 1.0))
            link(nc.gpsimd.affine_select(out=before[:, :], in_=before[:, :], compare_op=ALU.is_gt, fill=0.0, base=0,
                                         pattern=[[1, P]], channel_multiplier=-1))
            nc.gpsimd.memset(st_den[:, :, :], 0.0).then_inc(consts, 1)

            def bias_c(l, i):
                return cols[:, C_BADA + 48 * l + i * KB:C_BADA + 48 * l + (i + 1) * KB]

            def scales(s):
                l, base = s // 2, 3 * (s % 2)
                pool.wait_ge(cols_ready, 4)
                pool.wait_ge(mod_raw_ready, 12 * l + (4 if s % 2 == 0 else 10))
                raw = lambda i: mod_raw[:, l, i * KB:(i + 1) * KB]
                link(nc.gpsimd.tensor_tensor(tiny[:, 0, :], raw(base + 1), bias_c(l, base + 1), ALU.add))
                if s == 0:
                    link(nc.gpsimd.tensor_scalar(scale_c[:, 0, :], tiny[:, 0, :], 1.0, None, ALU.add))
                    nc.gpsimd.tensor_tensor(shift_c[:, 0, :], raw(0), bias_c(l, 0), ALU.add).then_inc(scales_ready, 1)
                    return
                gam = cols[:, C_LNG + KB * (s - 1):C_LNG + KB * s]
                bet = cols[:, C_LNB + KB * (s - 1):C_LNB + KB * s]
                link(nc.gpsimd.tensor_scalar(tiny[:, 0, :], tiny[:, 0, :], 1.0, None, ALU.add))
                link(nc.gpsimd.tensor_tensor(scale_c[:, s, :], tiny[:, 0, :], gam, ALU.mult))
                link(nc.gpsimd.tensor_tensor(tiny[:, 1, :], raw(base), bias_c(l, base), ALU.add))
                link(nc.gpsimd.tensor_tensor(tiny[:, 2, :], tiny[:, 0, :], bet, ALU.mult))
                nc.gpsimd.tensor_tensor(shift_c[:, s, :], tiny[:, 1, :], tiny[:, 2, :], ALU.add).then_inc(scales_ready, 1)

            def diagonal(s):
                l, i = s // 2, 2 + 3 * (s % 2)
                pool.wait_ge(mod_raw_ready, 12 * l + (6 if s % 2 == 0 else 12))
                if s % 2 == 0:
                    pool.wait_ge(probsT_done, 16 * (l + 1))
                link(nc.gpsimd.tensor_tensor(tiny[:, 3, :], mod_raw[:, l, i * KB:(i + 1) * KB], bias_c(l, i), ALU.add))
                nc.gpsimd.tensor_tensor(lnbuf.rearrange("p (k n) -> p k n", k=KB),
                                        ident[:, :].unsqueeze(1).to_broadcast([P, KB, P]),
                                        tiny[:, 3, :].unsqueeze(2).to_broadcast([P, KB, P]), ALU.mult)\
                    .then_inc(diag_ready, 1)

            def update(s):
                for n, par in enumerate((post_ln_g, post_ln_b)):
                    if n == 0:
                        pool.wait_ge(gains_done, s + 1 if s < 2 else 4)
                    pool.dma_start(lnbuf[:, :], par[s // 2, s % 2].partition_broadcast(P)).then_inc(ln_in, 16)
                    pool.wait_ge(ln_in, 16 * (2 * s + n + 1))
                    if n == 0:
                        pool.wait_ge(xn_ready, 2 * (s + 1))
                    for t in range(TB):
                        ins = nc.gpsimd.tensor_tensor(x_tok[:, t, :], xn[:, t, :] if n == 0 else x_tok[:, t, :],
                                                      lnbuf[:, :], ALU.mult if n == 0 else ALU.add)
                        if n == 0:
                            link(ins)
                        else:
                            ins.then_inc(x_ready, 1)

            def expert_constants():
                pool.wait_ge(xn_ready, 6)
                link(nc.gpsimd.iota(slot_no, pattern=[[1, P]], base=0, channel_multiplier=0,
                                    allow_small_or_imprecise_dtypes=True))
                link(nc.gpsimd.iota(e_rev, pattern=[[0, TB], [-1, E]], base=E, channel_multiplier=0,
                                    allow_small_or_imprecise_dtypes=True))
                link(nc.gpsimd.iota(extra_no[:, :, :], pattern=[[1, MAX_ITEMS - E], [0, E]], base=0,
                                    channel_multiplier=0, allow_small_or_imprecise_dtypes=True))
                nc.gpsimd.memset(y_sum, 0.0).then_inc(y_added, 1)
                nc.gpsimd.iota(e_idx, pattern=[[1, E]], base=0, channel_multiplier=0,
                               allow_small_or_imprecise_dtypes=True).then_inc(consts, 1)
                pool.dma_start(fin_g, post_ln_g[1, 1].partition_broadcast(P)).then_inc(fin_in, 16)
                pool.dma_start(fin_b, post_ln_b[1, 1].partition_broadcast(P)).then_inc(fin_in, 16)

            scales(0)
            for s in range(3):
                diagonal(s)
                scales(s + 1)
                if s == 2:
                    expert_constants()
                    pool.wait_ge(gains_done, 3)
                    diagonal(3)
                update(s)
                pool.wait_ge(x_ready, 2 * (s + 1))
        @block.sync
        def _(sp):
            small = [(rows[0:96, 0, :], b_ada.rearrange("l (r p) -> (l r) p", p=P)),
                     (rows[96:128, 0, :], post_ln_g.rearrange("l s (r p) -> (l s r) p", p=P)),
                     (rows[0:32, 1, :], post_ln_b.rearrange("l s (r p) -> (l s r) p", p=P)),
                     (rows[32:40, 1, :], c.rearrange("a (r p) -> (a r) p", p=P)),
                     (rows[40:48, 1, :], conv_ln_g.rearrange("l (r p) -> (l r) p", p=P)),
                     (rows[48:56, 1, :], conv_ln_b.rearrange("l (r p) -> (l r) p", p=P)),
                     (rows[56:64, 1, :], conv_dw_b.rearrange("l (r p) -> (l r) p", p=P))]
            small += [(rows[62 * h:62 * h + 62, 2 + l, :],
                       conv_dw_w[l].rearrange("j (r p) -> (j r) p", p=P)[62 * h:62 * h + 62, :])
                      for l in range(DEPTH) for h in range(2)]

            for n, g in enumerate(load):
                if n >= SLOTS:
                    old = load[n - SLOTS]
                    if old[0] == "ada":
                        sp.wait_ge(ada_used, ada_no[old] + 1)
                    else:
                        sp.wait_ge(lo_ready, split_no[old] + 1)
                if n == 6:
                    sp.dma_start(x_tok[:, :, :], x[0].rearrange("(t p) d -> p t d", p=P)).then_inc(x_in, 16)
                sp.dma_start(cut_in(ring[:, n % SLOTS, :], rows_of(g[0])), source(g)).then_inc(slot_in[n % SLOTS], 16)
                if n < 2:
                    for to, src in small[6 * n:6 * n + 6]:
                        sp.dma_start(to, src).then_inc(rows_in, 16)

            order = [None] * ITEM_GRAINS
            for f in range(NET):
                for g in range(2):
                    order[up_at(f) + g] = (moe1, f, g)
                    order[up_at(f) + 2 + g] = (moe3, f, g)
                    order[down_at(f) + g] = (moe2, f, g)

            def fetch(it, e, j):
                w, f, g = order[j % ITEM_GRAINS]
                if j < SLOTS and load[R0 + j - SLOTS][0] == "ada":
                    sp.wait_ge(ada_used, ada_no[load[R0 + j - SLOTS]] + 1)
                sp.wait_ge(lo_ready, it * ITEM_GRAINS + (K0 + j - SLOTS + 1))
                if w is moe2:
                    src = w[bass.ds(e, 1), :, 4 * f + 2 * g:4 * f + 2 * g + 2, :]
                else:
                    src = w[bass.ds(e, 1), :, 4 * g:4 * g + 4, ET * f:ET * f + ET]
                slot = (R0 + j) % SLOTS
                sp.dma_start(cut_in(ring[:, slot, :], 2 if w is moe2 else 4),
                             src.rearrange("a p k n -> (a p) k n")).then_inc(slot_in[slot], 16)

            with sp.Fori(0, E) as it:
                for j in range(ITEM_GRAINS):
                    fetch(it, it, j)
            sp.wait_ge(items_ready, 1)
            n_items = sp.value_load(items_i[0:1, 0:1], min_val=E, max_val=MAX_ITEMS)
            with sp.If(n_items > E):
                with sp.Fori(E, n_items) as it:
                    e = sp.value_load(items_i[0:1, bass.ds(it - (E - 1), 1)], min_val=0, max_val=E - 1)
                    for j in range(ITEM_GRAINS):
                        fetch(it, e, j)
            for j in range(AHEAD):
                fetch(n_items, 0, j)
            for t in range(TB):
                sp.wait_ge(out_ready, t + 1)
                sp.dma_start(out[0, P * t:P * t + P, :], xn[:, t, :]).then_inc(out_done, 16)
            sp.wait_ge(out_done, 16 * TB)


_INS = ['x', 'c', 'w_ada', 'b_ada', 'w_in', 'conv_dw_w', 'conv_dw_b', 'conv_ln_g', 'conv_ln_b', 'w_conv_out',
        'w_attn_out', 'attn_sinks', 'w_o', 'post_ln_g', 'post_ln_b', 'ffn_w1', 'ffn_w3', 'ffn_w2', 'moe_router',
        'moe_w1', 'moe_w3', 'moe_w2']
_OUTS = [((1, 256, 1024), 'float32')]


def kernel(**inputs):
    import numpy as _np
    import concourse.bacc as _bacc
    from concourse import mybir as _mybir
    from concourse.bass_utils import run_bass_kernel_spmd as _run

    nc = _bacc.Bacc("TRN2", target_bir_lowering=False, num_devices=1, dynamic_dma_scratch_size=4096)
    arrays, args = {}, []
    for name in _INS:
        a = _np.ascontiguousarray(inputs[name])
        arrays[f"in_{name}_dram"] = a
        args.append(nc.dram_tensor(f"in_{name}_dram", a.shape, _mybir.dt.from_np(a.dtype), kind="ExternalInput").ap())
    for i, (shape, dtype) in enumerate(_OUTS):
        dt = _mybir.dt.from_np(_np.dtype(dtype))
        args.append(nc.dram_tensor(f"out_{i}_dram", shape, dt, kind="ExternalOutput").ap())
    trunk(nc, *args)
    r = _run(nc, [arrays], core_ids=[0])
    got = tuple(r.results[0][f"out_{i}_dram"] for i in range(len(_OUTS)))
    return got[0]
```
